# Optimizing a Trainium2 kernel written in Bass

```python
import math
import jax, jax.numpy as jnp
from jax import lax
import numpy as np

D_MODEL = 2048
BATCH = 1
SEQ = 512
DEPTH = 2
DEC_BATCH = 1
DEC_SEQ = 32
PAST_LEN = 512

CHUNK = 64
Q_BLOCK = 128
N_ATT_LAYERS = (DEPTH + 1) // 2
N_POOL_LAYERS = DEPTH // 2
H_A = 8
DQK = 64
DV_A = 2 * DQK
W_A = H_A * DV_A
H_B = 8
Q_LORA = 512
KV_LORA = 512
NOPE_DIM = 128
ROPE_DIM = 64
V_DIM = 128
W_B = H_B * V_DIM
ROPE_THETA = 10000.0
W_ATT = W_A + W_B
ATT_SPLITS = [W_A, 2 * W_A, 3 * W_A, 3 * W_A + Q_LORA, 3 * W_A + Q_LORA + KV_LORA,
              3 * W_A + Q_LORA + KV_LORA + ROPE_DIM]
IN_ATT = 3 * W_A + Q_LORA + KV_LORA + ROPE_DIM + W_ATT
POOL_WINDOWS = (2, 4, 8, 16)
N_POOL_GROUPS = 4
W_C = D_MODEL
POOL_GW = W_C // N_POOL_GROUPS
POOL_STATE = max(POOL_WINDOWS) - 1
EPS = 1e-6
SUBLN_EPS = 1e-5
NEG_INF = -1e30
DIFF_SCALE = DQK ** -0.5
MLA_SCALE = (NOPE_DIM + ROPE_DIM) ** -0.5

kernel_name = "chunk_causal_diffattn_mla_pool_stream_step"

def _rmsnorm(x, g, eps=EPS):
    xf = x.astype(jnp.float32)
    y = xf * lax.rsqrt(jnp.mean(xf * xf, axis=-1, keepdims=True) + eps)
    return (y * g.astype(jnp.float32)).astype(x.dtype)

def _rope(x, pos):
    half = ROPE_DIM // 2
    inv = ROPE_THETA ** (-jnp.arange(half, dtype=jnp.float32) / half)
    ang = pos.astype(jnp.float32)[:, None] * inv[None, :]
    cos = jnp.cos(ang)[None, :, None, :]
    sin = jnp.sin(ang)[None, :, None, :]
    x1 = x[..., :half].astype(jnp.float32)
    x2 = x[..., half:].astype(jnp.float32)
    return jnp.concatenate([x1 * cos - x2 * sin, x1 * sin + x2 * cos], axis=-1).astype(x.dtype)

def _lambda_init(layer_idx):
    return 0.8 - 0.6 * math.exp(-0.3 * layer_idx)

def _masked_softmax(logits, q_chunk, k_chunk):
    mask = k_chunk[None, :] <= q_chunk[:, None]
    return jax.nn.softmax(jnp.where(mask, logits, NEG_INF), axis=-1)

def _sweep_query_blocks(fn, q_chunk, qs):
    sq = q_chunk.shape[0]
    if sq <= Q_BLOCK:
        return fn(q_chunk, qs)
    nb = sq // Q_BLOCK
    qc = q_chunk.reshape(nb, Q_BLOCK)
    qb = tuple(jnp.swapaxes(q.reshape(q.shape[0], nb, Q_BLOCK, *q.shape[2:]), 0, 1) for q in qs)
    out = lax.map(lambda a: fn(a[0], a[1]), (qc, qb))
    out = jnp.swapaxes(out, 0, 1)
    return out.reshape(out.shape[0], sq, *out.shape[3:])

def _diff_attention(q, k, v, lam, q_chunk, k_chunk):
    def blk(qc, qs):
        (qb,) = qs
        logits = jnp.einsum('bqhnd,bkhnd->bnhqk', qb, k,
                            preferred_element_type=jnp.float32) * DIFF_SCALE
        p = _masked_softmax(logits, qc, k_chunk)
        w = p[:, 0] - lam * p[:, 1]
        return jnp.einsum('bhqk,bkhe->bqhe', w.astype(v.dtype), v)
    return _sweep_query_blocks(blk, q_chunk, (q,))

def _mla_attention(q_lat, q_pe, c_kv, k_pe, q_chunk, k_chunk):
    def blk(qc, qs):
        ql, qp = qs
        logits = (jnp.einsum('bqhc,bkc->bhqk', ql, c_kv, preferred_element_type=jnp.float32)
                  + jnp.einsum('bqhr,bkr->bhqk', qp, k_pe, preferred_element_type=jnp.float32)) * MLA_SCALE
        p = _masked_softmax(logits, qc, k_chunk)
        return jnp.einsum('bhqk,bkc->bqhc', p.astype(c_kv.dtype), c_kv)
    return _sweep_query_blocks(blk, q_chunk, (q_lat, q_pe))

def _attn_mixer(h, pos, k_pos, lam_init, cache_k, cache_v, cache_ckv, cache_kpe,
                w_in, w_out, lam_q1, lam_k1, lam_q2, lam_k2, g_subln,
                g_qa, w_uq, w_uqr, w_uk, w_uv, g_kva):
    b, s, _ = h.shape
    z = h @ w_in
    qa, ka, va, cq, ckv, kpe, gate = jnp.split(z, ATT_SPLITS, axis=-1)
    qa = qa.reshape(b, s, H_A, 2, DQK)
    ka = ka.reshape(b, s, H_A, DV_A)
    va = va.reshape(b, s, H_A, DV_A)
    cq = _rmsnorm(cq, g_qa)
    q_nope = jnp.einsum('bsc,chd->bshd', cq, w_uq)
    q_pe = _rope(jnp.einsum('bsc,chr->bshr', cq, w_uqr), pos)
    q_lat = jnp.einsum('bshd,chd->bshc', q_nope, w_uk)
    ckv = _rmsnorm(ckv, g_kva)
    kpe = _rope(kpe[:, :, None, :], pos)[:, :, 0, :]
    new_rows = (ka, va, ckv, kpe)
    if cache_k is not None:
        k_all = jnp.concatenate([cache_k.astype(ka.dtype), ka], axis=1)
        v_all = jnp.concatenate([cache_v.astype(va.dtype), va], axis=1)
        ckv_all = jnp.concatenate([cache_ckv.astype(ckv.dtype), ckv], axis=1)
        kpe_all = jnp.concatenate([cache_kpe.astype(kpe.dtype), kpe], axis=1)
    else:
        k_all, v_all, ckv_all, kpe_all = ka, va, ckv, kpe
    sk = k_all.shape[1]
    q_chunk = pos // CHUNK
    k_chunk = k_pos // CHUNK
    lam = (jnp.exp(jnp.sum(lam_q1.astype(jnp.float32) * lam_k1.astype(jnp.float32)))
           - jnp.exp(jnp.sum(lam_q2.astype(jnp.float32) * lam_k2.astype(jnp.float32))) + lam_init)
    o_a = _diff_attention(qa, k_all.reshape(b, sk, H_A, 2, DQK), v_all, lam, q_chunk, k_chunk)
    o_a = _rmsnorm(o_a, g_subln, SUBLN_EPS) * (1.0 - lam_init)
    o_lat = _mla_attention(q_lat, q_pe, ckv_all, kpe_all, q_chunk, k_chunk)
    o_b = jnp.einsum('bshc,chv->bshv', o_lat, w_uv)
    o = jnp.concatenate([o_a.reshape(b, s, W_A), o_b.reshape(b, s, W_B)], axis=-1) * jax.nn.silu(gate)
    return o @ w_out, new_rows

def _pool_mixer(h, pos, prefix, w_in, w_grp, scale, w_out):
    b, s, _ = h.shape
    u, gate = jnp.split(h @ w_in, 2, axis=-1)
    u_ext = jnp.concatenate([prefix.astype(u.dtype), u], axis=1)
    p = POOL_STATE
    cs = jnp.cumsum(u_ext.astype(jnp.float32), axis=1)
    cs = jnp.pad(cs, ((0, 0), (1, 0), (0, 0)))
    end = cs[:, p + 1:p + 1 + s]
    pooled = []
    for g, w in enumerate(POOL_WINDOWS):
        sl = slice(g * POOL_GW, (g + 1) * POOL_GW)
        start = cs[:, p + 1 - w:p + 1 - w + s, sl]
        cnt = jnp.minimum(pos + 1, w).astype(jnp.float32)[None, :, None]
        pooled.append((end[..., sl] - start) / cnt)
    mean = jnp.concatenate(pooled, axis=-1)
    d = (mean - u.astype(jnp.float32)).astype(u.dtype).reshape(b, s, N_POOL_GROUPS, POOL_GW)
    m = jnp.einsum('bsgc,gcd->bsgd', d, w_grp).reshape(b, s, W_C) * scale
    y = (m * jax.nn.silu(gate)) @ w_out
    return y, u_ext[:, -POOL_STATE:]

def _trunk(x, c, pos, k_pos, cache_diff_k, cache_diff_v, cache_mla_ckv, cache_mla_kpe, state_pool,
           g_norm, w_ada, b_ada, w_in_att, w_out_att, lam_q1, lam_k1, lam_q2, lam_k2, g_subln,
           g_qa, w_uq, w_uqr, w_uk, w_uv, g_kva, w_in_pool, w_grp_pool, scale_pool, w_out_pool, g_final):
    b = x.shape[0]
    rows_k, rows_v, rows_ckv, rows_kpe, rows_pool = [], [], [], [], []
    cond = jax.nn.silu(c)
    has_cache = cache_diff_k is not None
    for i in range(DEPTH):
        j = i // 2
        mod = (cond @ w_ada[i] + b_ada[i])[:, None, :]
        shift, scale, gate = jnp.split(mod, 3, axis=-1)
        h = _rmsnorm(x, g_norm[i]) * (1 + scale) + shift
        if i % 2 == 0:
            y, (k_r, v_r, ckv_r, kpe_r) = _attn_mixer(
                h, pos, k_pos, _lambda_init(i),
                cache_diff_k[j] if has_cache else None, cache_diff_v[j] if has_cache else None,
                cache_mla_ckv[j] if has_cache else None, cache_mla_kpe[j] if has_cache else None,
                w_in_att[j], w_out_att[j], lam_q1[j], lam_k1[j], lam_q2[j], lam_k2[j], g_subln[j],
                g_qa[j], w_uq[j], w_uqr[j], w_uk[j], w_uv[j], g_kva[j])
            rows_k.append(k_r)
            rows_v.append(v_r)
            rows_ckv.append(ckv_r)
            rows_kpe.append(kpe_r)
        else:
            prefix = state_pool[j] if has_cache else jnp.zeros((b, POOL_STATE, W_C), x.dtype)
            y, st = _pool_mixer(h, pos, prefix, w_in_pool[j], w_grp_pool[j], scale_pool[j], w_out_pool[j])
            rows_pool.append(st)
        x = x + gate * y
    return (_rmsnorm(x, g_final), jnp.stack(rows_k), jnp.stack(rows_v), jnp.stack(rows_ckv),
            jnp.stack(rows_kpe), jnp.stack(rows_pool))

def setup_inputs(seed: int = 0) -> dict:
    key = jax.random.key(seed)
    ks = jax.random.split(key, 40)

    def nrm(k, shape, s):
        return s * jax.random.normal(k, shape, jnp.float32)

    d = D_MODEL
    return {
        "x_prompt": nrm(ks[0], (BATCH, SEQ, d), 1.0),
        "x_sample": nrm(ks[1], (DEC_BATCH, DEC_SEQ, d), 1.0),
        "c_prompt": nrm(ks[2], (BATCH, d), 1.0),
        "c_sample": nrm(ks[3], (DEC_BATCH, d), 1.0),
        "cache_diff_k": nrm(ks[4], (N_ATT_LAYERS, DEC_BATCH, PAST_LEN, H_A, DV_A), 1.0),
        "cache_diff_v": nrm(ks[5], (N_ATT_LAYERS, DEC_BATCH, PAST_LEN, H_A, DV_A), 1.0),
        "cache_mla_ckv": nrm(ks[6], (N_ATT_LAYERS, DEC_BATCH, PAST_LEN, KV_LORA), 1.0),
        "cache_mla_kpe": nrm(ks[7], (N_ATT_LAYERS, DEC_BATCH, PAST_LEN, ROPE_DIM), 1.0),
        "state_pool": nrm(ks[8], (N_POOL_LAYERS, DEC_BATCH, POOL_STATE, W_C), 1.0),
        "g_norm": 1.0 + nrm(ks[9], (DEPTH, d), 0.05),
        "w_ada": nrm(ks[10], (DEPTH, d, 3 * d), 0.2 * d ** -0.5),
        "b_ada": nrm(ks[11], (DEPTH, 3 * d), 0.02),
        "w_in_att": nrm(ks[12], (N_ATT_LAYERS, d, IN_ATT), d ** -0.5),
        "w_out_att": nrm(ks[13], (N_ATT_LAYERS, W_ATT, d), W_ATT ** -0.5),
        "lam_q1": nrm(ks[14], (N_ATT_LAYERS, DQK), 0.1),
        "lam_k1": nrm(ks[15], (N_ATT_LAYERS, DQK), 0.1),
        "lam_q2": nrm(ks[16], (N_ATT_LAYERS, DQK), 0.1),
        "lam_k2": nrm(ks[17], (N_ATT_LAYERS, DQK), 0.1),
        "g_subln": 1.0 + nrm(ks[18], (N_ATT_LAYERS, DV_A), 0.05),
        "g_qa": 1.0 + nrm(ks[19], (N_ATT_LAYERS, Q_LORA), 0.05),
        "w_uq": nrm(ks[20], (N_ATT_LAYERS, Q_LORA, H_B, NOPE_DIM), Q_LORA ** -0.5),
        "w_uqr": nrm(ks[21], (N_ATT_LAYERS, Q_LORA, H_B, ROPE_DIM), Q_LORA ** -0.5),
        "w_uk": nrm(ks[22], (N_ATT_LAYERS, KV_LORA, H_B, NOPE_DIM), KV_LORA ** -0.5),
        "w_uv": nrm(ks[23], (N_ATT_LAYERS, KV_LORA, H_B, V_DIM), KV_LORA ** -0.5),
        "g_kva": 1.0 + nrm(ks[24], (N_ATT_LAYERS, KV_LORA), 0.05),
        "w_in_pool": nrm(ks[25], (N_POOL_LAYERS, d, 2 * W_C), d ** -0.5),
        "w_grp_pool": nrm(ks[26], (N_POOL_LAYERS, N_POOL_GROUPS, POOL_GW, POOL_GW), POOL_GW ** -0.5),
        "scale_pool": 1.0 + nrm(ks[27], (N_POOL_LAYERS, W_C), 0.1),
        "w_out_pool": nrm(ks[28], (N_POOL_LAYERS, W_C, d), W_C ** -0.5),
        "g_final": 1.0 + nrm(ks[29], (d,), 0.05),
    }

def reference(x_prompt, x_sample, c_prompt, c_sample, cache_diff_k, cache_diff_v, cache_mla_ckv,
              cache_mla_kpe, state_pool, g_norm, w_ada, b_ada, w_in_att, w_out_att, lam_q1, lam_k1,
              lam_q2, lam_k2, g_subln, g_qa, w_uq, w_uqr, w_uk, w_uv, g_kva, w_in_pool, w_grp_pool,
              scale_pool, w_out_pool, g_final):
    weights = (g_norm, w_ada, b_ada, w_in_att, w_out_att, lam_q1, lam_k1, lam_q2, lam_k2, g_subln,
               g_qa, w_uq, w_uqr, w_uk, w_uv, g_kva, w_in_pool, w_grp_pool, scale_pool, w_out_pool, g_final)
    s_p = x_prompt.shape[1]
    pos_p = jnp.arange(s_p, dtype=jnp.int32)
    y_prompt, pk, pv, pckv, pkpe, ppool = _trunk(
        x_prompt, c_prompt, pos_p, pos_p, None, None, None, None, None, *weights)
    past = cache_diff_k.shape[2]
    n = x_sample.shape[1]
    pos_s = past + jnp.arange(n, dtype=jnp.int32)
    k_pos_s = jnp.arange(past + n, dtype=jnp.int32)
    y_sample, sk, sv, sckv, skpe, spool = _trunk(
        x_sample, c_sample, pos_s, k_pos_s, cache_diff_k, cache_diff_v, cache_mla_ckv, cache_mla_kpe,
        state_pool, *weights)
    return (y_prompt, y_sample, pk, pv, pckv, pkpe, ppool, sk, sv, sckv, skpe, spool)


_drawn_inputs = setup_inputs


def setup_inputs(seed=0):
    import zlib

    import numpy as np

    out = dict(_drawn_inputs(seed))
    spreads = {}
    factors = {'cache_mla_ckv': 8.0,
     'cache_mla_kpe': 8.0,
     'state_pool': 7.439,
     'lam_q1': 64.0,
     'lam_k1': 8.0,
     'lam_q2': 8.0,
     'lam_k2': 5.168,
     'g_subln': 27.789,
     'g_qa': 8.0,
     'w_uq': 8.0,
     'w_uqr': 8.0,
     'w_uk': 8.0,
     'w_uv': 5.919,
     'scale_pool': 8.0}
    for name, (base, spread) in spreads.items():
        noise = np.random.default_rng([zlib.crc32(name.encode()), seed]).standard_normal(out[name].shape)
        drawn = base * np.exp(spread * noise) if base else spread * noise
        out[name] = __import__('jax').numpy.asarray(drawn.astype(out[name].dtype))
    for name, factor in factors.items():
        out[name] = (out[name] * factor).astype(out[name].dtype)
    return out
```

```python
from contextlib import ExitStack
import math

import numpy as np

import concourse.bass as bass
from concourse import mybir

F32 = mybir.dt.float32
F32R = mybir.dt.float32r
ALU = mybir.AluOpType
ACT = mybir.ActivationFunctionType
AX = mybir.AxisListType

P = 128
D = 2048
KT = D // P
NP, NS = 512, 32
R = NP + NS
HALF = R // 2
PAST = 512
HEADS = 8
QT = NP // P
KTS = PAST // P + 1
SKEYS = PAST + NS
LORA = 512
LT = LORA // P
ZT = 32
ZQ, ZK, ZV = 8, 16, 24
GT = 16
ADA_PE = 20
ADA_P0 = 12
ADA_P1 = 48
ADA_T = 96
DQK = 64
LAM_INIT = 0.8 - 0.6 * math.exp(-0.3 * 0)
EPS, SUB_EPS = 1e-6, 1e-5
DIFF_SCALE = DQK ** -0.5
MLA_SCALE = (128 + 64) ** -0.5
MASKED = -float(2 ** 100)
WIN = (2, 4, 8, 16)
PAD = 15

G_KPE = ADA_PE
G_Z = G_KPE + 1
G_GATE = G_Z + ZT
G_OUT = G_GATE + GT
G_PIN = G_OUT + KT
G_GRP = G_PIN + 2 * KT
G_POUT = G_GRP + 4
G_END = G_POUT + KT
CHUNKS = ADA_PE // 4


def turn_of(g):
    return g // 2 - (G_KPE // 2 - 1)


class Tally:

    def __init__(self, sem):
        self.sem, self.base, self.k, self.t, self.per = sem, 0, 0, None, 0

    def loop(self, t, per):
        self.base, self.k, self.t, self.per = self.base + self.k, 0, t, per

    def end(self, count):
        assert self.k == self.per, (self.k, self.per)
        self.base, self.k, self.t, self.per = self.base + self.per * count, 0, None, 0

    def inc(self, ins):
        ins.then_inc(self.sem, 1)
        self.k += 1
        return self.base + self.k + (self.per * self.t if self.t is not None else 0)


def program(nc, xT, cT, cB, w_ada_pe, w_ada_dve, bada, gnorm, w_kpe, w_z, w_gate, w_out, w_pin, w_grp, w_pout,
            lamv, gsub, gqa, gkva, w_uq, w_uqr, w_ukT, w_uv, scale_pool, gfin,
            kc, vc, ckvT, ckv, kpeT, poolT, cosT, sinT, swap, ident, maskq, maskk, rcount, lamsel,
            y_out, z_out, ckv_out, kpe_out, pool_out):
    g_scr = nc.dram_tensor("gate_scratch", (GT, P, R), F32, kind="Internal").ap()
    d_scr = nc.dram_tensor("pool_d_scratch", (KT, P, R), F32, kind="Internal").ap()
    pg_scr = nc.dram_tensor("pool_gate_scratch", (KT, P, R), F32, kind="Internal").ap()

    keep = ExitStack()
    with keep:
        def sb(name, shape, dt=F32, scope=keep):
            return scope.enter_context(nc.sbuf_tensor(name, shape, dt))

        def sem(name):
            return keep.enter_context(nc.semaphore(name))

        h_hi = sb("h_hi", [P, KT, R], F32R)
        h_lo = sb("h_lo", [P, KT, R], F32R)
        w_raw = sb("w_raw", [P, 2, D])
        kpe = sb("kpe", [P, R])
        rstd = sb("rstd", [P, R])
        ssq = sb("ssq", [P, R])
        cos_t = sb("cos_t", [P, R])
        sin_t = sb("sin_t", [P, R])
        swap_t = sb("swap_t", [P, P])
        id_t = sb("id_t", [P, P])
        ones = sb("ones", [P, P])
        maskq_t = sb("maskq_t", [1, P])
        maskk_t = sb("maskk_t", [1, DQK])
        mod = sb("mod", [P, 2, ADA_T])
        bada_t = sb("bada_t", [P, ADA_T])
        gnorm_t = sb("gnorm_t", [P, 2, KT])
        aff = sb("aff", [P, 2, KT])
        cond_t = sb("cond_t", [P, KT, 2])
        vecs = sb("vecs", [P, 3, KT])
        pool_last = sb("pool_last", [P, KT, 2, PAD])
        pool_pre = sb("pool_pre", [P, KT, PAD])
        ada_acc = sb("ada_acc", [P, 2])
        act_tmp = sb("act_tmp", [P, 2])
        rcount_t = sb("rcount_t", [P, 4, 16])
        lam_in = sb("lam_in", [P, 4, DQK])
        lam_w = sb("lam_w", [P, 8])
        lamsel_t = sb("lamsel_t", [P, 2])
        PS = keep.enter_context(nc.psum_tensor("banks", [P, 8, 512], F32))

        scale_v, gfin_v = vecs[:, 0, :], vecs[:, 1, :]
        gsub_v, gqa_v, gkva_v = vecs[:, 2, 0:1], vecs[:, 2, 1:5], vecs[:, 2, 5:9]
        neg_lam, coef = lam_w[:, 6:7], lam_w[:, 7:8]
        rows = lambda ap: ap.rearrange("p (a r) -> p a r", a=2)
        acc = [PS[:, 2 * s:2 * s + 2, 0:HALF] for s in range(2)]
        ada_junk = PS[:, 4:8, :].rearrange("p a b -> p (a b)")

        stream = ExitStack()
        x = sb("x", [P, KT, R], scope=stream)
        w_hi = sb("w_hi", [P, 2, D], F32R, stream)
        w_lo = sb("w_lo", [P, 2, D], F32R, stream)
        stage = sb("stage", [P, 2, R], scope=stream)
        ada_stack = ExitStack()
        w_adr = sb("w_adr", [P, 2, D], scope=ada_stack)
        cond_b = sb("cond_b", [P, 2, D], scope=ada_stack)
        ada_stack.close()
        pin_stack = ExitStack()
        u_ext = sb("u_ext", [P, PAD + NP + PAD + NS], scope=pin_stack)
        w2 = sb("w2", [P, PAD + NP + PAD + NS], scope=pin_stack)
        w4 = sb("w4", [P, PAD + NP + PAD + NS], scope=pin_stack)
        d_st = sb("d_st", [P, R], scope=pin_stack)
        fix = sb("fix", [P, 16], scope=pin_stack)
        pin_stack.close()
        grp_stack = ExitStack()
        d_raw = sb("d_raw", [P, 4, R], scope=grp_stack)
        d_hi = sb("d_hi", [P, 4, R], F32R, grp_stack)
        d_lo = sb("d_lo", [P, 4, R], F32R, grp_stack)
        pg = sb("pg", [P, 4, R], scope=grp_stack)
        grp_stack.close()
        stream.close()

        mla = ExitStack()
        ckT = sb("ckT", [P, LT, R], scope=mla)
        ckR = sb("ckR", [P, QT + 1, LORA], scope=mla)
        kpc = sb("kpc", [P, PAST], scope=mla)
        qls = sb("qls", [P, LT, HEADS, NS], scope=mla)
        qps = sb("qps", [P, HEADS, NS], scope=mla)
        ml_loop = ExitStack()
        cq = sb("cq", [P, LT, R], scope=ml_loop)
        wq = sb("wq", [P, 2, LT, P], scope=ml_loop)
        wk = sb("wk", [P, 2, LORA], scope=ml_loop)
        wr = sb("wr", [P, LT, P], scope=ml_loop)
        wv = sb("wv", [P, 2, LT, P], scope=ml_loop)
        qn = sb("qn", [P, 2, R], scope=ml_loop)
        qpr = sb("qpr", [P, R], scope=ml_loop)
        qpe = sb("qpe", [P, R], scope=ml_loop)
        ql = sb("ql", [P, 2, LT, R], scope=ml_loop)
        px = sb("px", [P, 3, NP], scope=ml_loop)
        pt = sb("pt", [P, QT, NP], scope=ml_loop)
        ol = sb("ol", [P, LT, NP], scope=ml_loop)
        sg = sb("sg", [P, 2, R], scope=ml_loop)
        st = sb("st", [P, 4, 8], scope=ml_loop)
        ml_loop.close()
        ml_samp = ExitStack()
        ccT = sb("ccT", [P, LT, PAST], scope=ml_samp)
        ccR = sb("ccR", [P, LT, LORA], scope=ml_samp)
        wva = sb("wva", [P, LT, HEADS * P], scope=ml_samp)
        pxs = sb("pxs", [P, 2, SKEYS], scope=ml_samp)
        pts = sb("pts", [P, 2, KTS, P], scope=ml_samp)
        ols = sb("ols", [P, LT, HEADS, NS], scope=ml_samp)
        sgs = sb("sgs", [P, HEADS, NS], scope=ml_samp)
        ofs = sb("ofs", [P, HEADS, NS], scope=ml_samp)
        sts = sb("sts", [P, 2, 4], scope=ml_samp)
        ml_samp.close()
        mla.close()

        dif = ExitStack()
        qd = sb("qd", [P, 2, R], scope=dif)
        kd = sb("kd", [P, 2, R], scope=dif)
        vd = sb("vd", [P, 2, R], scope=dif)
        kcs = sb("kcs", [P, 2, PAST], scope=dif)
        vcs = sb("vcs", [P, 2, QT, P], scope=dif)
        sgd = sb("sgd", [P, 2, R], scope=dif)
        vr = sb("vr", [P, 2, KTS, P], scope=dif)
        pxd = sb("pxd", [P, 3, 2, NP], scope=dif)
        ptd = sb("ptd", [P, 2, QT, NP], scope=dif)
        od = sb("od", [P, 2, R], scope=dif)
        sqd = sb("sqd", [P, 2, R], scope=dif)
        rsd = sb("rsd", [P, 2, R], scope=dif)
        pxds = sb("pxds", [P, SKEYS], scope=dif)
        ptds = sb("ptds", [P, KTS, P], scope=dif)
        std = sb("std", [P, 9, 8], scope=dif)
        dif.close()

        consts_in = sem("consts_in"); x_in = sem("x_in"); cond_in = sem("cond_in"); condb_in = sem("condb_in")
        raw_in = [sem(f"raw_in{s}") for s in range(2)]
        adr_in = [sem(f"adr_in{s}") for s in range(2)]
        cond_ready = sem("cond_ready"); condb_ready = sem("condb_ready")
        adr_used = sem("adr_used")
        split_ready = sem("split_ready")
        mm_done = sem("mm_done")
        acc_free = [sem(f"acc_free{s}") for s in range(2)]
        sq_ready = sem("sq_ready"); sq_added = sem("sq_added"); ssq_zero = sem("ssq_zero"); var_eps = sem("var_eps")
        var_ready = sem("var_ready"); std_ready = sem("std_ready"); rstd_ready = sem("rstd_ready")
        xn_ready = sem("xn_ready"); hf_ready = sem("hf_ready"); h_ready = sem("h_ready")
        dve_step = sem("dve_step"); act_step = sem("act_step"); ada_row = sem("ada_row"); ada_turned = sem("ada_turned"); x_normed = sem("x_normed"); ones_ready = sem("ones_ready")
        staged = sem("staged"); stored = [sem(f"stored{s}") for s in range(2)]
        kpe_ready = sem("kpe_ready"); lam_ready = sem("lam_ready"); lam_exp = sem("lam_exp"); lam_sum = sem("lam_sum")
        out_done = sem("out_done")
        dv, ac = Tally(dve_step), Tally(act_step)
        mq_in = sem("mq_in"); mq_sq = sem("mq_sq"); mq_sum = sem("mq_sum"); mq_var = sem("mq_var")
        mq_std = sem("mq_std"); mq_norm = sem("mq_norm"); mq_tr = sem("mq_tr"); mq_ev = sem("mq_ev")
        kp_swap = sem("kp_swap"); kp_done = sem("kp_done"); latent_out = sem("latent_out")
        ml_w_in = sem("ml_w_in"); ml_v_in = sem("ml_v_in"); ml_item = sem("ml_item"); ml_item_ev = sem("ml_item_ev")
        ml_swap = sem("ml_swap"); ml_qpe = sem("ml_qpe"); ml_score = sem("ml_score"); ml_max = sem("ml_max")
        ml_exp = sem("ml_exp"); ml_norm = sem("ml_norm"); ml_tr = sem("ml_tr"); ml_ptev = sem("ml_ptev")
        ml_pv = sem("ml_pv"); ml_olev = sem("ml_olev"); ml_fin = sem("ml_fin"); qps_zero = sem("qps_zero")
        ms_in = sem("ms_in"); ms_score = sem("ms_score"); ms_max = sem("ms_max"); ms_exp = sem("ms_exp")
        ms_norm = sem("ms_norm"); ms_tr = sem("ms_tr"); ms_ptev = sem("ms_ptev"); ms_pv = sem("ms_pv")
        ms_olev = sem("ms_olev"); ms_ob = sem("ms_ob"); ms_fin = sem("ms_fin")
        df_a_in = sem("df_a_in"); df_v_in = sem("df_v_in"); df_g_in = sem("df_g_in"); df_vt = sem("df_vt")
        df_vrev = sem("df_vrev"); df_score = sem("df_score"); df_max = sem("df_max"); df_exp = sem("df_exp")
        df_norm = sem("df_norm"); df_tr = sem("df_tr"); df_ptev = sem("df_ptev"); df_pv = sem("df_pv")
        df_od = sem("df_od"); df_sq = sem("df_sq"); df_ssq = sem("df_ssq"); df_var = sem("df_var")
        df_std = sem("df_std"); df_fin = sem("df_fin"); lam_scaled = sem("lam_scaled")
        dfs_score = sem("dfs_score"); dfs_max = sem("dfs_max"); dfs_exp = sem("dfs_exp")
        dfs_norm = sem("dfs_norm"); dfs_tr = sem("dfs_tr"); dfs_ptev = sem("dfs_ptev"); dfs_pv = sem("dfs_pv")
        gy_ready = sem("gy_ready"); x_new = sem("x_new"); u_ready = sem("u_ready"); u_used = sem("u_used")
        pg_ready = sem("pg_ready"); d_ready = sem("d_ready"); pre_in = sem("pre_in"); d_stored = sem("d_stored")
        pg_stored = sem("pg_stored"); grp_in = [sem("grp_in0"), sem("grp_in1")]; grp_mm = sem("grp_mm")
        grp_y = sem("grp_y"); d_split = sem("d_split"); y_ready = sem("y_ready"); y_fin = sem("y_fin"); pool_pre_in = sem("pool_pre_in"); pad_zero = sem("pad_zero"); pad_free = sem("pad_free"); qps_free = sem("qps_free")
        y_stored = [sem(f"y_stored{s}") for s in range(2)]

        def vchain(dve, ins):
            dve.wait_ge(dve_step, dv.inc(ins))

        def achain(act, ins):
            act.wait_ge(act_step, ac.inc(ins))

        def pairs(ap):
            return ap.rearrange("(t s) p n -> s t p n", s=2)

        def tile_of(pair, s, t):
            return pair[s, bass.ds(t, 1)].rearrange("t p n -> p (t n)")

        def at(ap, k):
            return ap[:, bass.ds(k, 1), :].rearrange("p k r -> p (k r)")

        wz2, wg2, wo2, wp2, wy2 = (pairs(a) for a in (w_z, w_gate, w_out, w_pin, w_pout))
        wd2, z2, g2 = pairs(w_ada_dve), pairs(z_out), pairs(g_scr)
        CONSTS = 16 * 17
        block = keep.enter_context(nc.Block())

        @block.sync
        def _(sp):
            sp.dma_start(cond_t[:], cT).then_inc(cond_in, 16)

            def load_w(src, slot, ready=None):
                if ready is not None:
                    sp.wait_ge(split_ready, ready)
                sp.dma_start(w_raw[:, slot], src).then_inc(raw_in[slot], 16)

            def load_ada(pair_slot, src, used=None):
                if used is not None:
                    sp.wait_ge(adr_used, used)
                sp.dma_start(w_adr[:, pair_slot], src).then_inc(adr_in[pair_slot], 16)

            sp.dma_start(cond_b[:], cB.to_broadcast((P, 2 * D)).rearrange("p (a d) -> p a d", a=2)).then_inc(condb_in, 16)
            for s in range(2):
                load_w(w_ada_pe[s], s)
                load_ada(s, w_ada_dve[s])
            for g in range(2, ADA_PE):
                sp.wait_ge(mm_done, g - 1)
                load_w(w_ada_pe[g], g % 2)
                if g == 3:
                    sp.dma_start(x[:], xT).then_inc(x_in, 16)
                if 3 <= g < ADA_P0 + 1:
                    load_ada((g - 1) % 2, w_ada_dve[g - 1], g - 2)
            sp.wait_ge(mm_done, G_KPE - 1)
            load_w(w_kpe, G_KPE % 2)
            for a in range(ADA_P0, ADA_P0 + 2):
                load_ada(a % 2, w_ada_dve[a], a - 1)
            sp.wait_ge(mm_done, G_KPE)
            with sp.Fori(0, ZT // 2) as t:
                for s in range(2):
                    load_w(tile_of(wz2, s, t), (G_Z + s) % 2, 2 * t + G_Z - G_KPE + s)
            with sp.Fori(0, GT // 2) as t:
                for s in range(2):
                    load_w(tile_of(wg2, s, t), (G_GATE + s) % 2, 2 * t + G_GATE - G_KPE + s)
            for s in range(2):
                load_w(w_out[s], (G_OUT + s) % 2, G_OUT - G_KPE + s)

            sp.wait_ge(mm_done, G_OUT)
            sp.wait_ge(adr_used, ADA_P0 + ADA_P1)
            for s in range(2):
                sp.wait_ge(stored[s], 16 * (ZT + GT) // 2)
            sp.dma_start(cq[:], z_out[0:LT].rearrange("t p r -> p t r")).then_inc(mq_in, 16)
            sp.dma_start(ckT[:], z_out[LT:2 * LT].rearrange("t p r -> p t r")).then_inc(mq_in, 16)
            for e in range(2):
                sp.dma_start(kpc[64 * e:64 * e + 64, :], kpeT).then_inc(mq_in, 16)

            uq2, uk2, uv2 = (a.rearrange("(t s) p n -> s t p n", s=2) for a in (w_uq, w_ukT, w_uv))

            def load_mla_w(t):
                for s in range(2):
                    sp.dma_start(wq[:, s].rearrange("p c d -> p (c d)"), tile_of(uq2, s, t)).then_inc(ml_w_in, 16)
                    sp.dma_start(wk[:, s], tile_of(uk2, s, t)).then_inc(ml_w_in, 16)
                sp.dma_start(wr[:].rearrange("p c d -> p (c d)"),
                             w_uqr[bass.ds(t, 1)].rearrange("t p n -> p (t n)")).then_inc(ml_w_in, 16)

            def load_mla_v(t):
                for s in range(2):
                    sp.dma_start(wv[:, s].rearrange("p c d -> p (c d)"), tile_of(uv2, s, t)).then_inc(ml_v_in, 16)
                    sp.dma_start(sg[:, s], tile_of(g2, s, t + HEADS // 2)).then_inc(ml_v_in, 16)

            load_mla_w(0)
            load_mla_v(0)
            with sp.Fori(0, HEADS // 2 - 1) as t:
                sp.wait_ge(ml_item, 11 * t + 11)
                load_mla_w(t + 1)
                sp.wait_ge(ml_fin, 2 * t + 2)
                load_mla_v(t + 1)
            sp.wait_ge(ml_fin, HEADS)
            sp.dma_start(ccT[:], ckvT.rearrange("(c p) k -> p c k", p=P)).then_inc(ms_in, 16)
            sp.dma_start(ccR[:], ckv.rearrange("(k p) c -> p k c", p=P)).then_inc(ms_in, 16)
            for h in range(HEADS):
                sp.dma_start(wva[:, :, h * P:(h + 1) * P],
                             w_uv[h].rearrange("p (c v) -> p c v", c=LT)).then_inc(ms_in, 16)
            sp.dma_start(sgs[:], g_scr[HEADS:2 * HEADS, :, NP:R].rearrange("h p r -> p h r")).then_inc(ms_in, 16)

            sp.wait_ge(ms_fin, 1)
            sp.wait_ge(latent_out, 32)
            kc2 = kc.rearrange("(t s) p k -> s t p k", s=2)
            vc2 = vc.rearrange("(j p) (t s e) -> s t p j e", p=P, s=2, e=P)

            def load_qk(t):
                for s in range(2):
                    sp.dma_start(qd[:, s], tile_of(z2, s, t + ZQ // 2)).then_inc(df_a_in, 16)
                    sp.dma_start(kd[:, s], tile_of(z2, s, t + ZK // 2)).then_inc(df_a_in, 16)
                    sp.dma_start(kcs[:, s], tile_of(kc2, s, t)).then_inc(df_a_in, 16)

            def load_v(t):
                for s in range(2):
                    sp.dma_start(vd[:, s], tile_of(z2, s, t + ZV // 2)).then_inc(df_v_in, 16)
                    sp.dma_start(vcs[:, s], vc2[s, bass.ds(t, 1)].rearrange("t p j e -> p (t j) e")).then_inc(df_v_in, 16)

            def load_g(t):
                for s in range(2):
                    sp.dma_start(sgd[:, s], tile_of(g2, s, t)).then_inc(df_g_in, 16)

            load_v(0)
            load_qk(0)
            load_g(0)
            with sp.Fori(0, HEADS // 2 - 1) as t:
                sp.wait_ge(dfs_score, t + 1)
                load_qk(t + 1)
                sp.wait_ge(dfs_pv, t + 1)
                load_v(t + 1)
                sp.wait_ge(df_fin, 2 * t + 2)
                load_g(t + 1)

            sp.wait_ge(df_fin, HEADS)
            sp.dma_start(cond_b[:], cB.to_broadcast((P, 2 * D)).rearrange("p (a d) -> p a d", a=2)).then_inc(condb_in, 16)
            sp.dma_start(x[:], xT).then_inc(x_in, 16)
            for s in range(2):
                load_ada(s, w_ada_dve[ADA_P0 + ADA_P1 + s])
            with sp.Fori(0, KT // 2 - 1) as t:
                for s in range(2):
                    load_w(tile_of(wo2, s, t + 1), (G_OUT + s) % 2, 2 * t + 2 + G_OUT - G_KPE + s)
            with sp.Fori(0, KT) as t:
                for s in range(2):
                    load_w(tile_of(wp2, s, t), (G_PIN + s) % 2, 2 * t + G_PIN - G_KPE + s)
            for g in range(4):
                load_w(w_grp[g], (G_GRP + g) % 2, G_GRP - G_KPE + g)
                if g == 0:
                    sp.wait_ge(d_stored, 16 * KT)
                    sp.wait_ge(pg_stored, 16 * KT)
                else:
                    sp.wait_ge(d_split, g)
                sp.dma_start(d_raw[:], d_scr[4 * g:4 * g + 4].rearrange("t p r -> p t r")).then_inc(grp_in[0], 16)
                if g:
                    sp.wait_ge(grp_y, 4 * g)
                sp.dma_start(pg[:], pg_scr[4 * g:4 * g + 4].rearrange("t p r -> p t r")).then_inc(grp_in[1], 16)
            with sp.Fori(0, KT // 2) as t:
                for s in range(2):
                    load_w(tile_of(wy2, s, t), (G_POUT + s) % 2, 2 * t + G_POUT - G_KPE + s)
            for k in range(KT):
                sp.wait_ge(y_fin, k + 1)
                sp.dma_start(y_out[k], x[:, k]).then_inc(y_stored[k % 2], 16)
            sp.wait_ge(out_done, 16)
            for s in range(2):
                sp.wait_ge(y_stored[s], 16 * KT // 2)

        @block.gpsimd
        def _(pool):
            pool.memset(ones[:], 1.0).then_inc(ones_ready, 1)
            for dst, src in ((cos_t, cosT), (sin_t, sinT), (swap_t, swap), (id_t, ident), (maskq_t, maskq), (maskk_t, maskk),
                             (bada_t, bada), (gnorm_t, gnorm), (rcount_t, rcount), (lamsel_t, lamsel), (pool_pre, poolT)):
                pool.dma_start(dst[:], src).then_inc(consts_in, 16)
            for dst, src in ((scale_v, scale_pool), (gfin_v, gfin), (gsub_v, gsub), (gqa_v, gqa), (gkva_v, gkva)):
                pool.dma_start(dst, src).then_inc(consts_in, 16)
            pool.dma_start(lam_in[:], lamv.to_broadcast((P, 4 * DQK)).rearrange("p (a d) -> p a d", a=4)).then_inc(consts_in, 16)

            pool.wait_ge(split_ready, 1)
            for k in range(KT):
                pool.wait_ge(sq_ready, k + 1)
                pool.tensor_tensor(ssq[:], ssq[:], (stage[:, 0], rstd[:])[k % 2], ALU.add).then_inc(sq_added, 1)
                pool.wait_ge(sq_added, k + 1)
            pool.wait_ge(qps_free, 1)
            pool.memset(qps[:], 0.0).then_inc(qps_zero, 1)

            def add_squares(n):
                pool.wait_ge(ssq_zero, n)
                with pool.Fori(0, KT // 2) as t:
                    for s in range(2):
                        pool.wait_ge(sq_ready, 2 * t + (KT * n + s + 1))
                        pool.tensor_tensor(ssq[:], ssq[:], stage[:, s], ALU.add).then_inc(sq_added, 1)
                        pool.wait_ge(sq_added, 2 * t + (KT * n + s + 1))

            add_squares(1)
            pool.wait_ge(pad_free, 1)
            pool.memset(u_ext[:, 0:PAD], 0.0).then_inc(pad_zero, 1)
            add_squares(2)

        @block.tensor
        def _(pe):
            def small(out, lhsT, rhs, start, stop):
                return pe.matmul(out, lhsT, rhs, start=start, stop=stop)

            def row_sums(n):
                if n == 0:
                    pe.wait_ge(ones_ready, 1)
                pe.wait_ge(sq_added, KT * (n + 1))
                for a in range(2):
                    m = small(PS[:, (6 if n else 2) + a, 0:HALF], ones[:], ssq[:, a * HALF:(a + 1) * HALF], True, True)
                m.then_inc(var_ready, 1)

            pe.wait_ge(cond_ready, 1)

            def ada_turn(c):
                if c == 0:
                    pe.wait_ge(consts_in, CONSTS)
                pe.wait_ge(ada_row, c + 1)
                for q in range(4):
                    f = 2 * (4 * c + q)
                    m = pe.transpose(PS[:, 1, f:f + 2], stage[0:2, 1, q * P:(q + 1) * P], id_t[0:2, 0:2])
                m.then_inc(ada_turned, 1)

            for g in range(ADA_PE):
                c = g // 4
                pe.wait_ge(raw_in[g % 2], 16 * (g // 2 + 1))
                if g % 4 == 0 and c:
                    pe.wait_ge(ada_row, c)
                for k in range(4):
                    m = small(PS[0:2, 0, :], cond_t[:, 4 * (g % 4) + k, :], w_raw[:, g % 2, k * 512:(k + 1) * 512],
                              g % 4 == 0 and k == 0, g % 4 == 3 and k == 3)
                m.then_inc(mm_done, 1)
                if g % 4 == 1 and c:
                    ada_turn(c - 1)
                if g == ADA_PE - 3:
                    row_sums(0)

            def big_tile(slot, h_wait=None):
                for k in range(KT):
                    if h_wait is not None:
                        pe.wait_ge(h_ready, h_wait + k + 3)
                    ks = slice(k * P, (k + 1) * P)
                    for i, (w, h) in enumerate(((w_hi, h_hi), (w_hi, h_lo), (w_lo, h_hi))):
                        for a in range(2):
                            m = small(PS[:, 2 * slot + a, 0:HALF], w[:, slot, ks], h[:, k, a * HALF:(a + 1) * HALF],
                                      k == 0 and i == 0, k == KT - 1 and i == 2)
                m.then_inc(mm_done, 1)

            def big_wait(g, twice_t=0, t=0):
                pe.wait_ge(split_ready, twice_t + (g - G_KPE + 2))
                pe.wait_ge(acc_free[g % 2], t + turn_of(g))

            def big_loop(g0, first, end):
                with pe.Fori(first, end) as t:
                    for s in range(2):
                        big_wait(g0 + s, 2 * t, t)
                        big_tile((g0 + s) % 2)

            ada_turn(CHUNKS - 1)
            big_wait(G_KPE)
            big_tile(G_KPE % 2, 0)
            big_loop(G_Z, 0, ZT // 2)
            big_loop(G_GATE, 0, GT // 2)

            for s in range(2):
                pe.wait_ge(acc_free[s], turn_of(G_OUT + (G_OUT + s) % 2))
            for a in range(2):
                pe.wait_ge(mq_sq, a + 1)
                for hf in range(2):
                    for c in range(LT):
                        m = small(PS[:, 2 * a + hf, 0:HALF], ones[:], ql[:, a, c, hf * HALF:(hf + 1) * HALF], c == 0, c == LT - 1)
                m.then_inc(mq_sum, 1)
            for a in range(2):
                m = small(PS[:, 6 + a, 0:HALF], swap_t[:], kpe[:, a * HALF:(a + 1) * HALF], True, True)
            m.then_inc(kp_swap, 1)
            pe.wait_ge(mq_norm, 2)
            for j in range(QT + 1):
                nk = P if j < QT else NS
                if j >= 2:
                    pe.wait_ge(mq_ev, j - 1)
                for c in range(LT):
                    m = pe.transpose(PS[0:nk, 4 + j % 2, c * P:(c + 1) * P], ckT[:, c, j * P:j * P + nk], id_t[:])
                m.then_inc(mq_tr, 1)
            pe.wait_ge(mq_ev, QT + 1)
            pe.wait_ge(kp_done, 1)

            with pe.Fori(0, HEADS // 2) as t:
                def item_free(k):
                    if k >= 3:
                        pe.wait_ge(ml_item_ev, 11 * t + k - 2)

                def item_banks(k):
                    return 2 * (k % 3)

                pe.wait_ge(ml_w_in, 80 * t + 80)
                for k in range(3):
                    for hf in range(2):
                        for c in range(LT):
                            w = wq[:, k, c, :] if k < 2 else wr[:, c, :]
                            m = small(PS[:, item_banks(k) + hf, 0:HALF], w, cq[:, c, hf * HALF:(hf + 1) * HALF],
                                      c == 0, c == LT - 1)
                    m.then_inc(ml_item, 1)
                for k in range(3, 11):
                    s, c = (k - 3) // LT, (k - 3) % LT
                    item_free(k)
                    pe.wait_ge(ml_item_ev, 11 * t + max(s + 1, k - 2))
                    for hf in range(2):
                        m = small(PS[:, item_banks(k) + hf, 0:HALF], wk[:, s, c * P:(c + 1) * P],
                                  qn[:, s, hf * HALF:(hf + 1) * HALF], True, True)
                    m.then_inc(ml_item, 1)
                    if k == 5:
                        for hf in range(2):
                            m = small(PS[:, 6 + hf, 0:HALF], swap_t[:], qpr[:, hf * HALF:(hf + 1) * HALF], True, True)
                        m.then_inc(ml_swap, 1)

                def scores(u):
                    s, i = u // QT, u % QT
                    n, b = P * (i + 1), u % 4
                    if u >= 4:
                        pe.wait_ge(ml_exp, 8 * t + u - 3)
                    qs = slice(P * i, P * i + P)
                    for c in range(LT):
                        small(PS[:, b, 0:n], ql[:, s, c, qs], ckT[:, c, 0:n], c == 0, False)
                        if c == 0:
                            small(PS[:, b, n - DQK:n], maskq_t[:], maskk_t[:], False, False)
                    e = slice(DQK * s, DQK * s + DQK)
                    small(PS[:, b, 0:n], qpe[e, qs], kpe[e, 0:n], False, True).then_inc(ml_score, 1)

                def turn(u):
                    i = u % QT
                    pe.wait_ge(ml_norm, 8 * t + u + 1)
                    if u >= 2:
                        pe.wait_ge(ml_ptev, 8 * t + u - 1)
                    for j in range(i + 1):
                        m = pe.transpose(PS[:, 4 + u % 2, j * P:(j + 1) * P], px[:, u % 3, j * P:(j + 1) * P], id_t[:])
                    m.then_inc(ml_tr, 1)

                def values(s):
                    pe.wait_ge(ml_ptev, 8 * t + 4 * s + 4)
                    for c in range(LT):
                        q = 5 * s + c
                        if s == 1 and c == 1:
                            pe.wait_ge(ml_fin, 2 * t + 1)
                        elif q >= 2:
                            pe.wait_ge(ml_olev, 8 * t + (c - 1 if s == 0 else (4 if c == 0 else 3 + c)))
                        for j in range(QT):
                            m = small(PS[:, 6 + q % 2, P * j:NP], ckR[:, j, c * P:(c + 1) * P], pt[:, j, P * j:NP],
                                      j == 0, j == QT - 1)
                        m.then_inc(ml_pv, 1)
                    pe.wait_ge(ml_olev, 8 * t + 4 * s + 4)
                    pe.wait_ge(ml_v_in, 64 * t + 64)
                    for c in range(LT):
                        m = small(PS[:, 6 + (5 * s + 4) % 2, :], wv[:, s, c, :], ol[:, c, :], c == 0, c == LT - 1)
                    m.then_inc(ml_pv, 1)

                pe.wait_ge(ml_item_ev, 11 * t + 11)
                pe.wait_ge(ml_qpe, t + 1)
                for u in range(10):
                    if u < 8:
                        scores(u)
                    if u >= 2:
                        turn(u - 2)
                    if u == 5:
                        values(0)
                values(1)
                pe.wait_ge(ml_fin, 2 * t + 2)

            pe.wait_ge(ms_in, 16 * (3 + HEADS))
            SPLIT = HALF
            for g in range(2):
                heads = slice(4 * g, 4 * g + 4)
                for bank, cols, keys_c, keys_p in ((2 * g, slice(0, SPLIT), lambda c: ccT[:, c, 0:SPLIT], kpc[:, 0:SPLIT]),
                                                   (2 * g + 1, slice(0, PAST - SPLIT), lambda c: ccT[:, c, SPLIT:PAST], kpc[:, SPLIT:PAST]),
                                                   (2 * g + 1, slice(PAST - SPLIT, SPLIT), lambda c: ckT[:, c, NP:R], kpe[:, NP:R])):
                    for c in range(LT):
                        small(PS[:, bank, cols], qls[:, c, heads, :].rearrange("p h r -> p (h r)"), keys_c(c), c == 0, False)
                    m = small(PS[:, bank, cols], qps[:, heads, :].rearrange("p h r -> p (h r)"), keys_p, False, True)
                m.then_inc(ms_score, 1)
            for g in range(2):
                pe.wait_ge(ms_norm, g + 1)
                for j in range(KTS):
                    nk = P if j < KTS - 1 else NS
                    dst = PS[0:nk, 4 + g, j * P:(j + 1) * P] if j < KTS - 1 else PS[0:nk, 6 + g, 0:P]
                    m = pe.transpose(dst, pxs[:, g, j * P:j * P + nk], id_t[:])
                m.then_inc(ms_tr, 1)
            for g in range(2):
                pe.wait_ge(ms_ptev, g + 1)
                for c in range(LT):
                    cs = slice(c * P, (c + 1) * P)
                    for j in range(KTS):
                        last = j == KTS - 1
                        m = small(PS[:, g, cs], ckR[0:NS, QT, cs] if last else ccR[:, j, cs],
                                  pts[0:NS, g, j, :] if last else pts[:, g, j, :], j == 0, last)
                m.then_inc(ms_pv, 1)
            pe.wait_ge(ms_olev, 2)
            for h in range(HEADS):
                for c in range(LT):
                    m = small(PS[:, 2, NS * h:NS * h + NS], wva[:, c, h * P:(h + 1) * P], ols[:, c, h, :], c == 0, c == LT - 1)
            m.then_inc(ms_ob, 1)
            pe.wait_ge(ms_fin, 1)

            with pe.Fori(0, HEADS // 2) as t:
                pe.wait_ge(df_v_in, 64 * t + 64)
                for s in range(2):
                    if s:
                        pe.wait_ge(df_vrev, 2 * t + 1)
                    for j in range(KTS):
                        nk = P if j < KTS - 1 else NS
                        dst = PS[0:nk, 6, j * P:(j + 1) * P] if j < KTS - 1 else PS[0:nk, 7, 0:P]
                        m = pe.transpose(dst, vd[:, s, j * P:j * P + nk], id_t[:])
                    m.then_inc(df_vt, 1)
                pe.wait_ge(df_a_in, 96 * t + 96)

                def scores(u):
                    s, i = u // QT, u % QT
                    n = P * (i + 1)
                    if u >= 2:
                        pe.wait_ge(df_exp, 8 * t + u - 1)
                    for e in range(2):
                        b, es = 2 * (u % 2) + e, slice(DQK * e, DQK * e + DQK)
                        small(PS[:, b, 0:n], qd[es, s, P * i:P * i + P], kd[es, s, 0:n], True, False)
                        m = small(PS[:, b, n - DQK:n], maskq_t[:], maskk_t[:], False, True)
                    m.then_inc(df_score, 1)

                def turn(u):
                    i = u % QT
                    pe.wait_ge(df_norm, 8 * t + u + 1)
                    if u >= 2:
                        pe.wait_ge(df_ptev, 8 * t + u - 1)
                    for j in range(i + 1):
                        m = pe.transpose(PS[:, 4 + u % 2, j * P:(j + 1) * P], pxd[:, u % 3, 0, j * P:(j + 1) * P], id_t[:])
                    m.then_inc(df_tr, 1)

                def values(s):
                    if s == 0:
                        pe.wait_ge(df_vrev, 2 * t + 2)
                    pe.wait_ge(df_ptev, 8 * t + 4 * s + 4)
                    for j in range(QT):
                        m = small(PS[:, 6 + s, P * j:NP], vr[:, s, j, :], ptd[:, s, j, P * j:NP], j == 0, j == QT - 1)
                    m.then_inc(df_pv, 1)

                def sample_scores():
                    for s in range(2):
                        for e in range(2):
                            r, es = 32 * (2 * s + e), slice(DQK * e, DQK * e + DQK)
                            q = qd[es, s, NP:R]
                            small(PS[r:r + 32, 0, 0:HALF], q, kcs[es, s, 0:HALF], True, True)
                            small(PS[r:r + 32, 1, 0:PAST - HALF], q, kcs[es, s, HALF:PAST], True, True)
                            m = small(PS[r:r + 32, 1, PAST - HALF:HALF], q, kd[es, s, NP:R], True, True)
                    m.then_inc(dfs_score, 1)

                for u in range(10):
                    if u < 8:
                        scores(u)
                    if u >= 2:
                        turn(u - 2)
                    if u == 8:
                        sample_scores()
                    if u == 5:
                        values(0)
                values(1)
                pe.wait_ge(dfs_norm, t + 1)
                pe.wait_ge(df_ptev, 8 * t + 8)
                for j in range(KTS):
                    nk = P if j < KTS - 1 else NS
                    dst = PS[0:nk, 4, j * P:(j + 1) * P] if j < KTS - 1 else PS[0:nk, 5, 0:P]
                    m = pe.transpose(dst, pxds[:, j * P:j * P + nk], id_t[:])
                m.then_inc(dfs_tr, 1)
                pe.wait_ge(dfs_ptev, t + 1)
                pe.wait_ge(df_exp, 8 * t + 8)
                for s in range(2):
                    n = 0
                    for j in range(KTS):
                        last = j == KTS - 1
                        for e in range(2):
                            cs = slice(32 * (2 * s + e), 32 * (2 * s + e) + 32)
                            m = small(PS[:, 2 + s, 0:NS], vr[0:NS, s, QT, :] if last else vcs[:, s, j, :],
                                      ptds[0:NS, j, cs] if last else ptds[:, j, cs], n == 0, n == 2 * KTS - 1)
                            n += 1
                m.then_inc(dfs_pv, 1)
                pe.wait_ge(df_sq, t + 1)
                for s in range(2):
                    for a in range(2):
                        m = small(PS[:, 2 * s + a, 0:HALF], ones[:], sqd[:, s, a * HALF:(a + 1) * HALF], True, True)
                m.then_inc(df_ssq, 1)
                pe.wait_ge(df_fin, 2 * t + 2)

            big_loop(G_OUT, 0, KT // 2)
            row_sums(1)
            for s in range(2):
                big_wait(G_PIN + s)
                big_tile((G_PIN + s) % 2, KT)
            big_loop(G_PIN, 1, KT)
            for g in range(4):
                slot = (G_GRP + g) % 2
                pe.wait_ge(split_ready, G_GRP + g - G_KPE + 2)
                pe.wait_ge(d_split, g + 1)
                for n in range(4):
                    q = 4 * g + n
                    if q < 2:
                        pe.wait_ge(acc_free[n], turn_of(G_GRP + (G_GRP + n) % 2))
                    else:
                        pe.wait_ge(grp_y, q - 1)
                    for k in range(4):
                        ks = slice(k * LORA + n * P, k * LORA + (n + 1) * P)
                        for i, (w, d) in enumerate(((w_hi, d_hi), (w_hi, d_lo), (w_lo, d_hi))):
                            for a in range(2):
                                m = small(PS[:, 2 * (n % 2) + a, 0:HALF], w[:, slot, ks], d[:, k, a * HALF:(a + 1) * HALF],
                                          k == 0 and i == 0, k == 3 and i == 2)
                    m.then_inc(grp_mm, 1)
                pe.wait_ge(grp_mm, 4 * g + 4)
                pe.nop().then_inc(mm_done, 1)
            pe.wait_ge(y_ready, KT)
            big_loop(G_POUT, 0, KT // 2)
            row_sums(2)

        def parts(ap_rows):
            return ((0, slice(0, HALF), slice(0, HALF), 0), (1, slice(0, NP - HALF), slice(HALF, NP), 0),
                    (1, slice(NP - HALF, HALF), slice(NP, R), 1))

        @block.scalar
        def _(act):
            act.wait_ge(cond_in, 16)
            act.activation(cond_t[:], cond_t[:], ACT.Silu).then_inc(cond_ready, 1)
            act.wait_ge(condb_in, 16)
            act.activation(cond_b[:], cond_b[:], ACT.Silu).then_inc(condb_ready, 1)

            def square(k, dst):
                act.activation(dst, at(x, k), ACT.Square).then_inc(sq_ready, 1)

            for c in range(CHUNKS):
                act.wait_ge(mm_done, 4 * c + 4)
                if c:
                    act.wait_ge(ada_turned, c)
                act.activation(stage[0:2, 1, 0:512], PS[0:2, 0, :], ACT.Copy).then_inc(ada_row, 1)
                for k in range(8 * c, 8 * c + 8) if c < 2 else ():
                    if k == 0:
                        act.wait_ge(x_in, 16)
                    if k >= 2:
                        act.wait_ge(sq_added, k - 1)
                    act.activation((stage[:, 0], rstd[:])[k % 2], x[:, k], ACT.Square).then_inc(sq_ready, 1)
            act.wait_ge(ada_row, CHUNKS)
            for s in range(2):
                act.activation(act_tmp[0:1, s:s + 1], stage[0:1, 1, 0:1], ACT.Copy).then_inc(acc_free[s], 1)

            def root(n):
                act.wait_ge(var_eps, n + 1)
                act.activation(rstd[:], rstd[:], ACT.Sqrt).then_inc(std_ready, 1)

            def affine(n):
                with act.Fori(0, KT // 2) as t:
                    for s in range(2):
                        if n == 0:
                            act.wait_ge(x_normed, 2 * t + (s + 1))
                            act.wait_ge(h_ready, 2 * t + (s + 1))
                        else:
                            act.wait_ge(xn_ready, 2 * t + (s + 1))
                        for c, r in ((0, slice(0, NP)), (1, slice(NP, R))):
                            src = at(x, 2 * t + s)[:, r] if n == 0 else stage[:, s, r]
                            ins = act.activation(stage[:, s, r], src, ACT.Identity,
                                                 scale=aff[:, c, bass.ds(2 * t + s, 1)],
                                                 bias=mod[:, c, bass.ds(2 * t + (3 * KT * n + s), 1)])
                        ins.then_inc(hf_ready, 1)

            root(0)
            affine(0)
            act.wait_ge(mm_done, G_KPE + 1)
            act.activation(rows(kpe[:]), acc[G_KPE % 2], ACT.Copy).then_inc(acc_free[G_KPE % 2], 1)

            def load_ada(t, s, a):
                act.wait_ge(adr_used, 2 * t + (a + 1))
                act.dma_start(w_adr[:, a % 2], tile_of(wd2, s, t + (a // 2 + 1))).then_inc(adr_in[a % 2], 16)

            def store_loop(g0, first, end, func, out2, base, ada=None):
                with act.Fori(first, end) as t:
                    for s in range(2):
                        if ada is not None:
                            load_ada(t, s, ada + s)
                        slot = (g0 + s) % 2
                        act.wait_ge(mm_done, 2 * t + (g0 + s + 1))
                        act.activation(rows(stage[:, s]), acc[slot], func).then_inc(acc_free[slot], 1)
                        act.wait_ge(acc_free[slot], t + turn_of(g0 + s + 2))
                        act.dma_start(tile_of(out2, s, t), stage[:, s]).then_inc(stored[s], 16)
                    for s in range(2):
                        act.wait_ge(stored[s], 16 * t + (base + 16))

            store_loop(G_Z, 0, ZT // 2, ACT.Copy, z2, 0, ADA_P0)
            store_loop(G_GATE, 0, GT // 2 - 1, ACT.Silu, g2, 16 * ZT // 2, ADA_P0 + ZT)
            store_loop(G_GATE, GT // 2 - 1, GT // 2, ACT.Silu, g2, 16 * ZT // 2)

            act.wait_ge(lam_sum, 1)
            act.activation(lam_w[:, 2:4], lam_w[:, 0:2], ACT.Exp).then_inc(lam_exp, 1)

            act.wait_ge(mq_in, 64)
            act.activation(ql[:, 0], cq[:], ACT.Square).then_inc(mq_sq, 1)
            act.activation(ql[:, 1], ckT[:], ACT.Square).then_inc(mq_sq, 1)
            for a in range(2):
                act.wait_ge(mq_var, a + 1)
                act.activation(qn[:, a], qn[:, a], ACT.Sqrt).then_inc(mq_std, 1)
            act.wait_ge(mq_norm, 2)
            act.dma_start(ckv_out.rearrange("t p r -> p t r"), ckT[:]).then_inc(latent_out, 16)
            act.wait_ge(kp_done, 1)
            act.dma_start(kpe_out, kpe[0:DQK, :]).then_inc(latent_out, 16)
            for j in range(QT + 1):
                nk = P if j < QT else NS
                act.wait_ge(mq_tr, j + 1)
                act.activation(ckR[0:nk, j, :], PS[0:nk, 4 + j % 2, :], ACT.Copy).then_inc(mq_ev, 1)

            with act.Fori(0, HEADS // 2) as t:
                def latent_values(s):
                    if s == 1:
                        act.wait_ge(ml_pv, 10 * t + 5)
                    for c in range(LT):
                        q = 5 * s + c
                        act.wait_ge(ml_pv, 10 * t + q + 1)
                        act.activation(ol[:, c, :], PS[:, 6 + q % 2, :], ACT.Copy).then_inc(ml_olev, 1)

                for u in range(8):
                    n = P * (u % QT + 1)
                    if u >= 3:
                        act.wait_ge(ml_tr, 8 * t + u - 2)
                    act.wait_ge(ml_max, 8 * t + u + 1)
                    act.activation(px[:, u % 3, 0:n], PS[:, u % 4, 0:n], ACT.Exp, bias=st[:, 1, u:u + 1],
                                   scale=MLA_SCALE, accum_out=st[:, 2, u:u + 1]).then_inc(ml_exp, 1)
                    if u == 5:
                        latent_values(0)
                latent_values(1)
                act.wait_ge(ml_fin, 2 * t + 2)

            for g in range(2):
                act.wait_ge(ms_max, g + 1)
                act.activation(rows(pxs[:, g]), PS[:, 2 * g:2 * g + 2, 0:HALF], ACT.Exp, bias=sts[:, g, 1:2],
                               scale=MLA_SCALE, accum_out=sts[:, g, 2:3]).then_inc(ms_exp, 1)
            for g in range(2):
                act.wait_ge(ms_pv, g + 1)
                act.activation(ols[:, :, 4 * g:4 * g + 4, :].rearrange("p c h r -> p c (h r)"),
                               PS[:, g, :].rearrange("p (c n) -> p c n", c=LT), ACT.Copy).then_inc(ms_olev, 1)

            with act.Fori(0, HEADS // 2) as t:
                for s in range(2):
                    act.wait_ge(df_vt, 2 * t + s + 1)
                    act.activation(vr[:, s, 0:QT, :].rearrange("p j e -> p (j e)"), PS[:, 6, :], ACT.Copy)
                    act.activation(vr[0:NS, s, QT, :], PS[0:NS, 7, 0:P], ACT.Copy).then_inc(df_vrev, 1)
                for u in range(8):
                    n, slot = P * (u % QT + 1), u % 3
                    if u >= 3:
                        act.wait_ge(df_tr, 8 * t + u - 2)
                    act.wait_ge(df_max, 8 * t + u + 1)
                    for e in range(2):
                        ins = act.activation(pxd[:, slot, e, 0:n], PS[:, 2 * (u % 2) + e, 0:n], ACT.Exp,
                                             bias=std[:, u, 2 + e:3 + e], scale=DIFF_SCALE,
                                             accum_out=std[:, u, 4 + e:5 + e])
                    ins.then_inc(df_exp, 1)
                    if u == 5:
                        act.wait_ge(df_pv, 2 * t + 1)
                        act.activation(od[:, 0, 0:NP], PS[:, 6, :], ACT.Copy)
                act.wait_ge(dfs_max, t + 1)
                act.activation(rows(pxds[:]), PS[:, 0:2, 0:HALF], ACT.Exp, bias=std[:, 8, 1:2],
                               scale=DIFF_SCALE, accum_out=std[:, 8, 2:3]).then_inc(dfs_exp, 1)
                act.wait_ge(df_pv, 2 * t + 2)
                act.activation(od[:, 1, 0:NP], PS[:, 7, :], ACT.Copy)
                act.wait_ge(dfs_pv, t + 1)
                for s in range(2):
                    ins = act.activation(od[:, s, NP:R], PS[:, 2 + s, 0:NS], ACT.Copy)
                ins.then_inc(df_od, 1)
                act.wait_ge(df_od, t + 1)
                act.activation(sqd[:], od[:], ACT.Square).then_inc(df_sq, 1)
                act.wait_ge(df_var, t + 1)
                act.activation(rsd[:], rsd[:], ACT.Sqrt).then_inc(df_std, 1)
                act.wait_ge(df_fin, 2 * t + 2)

            act.wait_ge(condb_in, 32)
            act.activation(cond_b[:], cond_b[:], ACT.Silu).then_inc(condb_ready, 1)

            def gated(t, g0, n, gate_tile, ada=None):
                for s in range(2):
                    if ada is not None:
                        load_ada(t, s, ada + s)
                    slot = (g0 + s) % 2
                    act.wait_ge(mm_done, 2 * t + (g0 + s + 1))
                    act.wait_ge(sq_added, 2 * t + (KT * n + s - 1))
                    for bank, cols, r, c in parts(R):
                        ins = act.activation(stage[:, s, r], PS[:, 2 * slot + bank, cols], ACT.Identity,
                                             scale=mod[:, c, bass.ds(2 * t + (gate_tile + s), 1)])
                    ins.then_inc(acc_free[slot], 1)
                    act.wait_ge(x_new, 2 * t + (KT * (n - 1) + s + 1))
                    square(2 * t + s, stage[:, s])

            with act.Fori(0, KT // 2 - 1) as t:
                gated(t, G_OUT, 1, 2 * KT, ADA_P0 + ADA_P1)
            with act.Fori(KT // 2 - 1, KT // 2) as t:
                gated(t, G_OUT, 1, 2 * KT)
            root(1)
            affine(1)

            act.wait_ge(pad_zero, 1)
            with act.Fori(0, KT) as t:
                us, gs = G_PIN % 2, (G_PIN + 1) % 2
                act.activation(u_ext[:, PAD + NP:2 * PAD + NP], at(pool_pre, t), ACT.Copy)
                act.wait_ge(mm_done, 2 * t + (G_PIN + 1))
                for bank, cols, r, c in parts(R):
                    off = PAD + r.start + PAD * c
                    ins = act.activation(u_ext[:, off:off + r.stop - r.start], PS[:, 2 * us + bank, cols], ACT.Copy)
                ins.then_inc(acc_free[us], 1)
                act.wait_ge(d_ready, t + 1)
                act.dma_start(d_scr[bass.ds(t, 1)].rearrange("t p r -> p (t r)"), d_st[:]).then_inc(d_stored, 16)
                act.wait_ge(mm_done, 2 * t + (G_PIN + 2))
                act.activation(rows(stage[:, 1]), acc[gs], ACT.Silu).then_inc(acc_free[gs], 1)
                act.wait_ge(acc_free[gs], t + turn_of(G_PIN + 3))
                act.dma_start(pg_scr[bass.ds(t, 1)].rearrange("t p r -> p (t r)"), stage[:, 1]).then_inc(pg_stored, 16)
                act.wait_ge(pg_stored, 16 * t + 16)
            act.dma_start(pool_out, pool_last[:]).then_inc(out_done, 16)

            with act.Fori(0, KT // 2) as t:
                gated(t, G_POUT, 2, 5 * KT)
            root(2)

        @block.vector
        def _(dve):
            dve.memset(ssq[:], 0.0).then_inc(split_ready, 1)
            dve.wait_ge(split_ready, 1)

            def row_scale(n):
                dve.wait_ge(var_ready, n + 1)
                sums = PS[:, 6:8, 0:HALF] if n else PS[:, 2:4, 0:HALF]
                dve.tensor_scalar(rows(rstd[:]), sums, 1.0 / D, EPS, ALU.mult, ALU.add).then_inc(var_eps, 1)
                if n < 2:
                    dve.memset(ssq[:], 0.0).then_inc(ssq_zero, 1)
                    dve.wait_ge(ssq_zero, n + 1)
                dve.wait_ge(std_ready, n + 1)
                vchain(dve, dve.reciprocal(rstd[:], rstd[:]))

            def add_bias(a, b):
                for c in range(2):
                    ins = dve.tensor_tensor(mod[:, c, a:b], mod[:, c, a:b], bada_t[:, a:b], ALU.add)
                vchain(dve, ins)

            def fold_scale(n):
                a = (3 * n + 1) * KT
                for c in range(2):
                    ins = dve.scalar_tensor_tensor(out=aff[:, c, :], in0=mod[:, c, a:a + KT], scalar=1.0,
                                                   in1=gnorm_t[:, n, :], op0=ALU.add, op1=ALU.mult)
                vchain(dve, ins)

            def split(g, t2=0, t=0):
                slot = g % 2
                dve.wait_ge(raw_in[slot], 16 * t + 16 * (g // 2 + 1))
                dve.wait_ge(mm_done, t2 + (g - 1))
                vchain(dve, dve.tensor_copy(w_hi[:, slot], w_raw[:, slot]))
                dve.tensor_tensor(w_lo[:, slot], w_raw[:, slot], w_hi[:, slot].bitcast(F32),
                                  ALU.subtract).then_inc(split_ready, 1)

            def make_h(n):
                with dve.Fori(0, KT // 2) as t:
                    dv.loop(t, 2)
                    for s in range(2):
                        if n:
                            dve.tensor_tensor(stage[:, s], at(x, 2 * t + s), rstd[:], ALU.mult).then_inc(xn_ready, 1)
                    for s in range(2):
                        dve.wait_ge(hf_ready, 2 * t + (KT * n + s + 1))
                        vchain(dve, dve.tensor_copy(at(h_hi, 2 * t + s), stage[:, s]))
                        dve.tensor_tensor(at(h_lo, 2 * t + s), stage[:, s], at(h_hi, 2 * t + s).bitcast(F32),
                                          ALU.subtract).then_inc(h_ready, 1)
                    dve.wait_ge(h_ready, 2 * t + (KT * n + 4))
                dv.end(KT // 2)

            def ada_tile(a, t2, t):
                slot = a % 2
                dve.wait_ge(adr_in[slot], 16 * t + 16 * (a // 2 + 1))
                for c in range(2):
                    ins = dve.tensor_tensor_reduce(ada_junk, w_adr[:, slot], cond_b[:, c, :], 1.0, 0.0, ALU.mult, ALU.add,
                                                   ada_acc[:, c:c + 1])
                    if c == 0:
                        vchain(dve, ins)
                ins.then_inc(adr_used, 1)
                dve.wait_ge(adr_used, t2 + a + 1)
                vchain(dve, dve.tensor_copy(mod[:, :, bass.ds(t2 + (ADA_PE + a), 1)].rearrange("p c k -> p (c k)"),
                                            ada_acc[:]))

            dve.wait_ge(condb_ready, 1)
            with dve.Fori(0, ADA_P0 // 2) as t:
                dv.loop(t, 4)
                for s in range(2):
                    ada_tile(s, 2 * t, t)
            dv.end(ADA_P0 // 2)
            row_scale(0)
            for k in range(KT):
                dve.tensor_tensor(x[:, k], x[:, k], rstd[:], ALU.mult).then_inc(x_normed, 1)
            dve.wait_ge(consts_in, CONSTS)
            add_bias(ADA_PE, ADA_PE + ADA_P0)
            split(G_KPE)
            dve.wait_ge(ada_turned, CHUNKS)
            turned = PS[:, 1, 0:2 * ADA_PE].rearrange("p (t c) -> p c t", c=2)
            for c in range(2):
                ins = dve.tensor_tensor(mod[:, c, 0:ADA_PE], turned[:, c, :], bada_t[:, 0:ADA_PE], ALU.add)
            vchain(dve, ins)
            fold_scale(0)
            dve.wait_ge(sq_added, KT)
            for s in range(2):
                dve.memset(ada_acc[:, s:s + 1], 0.0).then_inc(h_ready, 1)
            make_h(0)
            with dve.Fori(0, ZT // 2) as t:
                dv.loop(t, 6)
                for s in range(2):
                    split(G_Z + s, 2 * t, t)
                    ada_tile(ADA_P0 + s, 2 * t, t)
            dv.end(ZT // 2)
            with dve.Fori(0, GT // 2) as t:
                dv.loop(t, 6)
                for s in range(2):
                    split(G_GATE + s, 2 * t, t)
                    ada_tile(ADA_P0 + ZT + s, 2 * t, t)
            dv.end(GT // 2)
            add_bias(ADA_PE + ADA_P0, ADA_PE + ADA_P0 + ADA_P1)

            for i in range(2):
                ins = dve.tensor_tensor_reduce(lam_in[:, 2 * i, :], lam_in[:, 2 * i, :], lam_in[:, 2 * i + 1, :], 1.0, 0.0,
                                               ALU.mult, ALU.add, lam_w[:, i:i + 1])
            ins.then_inc(lam_sum, 1)
            dve.wait_ge(lam_exp, 1)
            vchain(dve, dve.tensor_tensor(lam_w[:, 4:5], lam_w[:, 3:4], lam_w[:, 2:3], ALU.subtract))
            vchain(dve, dve.tensor_scalar(neg_lam, lam_w[:, 4:5], -LAM_INIT, None, ALU.add))
            vchain(dve, dve.scalar_tensor_tensor(out=coef, in0=lamsel_t[:, 1:2], scalar=neg_lam, in1=lamsel_t[:, 0:1],
                                                 op0=ALU.mult, op1=ALU.add))
            vchain(dve, dve.tensor_scalar(gsub_v, gsub_v, 1.0 - LAM_INIT, None, ALU.mult))

            dve.wait_ge(mm_done, G_OUT)
            for s in range(2):
                dve.wait_ge(acc_free[s], turn_of(G_OUT + (G_OUT + s) % 2))
            dve.wait_ge(stored[0], 16 * (ZT + GT) // 2)
            dve.wait_ge(stored[1], 16 * (ZT + GT) // 2)
            dve.memset(lam_in[:, 0, 0:1], 0.0).then_inc(qps_free, 1)
            for a in range(2):
                dve.wait_ge(mq_sum, a + 1)
                dve.tensor_scalar(rows(qn[:, a]), PS[:, 2 * a:2 * a + 2, 0:HALF], 1.0 / LORA, EPS, ALU.mult,
                                  ALU.add).then_inc(mq_var, 1)
            dve.wait_ge(kp_swap, 1)
            dve.tensor_tensor(rows(qpr[:]), PS[:, 6:8, 0:HALF], rows(sin_t[:]), ALU.mult)
            vchain(dve, dve.tensor_tensor(kpe[:], kpe[:], cos_t[:], ALU.mult))
            dve.tensor_tensor(kpe[:], kpe[:], qpr[:], ALU.add).then_inc(kp_done, 1)
            for a, (lat, g_v) in enumerate(((cq, gqa_v), (ckT, gkva_v))):
                dve.wait_ge(mq_std, a + 1)
                vchain(dve, dve.reciprocal(qn[:, a], qn[:, a]))
                for c in range(LT):
                    ins = dve.scalar_tensor_tensor(out=lat[:, c, :], in0=lat[:, c, :], scalar=g_v[:, c:c + 1],
                                                   in1=qn[:, a], op0=ALU.mult, op1=ALU.mult)
                ins.then_inc(mq_norm, 1)

            def halves_of_h(src, hi, lo, done):
                vchain(dve, dve.tensor_copy(hi, src))
                dve.tensor_tensor(lo, src, hi.bitcast(F32), ALU.subtract).then_inc(done, 1)

            dve.wait_ge(qps_zero, 1)
            with dve.Fori(0, HEADS // 2) as t:
                dv.loop(t, 1 + 8 * 2 + 2 * 2)
                for k in range(11):
                    dve.wait_ge(ml_item, 11 * t + k + 1)
                    src = PS[:, 2 * (k % 3):2 * (k % 3) + 2, 0:HALF]
                    dst = qn[:, k] if k < 2 else qpr[:] if k == 2 else ql[:, (k - 3) // LT, (k - 3) % LT]
                    dve.tensor_copy(rows(dst), src).then_inc(ml_item_ev, 1)
                    if k == 5:
                        turned = pt[:, 0:2, :].rearrange("p a b -> p (a b)")[:, 0:R]
                        dve.tensor_tensor(qpe[:], qpr[:], cos_t[:], ALU.mult)
                        dve.wait_ge(ml_swap, t + 1)
                        vchain(dve, dve.tensor_tensor(rows(turned), PS[:, 6:8, 0:HALF], rows(sin_t[:]), ALU.mult))
                        dve.tensor_tensor(qpe[:], qpe[:], turned, ALU.add).then_inc(ml_qpe, 1)
                dve.wait_ge(ml_item_ev, 11 * t + 11)
                dve.wait_ge(ml_qpe, t + 1)
                for s in range(2):
                    e = slice(DQK * s, DQK * s + DQK)
                    dve.tensor_copy(qls[:, :, bass.ds(2 * t + s, 1), :].rearrange("p c h r -> p c (h r)"), ql[:, s, :, NP:R])
                    dve.tensor_copy(qps[e, bass.ds(2 * t + s, 1), :].rearrange("p h r -> p (h r)"), qpe[e, NP:R])

                def maxima(u):
                    n = P * (u % QT + 1)
                    dve.wait_ge(ml_score, 8 * t + u + 1)
                    vchain(dve, dve.tensor_reduce(st[:, 0, u:u + 1], PS[:, u % 4, 0:n], AX.X, ALU.max))
                    dve.tensor_scalar(st[:, 1, u:u + 1], st[:, 0, u:u + 1], -MLA_SCALE, None, ALU.mult).then_inc(ml_max, 1)

                def normalise(u):
                    n = P * (u % QT + 1)
                    dve.wait_ge(ml_exp, 8 * t + u + 1)
                    vchain(dve, dve.reciprocal(st[:, 3, u:u + 1], st[:, 2, u:u + 1]))
                    dve.tensor_scalar(px[:, u % 3, 0:n], px[:, u % 3, 0:n], st[:, 3, u:u + 1], None,
                                      ALU.mult).then_inc(ml_norm, 1)

                def turned_out(u):
                    i = u % QT
                    dve.wait_ge(ml_tr, 8 * t + u + 1)
                    if u == 4:
                        dve.wait_ge(ml_pv, 10 * t + 4)
                    dve.tensor_copy(pt[:, 0:i + 1, P * i:P * i + P],
                                    PS[:, 4 + u % 2, 0:P * (i + 1)].rearrange("p (j q) -> p j q", q=P)).then_inc(ml_ptev, 1)

                def finish(s):
                    dve.wait_ge(ml_pv, 10 * t + 5 * s + 5)
                    dve.wait_ge(ml_v_in, 64 * t + 64)
                    vchain(dve, dve.tensor_tensor(qn[:, s, 0:NP], PS[:, 6 + (5 * s + 4) % 2, :], sg[:, s, 0:NP], ALU.mult))
                    hi, lo = (at(h, 2 * t + (HEADS + s))[:, 0:NP] for h in (h_hi, h_lo))
                    halves_of_h(qn[:, s, 0:NP], hi, lo, ml_fin)

                for u in range(10):
                    if u < 8:
                        maxima(u)
                    if 1 <= u < 9:
                        normalise(u - 1)
                    if u >= 2:
                        turned_out(u - 2)
                    if u == 5:
                        finish(0)
                finish(1)
            dv.end(HEADS // 2)

            for g in range(2):
                dve.wait_ge(ms_score, g + 1)
                vchain(dve, dve.tensor_reduce(sts[:, g, 0:1], PS[:, 2 * g:2 * g + 2, 0:HALF], AX.XY, ALU.max))
                dve.tensor_scalar(sts[:, g, 1:2], sts[:, g, 0:1], -MLA_SCALE, None, ALU.mult).then_inc(ms_max, 1)
            for g in range(2):
                dve.wait_ge(ms_exp, g + 1)
                vchain(dve, dve.reciprocal(sts[:, g, 3:4], sts[:, g, 2:3]))
                dve.tensor_scalar(pxs[:, g], pxs[:, g], sts[:, g, 3:4], None, ALU.mult).then_inc(ms_norm, 1)
            for g in range(2):
                dve.wait_ge(ms_tr, g + 1)
                dve.tensor_copy(pts[:, g, 0:KTS - 1, :].rearrange("p j q -> p (j q)"), PS[:, 4 + g, :])
                dve.tensor_copy(pts[0:NS, g, KTS - 1, :], PS[0:NS, 6 + g, 0:P]).then_inc(ms_ptev, 1)
            dve.wait_ge(ms_ob, 1)
            vchain(dve, dve.tensor_tensor(ofs[:], PS[:, 2, 0:HEADS * NS].rearrange("p (h r) -> p h r", r=NS), sgs[:], ALU.mult))
            halves_of_h(ofs[:], h_hi[:, HEADS:2 * HEADS, NP:R], h_lo[:, HEADS:2 * HEADS, NP:R], ms_fin)

            with dve.Fori(0, HEADS // 2) as t:
                dv.loop(t, 8 * 5 + 4 + 1 + 2 * 3)

                def maxima(u):
                    n, b = P * (u % QT + 1), 2 * (u % 2)
                    dve.wait_ge(df_score, 8 * t + u + 1)
                    vchain(dve, dve.tensor_reduce(std[:, u, 0:2], PS[:, b:b + 2, 0:n], AX.X, ALU.max))
                    dve.tensor_scalar(std[:, u, 2:4], std[:, u, 0:2], -DIFF_SCALE, None, ALU.mult).then_inc(df_max, 1)

                def combine(u):
                    n, slot = P * (u % QT + 1), u % 3
                    dve.wait_ge(df_exp, 8 * t + u + 1)
                    vchain(dve, dve.reciprocal(std[:, u, 6:8], std[:, u, 4:6]))
                    vchain(dve, dve.tensor_scalar(std[:, u, 0:1], std[:, u, 7:8], neg_lam, None, ALU.mult))
                    vchain(dve, dve.tensor_scalar(pxd[:, slot, 1, 0:n], pxd[:, slot, 1, 0:n], std[:, u, 0:1], None, ALU.mult))
                    vchain(dve, dve.scalar_tensor_tensor(out=pxd[:, slot, 0, 0:n], in0=pxd[:, slot, 0, 0:n],
                                                         scalar=std[:, u, 6:7], in1=pxd[:, slot, 1, 0:n],
                                                         op0=ALU.mult, op1=ALU.add))
                    dve.memset(lam_in[:, 0, 0:1], 0.0).then_inc(df_norm, 1)

                def turned_out(u):
                    s, i = u // QT, u % QT
                    dve.wait_ge(df_tr, 8 * t + u + 1)
                    dve.tensor_copy(ptd[:, s, 0:i + 1, P * i:P * i + P],
                                    PS[:, 4 + u % 2, 0:P * (i + 1)].rearrange("p (j q) -> p j q", q=P)).then_inc(df_ptev, 1)

                for u in range(10):
                    if u < 8:
                        maxima(u)
                    if u == 8:
                        dve.wait_ge(dfs_score, t + 1)
                        vchain(dve, dve.tensor_reduce(std[:, 8, 0:1], PS[:, 0:2, 0:HALF], AX.XY, ALU.max))
                        dve.tensor_scalar(std[:, 8, 1:2], std[:, 8, 0:1], -DIFF_SCALE, None, ALU.mult).then_inc(dfs_max, 1)
                    if 1 <= u < 9:
                        combine(u - 1)
                    if u >= 2:
                        turned_out(u - 2)
                dve.wait_ge(dfs_exp, t + 1)
                vchain(dve, dve.reciprocal(std[:, 8, 3:4], std[:, 8, 2:3]))
                vchain(dve, dve.tensor_scalar(std[:, 8, 4:5], std[:, 8, 3:4], coef, None, ALU.mult))
                vchain(dve, dve.tensor_scalar(pxds[:], pxds[:], std[:, 8, 4:5], None, ALU.mult))
                dve.memset(lam_in[:, 0, 0:1], 0.0).then_inc(dfs_norm, 1)
                dve.wait_ge(dfs_tr, t + 1)
                dve.tensor_copy(ptds[:, 0:KTS - 1, :].rearrange("p j q -> p (j q)"), PS[:, 4, :])
                dve.tensor_copy(ptds[0:NS, KTS - 1, :], PS[0:NS, 5, 0:P]).then_inc(dfs_ptev, 1)
                dve.wait_ge(df_ssq, t + 1)
                for s in range(2):
                    ins = dve.tensor_scalar(rows(rsd[:, s]), PS[:, 2 * s:2 * s + 2, 0:HALF], 1.0 / P, SUB_EPS,
                                            ALU.mult, ALU.add)
                ins.then_inc(df_var, 1)
                dve.wait_ge(df_std, t + 1)
                dve.wait_ge(df_g_in, 32 * t + 32)
                vchain(dve, dve.reciprocal(rsd[:], rsd[:]))
                for s in range(2):
                    vchain(dve, dve.scalar_tensor_tensor(out=od[:, s], in0=od[:, s], scalar=gsub_v, in1=rsd[:, s],
                                                         op0=ALU.mult, op1=ALU.mult))
                    vchain(dve, dve.tensor_tensor(od[:, s], od[:, s], sgd[:, s], ALU.mult))
                    halves_of_h(od[:, s], at(h_hi, 2 * t + s), at(h_lo, 2 * t + s), df_fin)
            dv.end(HEADS // 2)

            def update(g, t2, t, n, k, slot):
                dve.wait_ge(acc_free[g % 2], t + turn_of(g + 2))
                dve.tensor_tensor(at(x, t2 + k), at(x, t2 + k), stage[:, slot], ALU.add).then_inc(x_new, 1)

            dve.wait_ge(df_fin, HEADS)
            split(G_OUT)
            dve.wait_ge(x_in, 32)
            dve.wait_ge(condb_ready, 2)
            with dve.Fori(0, KT // 2) as t:
                dv.loop(t, 6)
                for s in range(2):
                    split(G_OUT + s + 1, 2 * t, t)
                    ada_tile(ADA_P0 + ADA_P1 + s, 2 * t, t)
                    update(G_OUT + s, 2 * t, t, 1, s, s)
            dv.end(KT // 2)
            add_bias(ADA_PE + ADA_P0 + ADA_P1, ADA_T)
            dve.memset(lam_in[:, 0, 0:1], 0.0).then_inc(pad_free, 1)
            fold_scale(1)
            row_scale(1)
            make_h(1)

            us = G_PIN % 2
            first, samp = slice(PAD, PAD + NP), slice(2 * PAD + NP, 2 * PAD + R)
            for grp, w in enumerate(WIN):
                with dve.Fori(4 * grp, 4 * grp + 4) as t:
                    t0 = t - 4 * grp
                    dv.loop(t0, 2 + grp + 1 + 1 + 1)
                    dve_t2 = 2 * t
                    split(G_PIN + 1, dve_t2, t)
                    dve.wait_ge(acc_free[us], t + turn_of(G_PIN + 2))
                    width = 2 * PAD + R
                    src = u_ext
                    for step, dst in zip(range(grp + 1), (w2, w4, w2, w4)):
                        lag = 1 << step
                        lo = 2 * lag - 1
                        vchain(dve, dve.tensor_tensor(dst[:, lo:width], src[:, lo:width], src[:, lo - lag:width - lag], ALU.add))
                        src = dst
                    dve.scalar_tensor_tensor(out=d_st[:, NP:R], in0=src[:, samp], scalar=1.0 / w, in1=u_ext[:, samp],
                                             op0=ALU.mult, op1=ALU.subtract)
                    dve.tensor_tensor(fix[:], src[:, PAD:PAD + 16], rcount_t[:, grp, :], ALU.mult)
                    vchain(dve, dve.scalar_tensor_tensor(out=d_st[:, 0:NP], in0=src[:, first], scalar=1.0 / w,
                                                         in1=u_ext[:, first], op0=ALU.mult, op1=ALU.subtract))
                    dve.tensor_tensor(d_st[:, 0:16], fix[:], u_ext[:, PAD:PAD + 16], ALU.subtract)
                    last = pool_last[:, bass.ds(t, 1), :, :].rearrange("p t a k -> p (t a) k")
                    dve.tensor_copy(last[:, 0, :], u_ext[:, NP:PAD + NP])
                    vchain(dve, dve.tensor_copy(last[:, 1, :], u_ext[:, PAD + R:2 * PAD + R]))
                    dve.memset(lam_in[:, 0, 0:1], 0.0).then_inc(d_ready, 1)
                    split(G_PIN + 2, dve_t2, t)
                    dve.wait_ge(d_stored, 16 * t + 16)
                dv.end(4)

            for g in range(4):
                dve.wait_ge(grp_in[0], 16 * g + 16)
                if g:
                    dve.wait_ge(grp_mm, 4 * g)
                vchain(dve, dve.tensor_copy(d_hi[:], d_raw[:]))
                dve.tensor_tensor(d_lo[:], d_raw[:], d_hi[:].bitcast(F32), ALU.subtract).then_inc(d_split, 1)
                split(G_GRP + g + 1)
                dve.wait_ge(grp_in[1], 16 * g + 16)
                for n in range(4):
                    q = 4 * g + n
                    dve.wait_ge(grp_mm, q + 1)
                    dve.scalar_tensor_tensor(out=rows(stage[:, n % 2]), in0=acc[n % 2], scalar=scale_v[:, q:q + 1],
                                             in1=rows(pg[:, n]), op0=ALU.mult, op1=ALU.mult).then_inc(grp_y, 1)
                    dve.wait_ge(grp_y, q + 1)
                    halves_of_h(stage[:, n % 2], h_hi[:, q], h_lo[:, q], y_ready)
                dve.memset(lam_in[:, 0, 0:1], 0.0).then_inc(acc_free[(G_GRP + g) % 2], 1)

            with dve.Fori(0, KT // 2 - 1) as t:
                dv.loop(t, 2)
                for s in range(2):
                    split(G_POUT + s + 1, 2 * t, t)
                    update(G_POUT + s, 2 * t, t, 2, s, s)
            dv.end(KT // 2 - 1)
            split(G_END - 1)
            for k in range(KT - 2, KT):
                update(G_POUT + k, 0, 0, 2, k, k % 2)
            row_scale(2)
            for k in range(KT):
                dve.scalar_tensor_tensor(out=x[:, k], in0=x[:, k], scalar=gfin_v[:, k:k + 1], in1=rstd[:],
                                         op0=ALU.mult, op1=ALU.mult).then_inc(y_fin, 1)


def tables():
    half = DQK // 2
    inv = (np.float32(10000.0) ** (-np.arange(half, dtype=np.float32) / np.float32(half))).astype(np.float32)
    pos = np.concatenate([np.arange(NP), PAST + np.arange(NS)]).astype(np.float32)
    ang = (pos[None, :] * inv[:, None]).astype(np.float32)
    cos, sin = np.tile(np.cos(ang), (4, 1)), np.tile(np.sin(ang), (4, 1))
    swap = np.zeros((P, P), np.float32)
    for m in range(P):
        if m % DQK < half:
            swap[m + half, m] = -1.0
        else:
            swap[m - half, m] = 1.0
    maskq = np.zeros((1, P), np.float32)
    maskq[0, :DQK] = 1.0
    maskk = np.full((1, DQK), MASKED, np.float32)
    rcount = np.zeros((P, 4, 16), np.float32)
    for g, w in enumerate(WIN):
        rcount[:, g, :] = np.float32(1.0) / np.minimum(np.arange(16) + 1, w).astype(np.float32)
    lamsel = np.zeros((P, 2), np.float32)
    for r in range(P):
        lamsel[r, (r // NS) % 2] = 1.0
    return {"cosT": cos.astype(np.float32), "sinT": sin.astype(np.float32), "swap": swap, "ident": np.eye(P, dtype=np.float32),
            "maskq": maskq, "maskk": maskk, "rcount": rcount, "lamsel": lamsel}


def lay_out(i):
    def tiles(w):
        k, n = w.shape
        return np.ascontiguousarray(w.reshape(k // P, P, n // P, P).transpose(2, 1, 0, 3)).reshape(n // P, P, k)

    def vec(v):
        return np.ascontiguousarray(v.reshape(-1, P).T)

    def featT(a):
        return np.ascontiguousarray(a.T.reshape(-1, P, a.shape[0]).transpose(1, 0, 2))

    f = {k: np.asarray(v) for k, v in i.items()}
    w_in = f["w_in_att"][0]
    c0 = 3 * HEADS * P
    q_w, k_w, v_w = w_in[:, 0:1024], w_in[:, 1024:2048], w_in[:, 2048:c0]
    cq_w, ckv_w, kpe_w = w_in[:, c0:c0 + LORA], w_in[:, c0 + LORA:c0 + 2 * LORA], w_in[:, c0 + 2 * LORA:c0 + 2 * LORA + DQK]
    gate_w = w_in[:, c0 + 2 * LORA + DQK:]
    ada = np.concatenate([f["w_ada"][0], f["w_ada"][1]], axis=1)
    pin = f["w_in_pool"][0].reshape(D, 2, KT, P).transpose(0, 2, 1, 3).reshape(D, 4096)
    c = np.concatenate([f["c_prompt"], f["c_sample"]], axis=0)
    heads_first = lambda w: np.ascontiguousarray(w.reshape(LT, P, HEADS, P).transpose(2, 1, 0, 3)).reshape(HEADS, P, LORA)
    out = {
        "xT": featT(np.concatenate([f["x_prompt"][0], f["x_sample"][0]], axis=0)),
        "cT": np.ascontiguousarray(c.T.reshape(KT, P, 2).transpose(1, 0, 2)),
        "cB": c.reshape(1, 2 * D),
        "w_ada_pe": np.ascontiguousarray(ada[:, :ADA_PE * P].reshape(4, 4, P, CHUNKS, 512).transpose(3, 0, 2, 1, 4))
                    .reshape(ADA_PE, P, D),
        "w_ada_dve": np.ascontiguousarray(ada[:, ADA_PE * P:].T).reshape(ADA_T - ADA_PE, P, D),
        "bada": vec(f["b_ada"].reshape(-1)),
        "gnorm": np.ascontiguousarray(f["g_norm"].reshape(2, KT, P).transpose(2, 0, 1)),
        "w_kpe": tiles(np.concatenate([kpe_w, kpe_w], axis=1))[0],
        "w_z": tiles(np.concatenate([cq_w, ckv_w, q_w, k_w, v_w], axis=1)),
        "w_gate": tiles(gate_w), "w_out": tiles(f["w_out_att"][0]), "w_pin": tiles(pin),
        "w_grp": np.ascontiguousarray(f["w_grp_pool"][0].reshape(4, 4, P, LORA).transpose(0, 2, 1, 3)).reshape(4, P, D),
        "w_pout": tiles(f["w_out_pool"][0]),
        "lamv": np.concatenate([f[k][0] for k in ("lam_q1", "lam_k1", "lam_q2", "lam_k2")]).reshape(1, 4 * DQK),
        "gsub": vec(f["g_subln"][0]), "gqa": vec(f["g_qa"][0]), "gkva": vec(f["g_kva"][0]),
        "w_uq": heads_first(f["w_uq"][0]),
        "w_uqr": np.ascontiguousarray(f["w_uqr"][0].reshape(LT, P, 4, P).transpose(2, 1, 0, 3)).reshape(4, P, LORA),
        "w_ukT": np.ascontiguousarray(f["w_uk"][0].transpose(1, 2, 0)),
        "w_uv": heads_first(f["w_uv"][0]),
        "scale_pool": vec(f["scale_pool"][0]), "gfin": vec(f["g_final"]),
        "kc": np.ascontiguousarray(f["cache_diff_k"][0, 0].transpose(1, 2, 0)),
        "vc": f["cache_diff_v"][0, 0].reshape(PAST, HEADS * P),
        "ckvT": np.ascontiguousarray(f["cache_mla_ckv"][0, 0].T), "ckv": f["cache_mla_ckv"][0, 0],
        "kpeT": np.ascontiguousarray(f["cache_mla_kpe"][0, 0].T),
        "poolT": featT(f["state_pool"][0, 0]),
    }
    out.update(tables())
    return out


_ARGS = ("xT cT cB w_ada_pe w_ada_dve bada gnorm w_kpe w_z w_gate w_out w_pin w_grp w_pout lamv gsub gqa gkva w_uq w_uqr "
         "w_ukT w_uv scale_pool gfin kc vc ckvT ckv kpeT poolT cosT sinT swap ident maskq maskk rcount lamsel").split()
_OUTS = (("y", (KT, P, R)), ("z", (ZT, P, R)), ("ckv_new", (LT, P, R)), ("kpe_new", (DQK, R)), ("pool_new", (P, KT, 2, PAD)))


def kernel(**inputs):
    import concourse.bacc as _bacc
    from concourse.bass_utils import run_bass_kernel_spmd as _run

    nc = _bacc.Bacc("TRN2", target_bir_lowering=False, num_devices=1)
    arrays, args = {}, []
    laid = lay_out(inputs)
    for name in _ARGS:
        a = np.ascontiguousarray(laid[name])
        arrays[f"in_{name}"] = a
        args.append(nc.dram_tensor(f"in_{name}", a.shape, mybir.dt.from_np(a.dtype), kind="ExternalInput").ap())
    for name, shape in _OUTS:
        args.append(nc.dram_tensor(f"out_{name}", shape, F32, kind="ExternalOutput").ap())
    program(nc, *args)
    res = _run(nc, [arrays], core_ids=[0]).results[0]
    yT = res["out_y"].reshape(D, R).T
    z = res["out_z"].reshape(ZT * P, R).T
    ck = res["out_ckv_new"].reshape(LORA, R).T
    kp = res["out_kpe_new"].T
    pool = res["out_pool_new"].transpose(2, 3, 1, 0).reshape(2, PAD, D)
    ka, va = z[:, ZK * P:ZV * P], z[:, ZV * P:ZT * P]
    C = np.ascontiguousarray
    group = lambda r0, r1, n: (C(ka[r0:r1]).reshape(1, 1, n, HEADS, P), C(va[r0:r1]).reshape(1, 1, n, HEADS, P),
                               C(ck[r0:r1]).reshape(1, 1, n, LORA), C(kp[r0:r1]).reshape(1, 1, n, DQK))
    return (C(yT[0:NP]).reshape(1, NP, D), C(yT[NP:R]).reshape(1, NS, D),
            *group(0, NP, NP), C(pool[0]).reshape(1, 1, PAD, D),
            *group(NP, R, NS), C(pool[1]).reshape(1, 1, PAD, D))
```

```python
from contextlib import ExitStack
import math

import numpy as np

import concourse.bass as bass
from concourse import mybir

F32 = mybir.dt.float32
F32R = mybir.dt.float32r
ALU = mybir.AluOpType
ACT = mybir.ActivationFunctionType
AX = mybir.AxisListType

P = 128
D = 2048
KT = D // P
NP, NS = 512, 32
R = NP + NS
HALF = R // 2
PAST = 512
HEADS = 8
QT = NP // P
KTS = PAST // P + 1
SKEYS = PAST + NS
LORA = 512
LT = LORA // P
ZT = 32
ZQ, ZK, ZV = 8, 16, 24
GT = 16
ADA_PE = 20
ADA_P0 = 12
ADA_P1 = 48
ADA_T = 96
DQK = 64
LAM_INIT = 0.8 - 0.6 * math.exp(-0.3 * 0)
EPS, SUB_EPS = 1e-6, 1e-5
DIFF_SCALE = DQK ** -0.5
MLA_SCALE = (128 + 64) ** -0.5
MASKED = -float(2 ** 100)
WIN = (2, 4, 8, 16)
PAD = 15

G_KPE = ADA_PE
G_Z = G_KPE + 1
G_GATE = G_Z + ZT
G_OUT = G_GATE + GT
G_PIN = G_OUT + KT
G_GRP = G_PIN + 2 * KT
G_POUT = G_GRP + 4
G_END = G_POUT + KT
CHUNKS = ADA_PE // 4


def turn_of(g):
    return g // 2 - (G_KPE // 2 - 1)


class Tally:

    def __init__(self, sem):
        self.sem, self.base, self.k, self.t, self.per = sem, 0, 0, None, 0

    def loop(self, t, per):
        self.base, self.k, self.t, self.per = self.base + self.k, 0, t, per

    def end(self, count):
        assert self.k == self.per, (self.k, self.per)
        self.base, self.k, self.t, self.per = self.base + self.per * count, 0, None, 0

    def inc(self, ins):
        ins.then_inc(self.sem, 1)
        self.k += 1
        return self.base + self.k + (self.per * self.t if self.t is not None else 0)


def program(nc, xT, cT, cB, w_ada_pe, w_ada_dve, bada, gnorm, w_kpe, w_z, w_gate, w_out, w_pin, w_grp, w_pout,
            lamv, gsub, gqa, gkva, w_uq, w_uqr, w_ukT, w_uv, w_uk, w_uv2, scale_pool, gfin,
            kc, vc, ckvT, ckv, kpeT, poolT, cosT, sinT, swap, ident, maskq, maskk, rcount, lamsel, selc, selr,
            y_out, z_out, ckv_out, kpe_out, pool_out):
    g_scr = nc.dram_tensor("gate_scratch", (GT, P, R), F32, kind="Internal").ap()
    d_scr = nc.dram_tensor("pool_d_scratch", (KT, P, R), F32, kind="Internal").ap()
    pg_scr = nc.dram_tensor("pool_gate_scratch", (KT, P, R), F32, kind="Internal").ap()

    keep = ExitStack()
    with keep:
        def sb(name, shape, dt=F32, scope=keep):
            return scope.enter_context(nc.sbuf_tensor(name, shape, dt))

        def sem(name):
            return keep.enter_context(nc.semaphore(name))

        h_hi = sb("h_hi", [P, KT, R], F32R)
        h_lo = sb("h_lo", [P, KT, R], F32R)
        w_raw = sb("w_raw", [P, 2, D])
        kpe = sb("kpe", [P, R])
        rstd = sb("rstd", [P, R])
        ssq = sb("ssq", [P, R])
        cos_t = sb("cos_t", [P, R])
        sin_t = sb("sin_t", [P, R])
        swap_t = sb("swap_t", [P, P])
        id_t = sb("id_t", [P, P])
        ones = sb("ones", [P, P])
        maskq_f = sb("maskq_f", [1, P])
        maskk_f = sb("maskk_f", [1, DQK])
        maskq_t = sb("maskq_t", [1, P], mybir.dt.bfloat16)
        maskk_t = sb("maskk_t", [1, DQK], mybir.dt.bfloat16)
        sel_col = sb("sel_col", [P, HEADS, HEADS])
        mod = sb("mod", [P, 2, ADA_T])
        bada_t = sb("bada_t", [P, ADA_T])
        gnorm_t = sb("gnorm_t", [P, 2, KT])
        aff = sb("aff", [P, 2, KT])
        cond_t = sb("cond_t", [P, KT, 2])
        vecs = sb("vecs", [P, 3, KT])
        pool_last = sb("pool_last", [P, KT, 2, PAD])
        pool_pre = sb("pool_pre", [P, KT, PAD])
        ada_acc = sb("ada_acc", [P, 2])
        act_tmp = sb("act_tmp", [P, 2])
        rcount_t = sb("rcount_t", [P, 4, 16])
        lam_in = sb("lam_in", [P, 4, DQK])
        lam_w = sb("lam_w", [P, 8])
        lamsel_t = sb("lamsel_t", [P, 2])
        PS = keep.enter_context(nc.psum_tensor("banks", [P, 8, 512], F32))

        scale_v, gfin_v = vecs[:, 0, :], vecs[:, 1, :]
        gsub_v, gqa_v, gkva_v = vecs[:, 2, 0:1], vecs[:, 2, 1:5], vecs[:, 2, 5:9]
        neg_lam, coef = lam_w[:, 6:7], lam_w[:, 7:8]
        rows = lambda ap: ap.rearrange("p (a r) -> p a r", a=2)
        acc = [PS[:, 2 * s:2 * s + 2, 0:HALF] for s in range(2)]
        ada_junk = PS[:, 4:8, :].rearrange("p a b -> p (a b)")

        stream = ExitStack()
        x = sb("x", [P, KT, R], scope=stream)
        w_hi = sb("w_hi", [P, 2, D], F32R, stream)
        w_lo = sb("w_lo", [P, 2, D], F32R, stream)
        stage = sb("stage", [P, 2, R], scope=stream)
        ada_stack = ExitStack()
        w_adr = sb("w_adr", [P, 2, D], scope=ada_stack)
        cond_b = sb("cond_b", [P, 2, D], scope=ada_stack)
        ada_stack.close()
        pin_stack = ExitStack()
        u_ext = sb("u_ext", [P, PAD + NP + PAD + NS], scope=pin_stack)
        w2 = sb("w2", [P, PAD + NP + PAD + NS], scope=pin_stack)
        w4 = sb("w4", [P, PAD + NP + PAD + NS], scope=pin_stack)
        d_st = sb("d_st", [P, R], scope=pin_stack)
        fix = sb("fix", [P, 16], scope=pin_stack)
        pin_stack.close()
        grp_stack = ExitStack()
        d_raw = sb("d_raw", [P, 4, R], scope=grp_stack)
        d_hi = sb("d_hi", [P, 4, R], F32R, grp_stack)
        d_lo = sb("d_lo", [P, 4, R], F32R, grp_stack)
        pg = sb("pg", [P, 4, R], scope=grp_stack)
        grp_stack.close()
        stream.close()

        mla = ExitStack()
        ckT = sb("ckT", [P, LT, R], scope=mla)
        ckR = sb("ckR", [P, QT + 1, LORA], scope=mla)
        kpc = sb("kpc", [P, PAST], scope=mla)
        qls = sb("qls", [P, LT, HEADS, NS], scope=mla)
        qps = sb("qps", [P, HEADS, NS], scope=mla)
        ml_loop = ExitStack()
        cq = sb("cq", [P, LT, R], scope=ml_loop)
        wq = sb("wq", [P, 2, LT, P], scope=ml_loop)
        wk = sb("wk", [P, 2, LT, P], scope=ml_loop)
        wkT = sb("wkT", [P, 2, LORA], scope=ml_loop)
        wr = sb("wr", [P, LT, P], scope=ml_loop)
        wv = sb("wv", [P, LT, 2 * P], scope=ml_loop)
        qn = sb("qn", [P, 2, R], scope=ml_loop)
        qpr = sb("qpr", [P, R], scope=ml_loop)
        qpe = sb("qpe", [P, R], scope=ml_loop)
        qsin = sb("qsin", [P, R], scope=ml_loop)
        kn = sb("kn", [P, 2, NP], scope=ml_loop)
        vb = sb("vb", [P, QT, 2 * P], scope=ml_loop)
        px = sb("px", [P, 3, NP], scope=ml_loop)
        over = ExitStack()
        lat_sq = sb("lat_sq", [P, 2, LT, R], scope=over)
        over.close()
        pt = sb("pt", [P, 2, QT, NP], scope=ml_loop)
        fo = sb("fo", [P, NP], scope=ml_loop)
        sg = sb("sg", [P, 2, R], scope=ml_loop)
        st = sb("st", [P, 4, 8], scope=ml_loop)
        ml_loop.close()
        ml_samp = ExitStack()
        ccT = sb("ccT", [P, LT, PAST], scope=ml_samp)
        ccR = sb("ccR", [P, LT, LORA], scope=ml_samp)
        wva = sb("wva", [P, LT, HEADS * P], scope=ml_samp)
        pxs = sb("pxs", [P, 2, SKEYS], scope=ml_samp)
        pts = sb("pts", [P, 2, KTS, P], scope=ml_samp)
        ols = sb("ols", [P, LT, HEADS, NS], scope=ml_samp)
        sgs = sb("sgs", [P, HEADS, NS], scope=ml_samp)
        ofs = sb("ofs", [P, HEADS, NS], scope=ml_samp)
        sts = sb("sts", [P, 2, 4], scope=ml_samp)
        ml_samp.close()
        mla.close()

        dif = ExitStack()
        od = sb("od", [P, HEADS, R], scope=dif)
        sgd = sb("sgd", [P, HEADS, R], scope=dif)
        qd = sb("qd", [P, 2, R], scope=dif)
        kd = sb("kd", [P, 2, R], scope=dif)
        vd = sb("vd", [P, 2, R], scope=dif)
        kcs = sb("kcs", [P, 2, PAST], scope=dif)
        vcs = sb("vcs", [P, 2, QT, P], scope=dif)
        vr = sb("vr", [P, 2, KTS, P], scope=dif)
        pxd = sb("pxd", [P, 3, 2, NP], scope=dif)
        ptd = sb("ptd", [P, 2, QT, NP], scope=dif)
        pxds = sb("pxds", [P, SKEYS], scope=dif)
        ptds = sb("ptds", [P, KTS, 2, NS], scope=dif)
        ptd1 = sb("ptd1", [P, KTS, 2, NS], scope=dif)
        std = sb("std", [P, 9, 8], scope=dif)
        sqd = sb("sqd", [P, 2, R], scope=dif)
        rs8 = sb("rs8", [HEADS, R], scope=dif)
        sel_row = sb("sel_row", [HEADS, HEADS, P], scope=dif)
        dif.close()

        consts_in = sem("consts_in"); x_in = sem("x_in"); cond_in = sem("cond_in"); condb_in = sem("condb_in")
        raw_in = [sem(f"raw_in{s}") for s in range(2)]
        adr_in = [sem(f"adr_in{s}") for s in range(2)]
        cond_ready = sem("cond_ready"); condb_ready = sem("condb_ready")
        adr_used = sem("adr_used")
        split_ready = sem("split_ready")
        mm_done = sem("mm_done")
        acc_free = [sem(f"acc_free{s}") for s in range(2)]
        sq_ready = sem("sq_ready"); sq_added = sem("sq_added"); ssq_zero = sem("ssq_zero"); var_eps = sem("var_eps")
        var_ready = sem("var_ready"); std_ready = sem("std_ready"); rstd_ready = sem("rstd_ready")
        xn_ready = sem("xn_ready"); hf_ready = sem("hf_ready"); h_ready = sem("h_ready")
        dve_step = sem("dve_step"); act_step = sem("act_step"); ada_row = sem("ada_row"); ada_turned = sem("ada_turned"); x_normed = sem("x_normed"); ones_ready = sem("ones_ready")
        staged = sem("staged"); stored = [sem(f"stored{s}") for s in range(2)]
        kpe_ready = sem("kpe_ready"); lam_ready = sem("lam_ready"); lam_exp = sem("lam_exp"); lam_sum = sem("lam_sum")
        out_done = sem("out_done")
        dv, ac = Tally(dve_step), Tally(act_step)
        mq_in = sem("mq_in"); mq_sq = sem("mq_sq"); mq_sum = sem("mq_sum"); mq_var = sem("mq_var")
        mq_std = sem("mq_std"); mq_norm = sem("mq_norm"); mq_tr = sem("mq_tr"); mq_ev = sem("mq_ev")
        kp_swap = sem("kp_swap"); kp_done = sem("kp_done"); latent_out = sem("latent_out")
        ml_w_in = sem("ml_w_in"); ml_v_in = sem("ml_v_in"); ml_item = sem("ml_item"); ml_ev_d = sem("ml_ev_d"); ml_ev_a = sem("ml_ev_a")
        ml_swap = sem("ml_swap"); ml_qpe = sem("ml_qpe"); ml_score = sem("ml_score"); ml_max = sem("ml_max")
        ml_exp = sem("ml_exp"); ml_norm = sem("ml_norm"); ml_tr = sem("ml_tr"); ml_ptev = sem("ml_ptev")
        ml_pv = sem("ml_pv"); masks_ready = sem("masks_ready"); ml_fin = sem("ml_fin"); qps_zero = sem("qps_zero")
        ms_in = sem("ms_in"); ms_score = sem("ms_score"); ms_max = sem("ms_max"); ms_exp = sem("ms_exp")
        ms_norm = sem("ms_norm"); ms_tr = sem("ms_tr"); ms_ptev = sem("ms_ptev"); ms_pv = sem("ms_pv")
        ms_olev = sem("ms_olev"); ms_ob = sem("ms_ob"); ms_fin = sem("ms_fin")
        df_a_in = sem("df_a_in"); df_v_in = sem("df_v_in"); df_g_in = sem("df_g_in"); df_vt = sem("df_vt")
        df_vrev = sem("df_vrev"); df_score = sem("df_score"); df_max = sem("df_max"); df_exp = sem("df_exp")
        df_norm = sem("df_norm"); df_tr = sem("df_tr"); df_ptev = sem("df_ptev"); df_pv = sem("df_pv")
        df_od = sem("df_od"); df_vd_in = sem("df_vd_in"); df_sq = sem("df_sq"); df_ssq = sem("df_ssq"); df_var = sem("df_var")
        df_std = sem("df_std"); df_rs = sem("df_rs"); df_wide = sem("df_wide"); df_tmp = sem("df_tmp"); df_fin = sem("df_fin"); lam_scaled = sem("lam_scaled")
        dfs_score = sem("dfs_score"); dfs_max = sem("dfs_max"); dfs_exp = sem("dfs_exp")
        dfs_norm = sem("dfs_norm"); dfs_tr = sem("dfs_tr"); dfs_ptev = sem("dfs_ptev"); dfs_pv = sem("dfs_pv")
        gy_ready = sem("gy_ready"); x_new = sem("x_new"); u_ready = sem("u_ready"); u_used = sem("u_used")
        pg_ready = sem("pg_ready"); d_ready = sem("d_ready"); pre_in = sem("pre_in"); d_stored = sem("d_stored")
        pg_stored = sem("pg_stored"); grp_in = [sem("grp_in0"), sem("grp_in1")]; grp_mm = sem("grp_mm")
        grp_y = sem("grp_y"); d_split = sem("d_split"); y_ready = sem("y_ready"); y_fin = sem("y_fin"); pool_pre_in = sem("pool_pre_in"); pad_zero = sem("pad_zero"); pad_free = sem("pad_free"); qps_free = sem("qps_free")
        y_stored = [sem(f"y_stored{s}") for s in range(2)]

        def vchain(dve, ins):
            dve.wait_ge(dve_step, dv.inc(ins))

        def achain(act, ins):
            act.wait_ge(act_step, ac.inc(ins))

        def pairs(ap):
            return ap.rearrange("(t s) p n -> s t p n", s=2)

        def tile_of(pair, s, t):
            return pair[s, bass.ds(t, 1)].rearrange("t p n -> p (t n)")

        def at(ap, k):
            return ap[:, bass.ds(k, 1), :].rearrange("p k r -> p (k r)")

        wz2, wg2, wo2, wp2, wy2 = (pairs(a) for a in (w_z, w_gate, w_out, w_pin, w_pout))
        wd2, z2, g2 = pairs(w_ada_dve), pairs(z_out), pairs(g_scr)
        CONSTS = 16 * 18
        block = keep.enter_context(nc.Block())

        @block.sync
        def _(sp):
            sp.dma_start(cond_t[:], cT).then_inc(cond_in, 16)

            def load_w(src, slot, ready=None):
                if ready is not None:
                    sp.wait_ge(split_ready, ready)
                sp.dma_start(w_raw[:, slot], src).then_inc(raw_in[slot], 16)

            def load_ada(pair_slot, src, used=None):
                if used is not None:
                    sp.wait_ge(adr_used, used)
                sp.dma_start(w_adr[:, pair_slot], src).then_inc(adr_in[pair_slot], 16)

            sp.dma_start(cond_b[:], cB.to_broadcast((P, 2 * D)).rearrange("p (a d) -> p a d", a=2)).then_inc(condb_in, 16)
            for s in range(2):
                load_w(w_ada_pe[s], s)
                load_ada(s, w_ada_dve[s])
            for g in range(2, ADA_PE):
                sp.wait_ge(mm_done, g - 1)
                load_w(w_ada_pe[g], g % 2)
                if g == 3:
                    sp.dma_start(x[:], xT).then_inc(x_in, 16)
                if 3 <= g < ADA_P0 + 1:
                    load_ada((g - 1) % 2, w_ada_dve[g - 1], g - 2)
            sp.wait_ge(mm_done, G_KPE - 1)
            load_w(w_kpe, G_KPE % 2)
            for a in range(ADA_P0, ADA_P0 + 2):
                load_ada(a % 2, w_ada_dve[a], a - 1)
            sp.wait_ge(mm_done, G_KPE)
            with sp.Fori(0, ZT // 2) as t:
                for s in range(2):
                    load_w(tile_of(wz2, s, t), (G_Z + s) % 2, 2 * t + G_Z - G_KPE + s)
            with sp.Fori(0, GT // 2) as t:
                for s in range(2):
                    load_w(tile_of(wg2, s, t), (G_GATE + s) % 2, 2 * t + G_GATE - G_KPE + s)
            for s in range(2):
                load_w(w_out[s], (G_OUT + s) % 2, G_OUT - G_KPE + s)

            sp.wait_ge(mm_done, G_OUT)
            sp.wait_ge(adr_used, ADA_P0 + ADA_P1)
            for s in range(2):
                sp.wait_ge(stored[s], 16 * (ZT + GT) // 2)
            sp.dma_start(cq[:], z_out[0:LT].rearrange("t p r -> p t r")).then_inc(mq_in, 16)
            sp.dma_start(ckT[:], z_out[LT:2 * LT].rearrange("t p r -> p t r")).then_inc(mq_in, 16)
            for e in range(2):
                sp.dma_start(kpc[64 * e:64 * e + 64, :], kpeT).then_inc(mq_in, 16)

            uq2, uk2, ukT2 = (a.rearrange("(t s) p n -> s t p n", s=2) for a in (w_uq, w_uk, w_ukT))

            def load_mla_w(t):
                for s in range(2):
                    sp.dma_start(wq[:, s].rearrange("p c d -> p (c d)"), tile_of(uq2, s, t)).then_inc(ml_w_in, 16)
                    sp.dma_start(wk[:, s].rearrange("p c d -> p (c d)"), tile_of(uk2, s, t)).then_inc(ml_w_in, 16)
                    sp.dma_start(wkT[:, s], tile_of(ukT2, s, t)).then_inc(ml_w_in, 16)
                sp.dma_start(wr[:].rearrange("p c d -> p (c d)"),
                             w_uqr[bass.ds(t, 1)].rearrange("t p n -> p (t n)")).then_inc(ml_w_in, 16)
                sp.dma_start(wv[:].rearrange("p c d -> p (c d)"),
                             w_uv2[bass.ds(t, 1)].rearrange("t p n -> p (t n)")).then_inc(ml_w_in, 16)

            def load_mla_g(t):
                for s in range(2):
                    sp.dma_start(sg[:, s], tile_of(g2, s, t + HEADS // 2)).then_inc(ml_v_in, 16)

            load_mla_w(0)
            load_mla_g(0)
            with sp.Fori(0, HEADS // 2 - 1) as t:
                sp.wait_ge(ml_item, 6 * t + 6)
                load_mla_w(t + 1)
                sp.wait_ge(ml_fin, 2 * t + 3)
                load_mla_g(t + 1)
            sp.wait_ge(ml_fin, HEADS + 1)
            sp.wait_ge(ml_item, 6 * (HEADS // 2))
            sp.dma_start(ccT[:], ckvT.rearrange("(c p) k -> p c k", p=P)).then_inc(ms_in, 16)
            sp.dma_start(ccR[:], ckv.rearrange("(k p) c -> p k c", p=P)).then_inc(ms_in, 16)
            for h in range(HEADS):
                sp.dma_start(wva[:, :, h * P:(h + 1) * P],
                             w_uv[h].rearrange("p (c v) -> p c v", c=LT)).then_inc(ms_in, 16)
            sp.dma_start(sgs[:], g_scr[HEADS:2 * HEADS, :, NP:R].rearrange("h p r -> p h r")).then_inc(ms_in, 16)

            sp.wait_ge(ms_fin, 1)
            sp.wait_ge(latent_out, 32)
            kc2 = kc.rearrange("(t s) p k -> s t p k", s=2)
            vc2 = vc.rearrange("(j p) (t s e) -> s t p j e", p=P, s=2, e=P)

            def load_qk(t):
                for s in range(2):
                    sp.dma_start(qd[:, s], tile_of(z2, s, t + ZQ // 2)).then_inc(df_a_in, 16)
                    sp.dma_start(kd[:, s], tile_of(z2, s, t + ZK // 2)).then_inc(df_a_in, 16)
                    sp.dma_start(kcs[:, s], tile_of(kc2, s, t)).then_inc(df_a_in, 16)

            def load_v(t):
                for s in range(2):
                    sp.dma_start(vd[:, s], tile_of(z2, s, t + ZV // 2)).then_inc(df_vd_in, 16)

            def load_vc(t):
                for s in range(2):
                    sp.dma_start(vcs[:, s], vc2[s, bass.ds(t, 1)].rearrange("t p j e -> p (t j) e")).then_inc(df_v_in, 16)

            load_v(0)
            load_qk(0)
            load_vc(0)
            sp.dma_start(sgd[:], g_scr[0:HEADS].rearrange("h p r -> p h r")).then_inc(df_g_in, 16)
            sp.dma_start(sel_row[:], selr).then_inc(df_g_in, 16)
            with sp.Fori(0, HEADS // 2 - 1) as t:
                sp.wait_ge(df_vt, 2 * t + 2)
                load_v(t + 1)
                sp.wait_ge(dfs_score, t + 1)
                load_qk(t + 1)
                sp.wait_ge(dfs_pv, t + 1)
                load_vc(t + 1)

            sp.wait_ge(df_fin, HEADS)
            sp.dma_start(cond_b[:], cB.to_broadcast((P, 2 * D)).rearrange("p (a d) -> p a d", a=2)).then_inc(condb_in, 16)
            sp.dma_start(x[:], xT).then_inc(x_in, 16)
            for s in range(2):
                load_ada(s, w_ada_dve[ADA_P0 + ADA_P1 + s])
            with sp.Fori(0, KT // 2 - 1) as t:
                for s in range(2):
                    load_w(tile_of(wo2, s, t + 1), (G_OUT + s) % 2, 2 * t + 2 + G_OUT - G_KPE + s)
            with sp.Fori(0, KT) as t:
                for s in range(2):
                    load_w(tile_of(wp2, s, t), (G_PIN + s) % 2, 2 * t + G_PIN - G_KPE + s)
            for g in range(4):
                load_w(w_grp[g], (G_GRP + g) % 2, G_GRP - G_KPE + g)
                if g == 0:
                    sp.wait_ge(d_stored, 16 * KT)
                    sp.wait_ge(pg_stored, 16 * KT)
                else:
                    sp.wait_ge(d_split, g)
                sp.dma_start(d_raw[:], d_scr[4 * g:4 * g + 4].rearrange("t p r -> p t r")).then_inc(grp_in[0], 16)
                if g:
                    sp.wait_ge(grp_y, 4 * g)
                sp.dma_start(pg[:], pg_scr[4 * g:4 * g + 4].rearrange("t p r -> p t r")).then_inc(grp_in[1], 16)
            with sp.Fori(0, KT // 2) as t:
                for s in range(2):
                    load_w(tile_of(wy2, s, t), (G_POUT + s) % 2, 2 * t + G_POUT - G_KPE + s)
            for k in range(KT):
                sp.wait_ge(y_fin, k + 1)
                sp.dma_start(y_out[k], x[:, k]).then_inc(y_stored[k % 2], 16)
            sp.wait_ge(out_done, 16)
            for s in range(2):
                sp.wait_ge(y_stored[s], 16 * KT // 2)

        @block.gpsimd
        def _(pool):
            pool.memset(ones[:], 1.0).then_inc(ones_ready, 1)
            for dst, src in ((cos_t, cosT), (sin_t, sinT), (swap_t, swap), (id_t, ident), (maskq_f, maskq), (maskk_f, maskk), (sel_col, selc),
                             (bada_t, bada), (gnorm_t, gnorm), (rcount_t, rcount), (lamsel_t, lamsel), (pool_pre, poolT)):
                pool.dma_start(dst[:], src).then_inc(consts_in, 16)
            for dst, src in ((scale_v, scale_pool), (gfin_v, gfin), (gsub_v, gsub), (gqa_v, gqa), (gkva_v, gkva)):
                pool.dma_start(dst, src).then_inc(consts_in, 16)
            pool.dma_start(lam_in[:], lamv.to_broadcast((P, 4 * DQK)).rearrange("p (a d) -> p a d", a=4)).then_inc(consts_in, 16)

            pool.wait_ge(split_ready, 1)
            for k in range(KT):
                pool.wait_ge(sq_ready, k + 1)
                pool.tensor_tensor(ssq[:], ssq[:], (stage[:, 0], rstd[:])[k % 2], ALU.add).then_inc(sq_added, 1)
                pool.wait_ge(sq_added, k + 1)
            pool.wait_ge(qps_free, 1)
            pool.memset(qps[:], 0.0).then_inc(qps_zero, 1)

            def add_squares(n):
                pool.wait_ge(ssq_zero, n)
                with pool.Fori(0, KT // 2) as t:
                    for s in range(2):
                        pool.wait_ge(sq_ready, 2 * t + (KT * n + s + 1))
                        pool.tensor_tensor(ssq[:], ssq[:], stage[:, s], ALU.add).then_inc(sq_added, 1)
                        pool.wait_ge(sq_added, 2 * t + (KT * n + s + 1))

            add_squares(1)
            pool.wait_ge(pad_free, 1)
            pool.memset(u_ext[:, 0:PAD], 0.0).then_inc(pad_zero, 1)
            add_squares(2)

        @block.tensor
        def _(pe):
            def small(out, lhsT, rhs, start, stop):
                return pe.matmul(out, lhsT, rhs, start=start, stop=stop)

            def row_sums(n):
                if n == 0:
                    pe.wait_ge(ones_ready, 1)
                pe.wait_ge(sq_added, KT * (n + 1))
                for a in range(2):
                    m = small(PS[:, (6 if n else 2) + a, 0:HALF], ones[:], ssq[:, a * HALF:(a + 1) * HALF], True, True)
                m.then_inc(var_ready, 1)

            pe.wait_ge(cond_ready, 1)

            def ada_turn(c):
                if c == 0:
                    pe.wait_ge(consts_in, CONSTS)
                pe.wait_ge(ada_row, c + 1)
                for q in range(4):
                    f = 2 * (4 * c + q)
                    m = pe.transpose(PS[:, 1, f:f + 2], stage[0:2, 1, q * P:(q + 1) * P], id_t[0:2, 0:2])
                m.then_inc(ada_turned, 1)

            for g in range(ADA_PE):
                c = g // 4
                pe.wait_ge(raw_in[g % 2], 16 * (g // 2 + 1))
                if g % 4 == 0 and c:
                    pe.wait_ge(ada_row, c)
                for k in range(4):
                    m = small(PS[0:2, 0, :], cond_t[:, 4 * (g % 4) + k, :], w_raw[:, g % 2, k * 512:(k + 1) * 512],
                              g % 4 == 0 and k == 0, g % 4 == 3 and k == 3)
                m.then_inc(mm_done, 1)
                if g % 4 == 1 and c:
                    ada_turn(c - 1)
                if g == ADA_PE - 3:
                    row_sums(0)

            def big_tile(slot, h_wait=None, order=None):
                for n, (k, heads) in enumerate(order or [(k, 0) for k in range(KT)]):
                    if h_wait is not None:
                        pe.wait_ge(h_ready, h_wait + k + 3)
                    if heads:
                        pe.wait_ge(df_fin, heads)
                    ks = slice(k * P, (k + 1) * P)
                    for i, (w, h) in enumerate(((w_hi, h_hi), (w_hi, h_lo), (w_lo, h_hi))):
                        for a in range(2):
                            m = small(PS[:, 2 * slot + a, 0:HALF], w[:, slot, ks], h[:, k, a * HALF:(a + 1) * HALF],
                                      n == 0 and i == 0, n == KT - 1 and i == 2)
                m.then_inc(mm_done, 1)

            def big_wait(g, twice_t=0, t=0):
                pe.wait_ge(split_ready, twice_t + (g - G_KPE + 2))
                pe.wait_ge(acc_free[g % 2], t + turn_of(g))

            def big_loop(g0, first, end):
                with pe.Fori(first, end) as t:
                    for s in range(2):
                        big_wait(g0 + s, 2 * t, t)
                        big_tile((g0 + s) % 2)

            ada_turn(CHUNKS - 1)
            big_wait(G_KPE)
            big_tile(G_KPE % 2, 0)
            big_loop(G_Z, 0, ZT // 2)
            big_loop(G_GATE, 0, GT // 2)

            for s in range(2):
                pe.wait_ge(acc_free[s], turn_of(G_OUT + (G_OUT + s) % 2))
            for a in range(2):
                pe.wait_ge(mq_sq, a + 1)
                for hf in range(2):
                    for c in range(LT):
                        m = small(PS[:, 2 * a + hf, 0:HALF], ones[:], lat_sq[:, a, c, hf * HALF:(hf + 1) * HALF], c == 0, c == LT - 1)
                m.then_inc(mq_sum, 1)
            for a in range(2):
                m = small(PS[:, 6 + a, 0:HALF], swap_t[:], kpe[:, a * HALF:(a + 1) * HALF], True, True)
            m.then_inc(kp_swap, 1)
            pe.wait_ge(mq_norm, 2)
            for j in range(QT + 1):
                nk = P if j < QT else NS
                if j >= 2:
                    pe.wait_ge(mq_ev, j - 1)
                for c in range(LT):
                    m = pe.transpose(PS[0:nk, 4 + j % 2, c * P:(c + 1) * P], ckT[:, c, j * P:j * P + nk], id_t[:])
                m.then_inc(mq_tr, 1)
            pe.wait_ge(mq_ev, QT + 1)
            pe.wait_ge(kp_done, 1)

            pe.wait_ge(masks_ready, 2)
            with pe.Fori(0, HEADS // 2) as t:
                halves = [slice(0, HALF), slice(HALF, R)]
                pe.wait_ge(ml_w_in, 128 * t + 128)
                for k in range(3):
                    for hf in range(2):
                        for c in range(LT):
                            w = wq[:, k, c, :] if k < 2 else wr[:, c, :]
                            m = small(PS[:, 2 * k + hf, 0:HALF], w, cq[:, c, halves[hf]], c == 0, c == LT - 1)
                    m.then_inc(ml_item, 1)
                pe.wait_ge(ml_ev_d, 3 * t + 1)
                for s in range(2):
                    for c in range(LT):
                        m = small(PS[:, s, :], wk[:, s, c, :], ckT[:, c, 0:NP], c == 0, c == LT - 1)
                m.then_inc(ml_item, 1)
                pe.wait_ge(ml_ev_d, 3 * t + 2)
                pe.wait_ge(ml_fin, 2 * t + 1)
                for hf in range(2):
                    m = small(PS[:, 6 + hf, 0:HALF], swap_t[:], qpr[:, halves[hf]], True, True)
                m.then_inc(ml_swap, 1)
                pe.wait_ge(ml_ev_a, 3 * t + 1)
                for j in range(QT):
                    for c in range(LT):
                        m = small(PS[:, 2 + j // 2, 2 * P * (j % 2):2 * P * (j % 2) + 2 * P], ckT[:, c, j * P:(j + 1) * P],
                                  wv[:, c, :], c == 0, c == LT - 1)
                m.then_inc(ml_item, 1)
                for s in range(2):
                    for c in range(LT):
                        f = NS * (LT * s + c)
                        m = small(PS[:, 4, f:f + NS], wkT[:, s, c * P:(c + 1) * P], qn[:, s, NP:R], True, True)
                m.then_inc(ml_item, 1)

                def scores(u):
                    s, i = u // QT, u % QT
                    n, b = P * (i + 1), u % 4
                    if u >= 4:
                        pe.wait_ge(ml_exp, 8 * t + u - 3)
                    qs, e = slice(P * i, P * i + P), slice(DQK * s, DQK * s + DQK)
                    small(PS[:, b, 0:n], qn[:, s, qs], kn[:, s, 0:n], True, False)
                    small(PS[:, b, n - DQK:n], maskq_t[:], maskk_t[:], False, False)
                    small(PS[:, b, 0:n], qpe[e, qs], kpe[e, 0:n], False, True).then_inc(ml_score, 1)

                def turn(u):
                    i = u % QT
                    pe.wait_ge(ml_norm, 8 * t + u + 1)
                    if u >= 2:
                        pe.wait_ge(ml_ptev, 8 * t + u - 1)
                    for j in range(i + 1):
                        m = pe.transpose(PS[:, 4 + u % 2, j * P:(j + 1) * P], px[:, u % 3, j * P:(j + 1) * P], id_t[:])
                    m.then_inc(ml_tr, 1)

                def values(s):
                    pe.wait_ge(ml_ptev, 8 * t + 4 * s + 4)
                    for j in range(QT):
                        m = small(PS[:, 6 + s, P * j:NP], vb[:, j, s * P:(s + 1) * P], pt[:, s, j, P * j:NP],
                                  j == 0, j == QT - 1)
                    m.then_inc(ml_pv, 1)

                pe.wait_ge(ml_ev_a, 3 * t + 3)
                pe.wait_ge(ml_ev_d, 3 * t + 3)
                pe.wait_ge(ml_qpe, t + 1)
                for u in range(10):
                    if u < 8:
                        scores(u)
                    if u >= 2:
                        turn(u - 2)
                    if u == 6:
                        values(0)
                values(1)

            pe.wait_ge(ml_fin, HEADS + 1)
            pe.wait_ge(ms_in, 16 * (3 + HEADS))
            SPLIT = HALF
            for g in range(2):
                heads = slice(4 * g, 4 * g + 4)
                for bank, cols, keys_c, keys_p in ((2 * g, slice(0, SPLIT), lambda c: ccT[:, c, 0:SPLIT], kpc[:, 0:SPLIT]),
                                                   (2 * g + 1, slice(0, PAST - SPLIT), lambda c: ccT[:, c, SPLIT:PAST], kpc[:, SPLIT:PAST]),
                                                   (2 * g + 1, slice(PAST - SPLIT, SPLIT), lambda c: ckT[:, c, NP:R], kpe[:, NP:R])):
                    for c in range(LT):
                        small(PS[:, bank, cols], qls[:, c, heads, :].rearrange("p h r -> p (h r)"), keys_c(c), c == 0, False)
                    m = small(PS[:, bank, cols], qps[:, heads, :].rearrange("p h r -> p (h r)"), keys_p, False, True)
                m.then_inc(ms_score, 1)
            for g in range(2):
                pe.wait_ge(ms_norm, g + 1)
                for j in range(KTS):
                    nk = P if j < KTS - 1 else NS
                    dst = PS[0:nk, 4 + g, j * P:(j + 1) * P] if j < KTS - 1 else PS[0:nk, 6 + g, 0:P]
                    m = pe.transpose(dst, pxs[:, g, j * P:j * P + nk], id_t[:])
                m.then_inc(ms_tr, 1)
            for g in range(2):
                pe.wait_ge(ms_ptev, g + 1)
                for c in range(LT):
                    cs = slice(c * P, (c + 1) * P)
                    for j in range(KTS):
                        last = j == KTS - 1
                        m = small(PS[:, g, cs], ckR[0:NS, QT, cs] if last else ccR[:, j, cs],
                                  pts[0:NS, g, j, :] if last else pts[:, g, j, :], j == 0, last)
                m.then_inc(ms_pv, 1)
            pe.wait_ge(ms_olev, 2)
            for h in range(HEADS):
                for c in range(LT):
                    m = small(PS[:, 2, NS * h:NS * h + NS], wva[:, c, h * P:(h + 1) * P], ols[:, c, h, :], c == 0, c == LT - 1)
            m.then_inc(ms_ob, 1)
            pe.wait_ge(ms_fin, 1)

            with pe.Fori(0, HEADS // 2) as t:
                pe.wait_ge(df_vd_in, 32 * t + 32)
                pe.wait_ge(df_od, 3 * t + 1)
                for s in range(2):
                    if s:
                        pe.wait_ge(df_vrev, 2 * t + 1)
                    for j in range(KTS):
                        nk = P if j < KTS - 1 else NS
                        dst = PS[0:nk, 6, j * P:(j + 1) * P] if j < KTS - 1 else PS[0:nk, 7, 0:P]
                        m = pe.transpose(dst, vd[:, s, j * P:j * P + nk], id_t[:])
                    m.then_inc(df_vt, 1)
                pe.wait_ge(df_a_in, 96 * t + 96)

                def scores(u):
                    s, i = u // QT, u % QT
                    n = P * (i + 1)
                    if u >= 2:
                        pe.wait_ge(df_exp, 8 * t + u - 1)
                    for e in range(2):
                        b, es = 2 * (u % 2) + e, slice(DQK * e, DQK * e + DQK)
                        small(PS[:, b, 0:n], qd[es, s, P * i:P * i + P], kd[es, s, 0:n], True, False)
                        m = small(PS[:, b, n - DQK:n], maskq_t[:], maskk_t[:], False, True)
                    m.then_inc(df_score, 1)

                def turn(u):
                    i = u % QT
                    pe.wait_ge(df_norm, 8 * t + u + 1)
                    if u >= 2:
                        pe.wait_ge(df_ptev, 8 * t + u - 1)
                    for j in range(i + 1):
                        m = pe.transpose(PS[:, 4 + u % 2, j * P:(j + 1) * P], pxd[:, u % 3, 0, j * P:(j + 1) * P], id_t[:])
                    m.then_inc(df_tr, 1)

                def values(s):
                    if s == 0:
                        pe.wait_ge(df_vrev, 2 * t + 2)
                    pe.wait_ge(df_ptev, 8 * t + 4 * s + 4)
                    for j in range(QT):
                        m = small(PS[:, 6 + s, P * j:NP], vr[:, s, j, :], ptd[:, s, j, P * j:NP], j == 0, j == QT - 1)
                    m.then_inc(df_pv, 1)

                def sample_scores():
                    for s in range(2):
                        for e in range(2):
                            r, es = 32 * (2 * s + e), slice(DQK * e, DQK * e + DQK)
                            q = qd[es, s, NP:R]
                            small(PS[r:r + 32, 0, 0:HALF], q, kcs[es, s, 0:HALF], True, True)
                            small(PS[r:r + 32, 1, 0:PAST - HALF], q, kcs[es, s, HALF:PAST], True, True)
                            m = small(PS[r:r + 32, 1, PAST - HALF:HALF], q, kd[es, s, NP:R], True, True)
                    m.then_inc(dfs_score, 1)

                for u in range(10):
                    if u < 8:
                        scores(u)
                    if u >= 2:
                        turn(u - 2)
                    if u == 8:
                        sample_scores()
                    if u == 5:
                        values(0)
                values(1)
                pe.wait_ge(dfs_norm, t + 1)
                pe.wait_ge(df_ptev, 8 * t + 8)
                for j in range(KTS):
                    nk = P if j < KTS - 1 else NS
                    dst = PS[0:nk, 4, j * P:(j + 1) * P] if j < KTS - 1 else PS[0:nk, 5, 0:P]
                    m = pe.transpose(dst, pxds[:, j * P:j * P + nk], id_t[:])
                m.then_inc(dfs_tr, 1)
                pe.wait_ge(dfs_ptev, t + 1)
                pe.wait_ge(df_exp, 8 * t + 8)
                pe.wait_ge(df_v_in, 32 * t + 32)
                for s in range(2):
                    for j in range(KTS):
                        last = j == KTS - 1
                        m = small(PS[:, 2 + s, 0:NS], vr[0:NS, s, QT, :] if last else vcs[:, s, j, :],
                                  ptds[0:NS, j, s, :] if last else ptds[:, j, s, :], j == 0, last)
                m.then_inc(dfs_pv, 1)

            pe.wait_ge(df_od, 3 * (HEADS // 2) + 1)
            for h in range(HEADS):
                pe.wait_ge(df_sq, h + 1)
                for a in range(2):
                    m = small(PS[0:HEADS, 4 + a, 0:HALF], sel_col[:, h, :], sqd[:, h % 2, a * HALF:(a + 1) * HALF],
                              h == 0, h == HEADS - 1)
                m.then_inc(df_ssq, 1)
            pe.wait_ge(df_rs, 1)
            pe.wait_ge(df_g_in, 32)
            for h in range(HEADS):
                b = 4 + 2 * (h % 2)
                if h >= 2:
                    pe.wait_ge(df_fin, h - 1)
                for a in range(2):
                    m = small(PS[:, b + a, 0:HALF], sel_row[:, h, :], rs8[:, a * HALF:(a + 1) * HALF], True, True)
                m.then_inc(df_wide, 1)

            big_wait(G_OUT)
            big_tile(G_OUT % 2, None, [(k, 0) for k in range(HEADS, 2 * HEADS)] + [(k, k + 1) for k in range(HEADS)])
            big_wait(G_OUT + 1)
            big_tile((G_OUT + 1) % 2)
            big_loop(G_OUT, 1, KT // 2)
            row_sums(1)
            for s in range(2):
                big_wait(G_PIN + s)
                big_tile((G_PIN + s) % 2, KT)
            big_loop(G_PIN, 1, KT)
            for g in range(4):
                slot = (G_GRP + g) % 2
                pe.wait_ge(split_ready, G_GRP + g - G_KPE + 2)
                pe.wait_ge(d_split, g + 1)
                for n in range(4):
                    q = 4 * g + n
                    if q < 2:
                        pe.wait_ge(acc_free[n], turn_of(G_GRP + (G_GRP + n) % 2))
                    else:
                        pe.wait_ge(grp_y, q - 1)
                    for k in range(4):
                        ks = slice(k * LORA + n * P, k * LORA + (n + 1) * P)
                        for i, (w, d) in enumerate(((w_hi, d_hi), (w_hi, d_lo), (w_lo, d_hi))):
                            for a in range(2):
                                m = small(PS[:, 2 * (n % 2) + a, 0:HALF], w[:, slot, ks], d[:, k, a * HALF:(a + 1) * HALF],
                                          k == 0 and i == 0, k == 3 and i == 2)
                    m.then_inc(grp_mm, 1)
                pe.wait_ge(grp_mm, 4 * g + 4)
                pe.nop().then_inc(mm_done, 1)
            pe.wait_ge(y_ready, KT)
            big_loop(G_POUT, 0, KT // 2)
            row_sums(2)

        def parts(ap_rows):
            return ((0, slice(0, HALF), slice(0, HALF), 0), (1, slice(0, NP - HALF), slice(HALF, NP), 0),
                    (1, slice(NP - HALF, HALF), slice(NP, R), 1))

        @block.scalar
        def _(act):
            act.wait_ge(cond_in, 16)
            act.activation(cond_t[:], cond_t[:], ACT.Silu).then_inc(cond_ready, 1)
            act.wait_ge(condb_in, 16)
            act.activation(cond_b[:], cond_b[:], ACT.Silu).then_inc(condb_ready, 1)

            def square(k, dst):
                act.activation(dst, at(x, k), ACT.Square).then_inc(sq_ready, 1)

            for c in range(CHUNKS):
                act.wait_ge(mm_done, 4 * c + 4)
                if c:
                    act.wait_ge(ada_turned, c)
                act.activation(stage[0:2, 1, 0:512], PS[0:2, 0, :], ACT.Copy).then_inc(ada_row, 1)
                for k in range(8 * c, 8 * c + 8) if c < 2 else ():
                    if k == 0:
                        act.wait_ge(x_in, 16)
                    if k >= 2:
                        act.wait_ge(sq_added, k - 1)
                    act.activation((stage[:, 0], rstd[:])[k % 2], x[:, k], ACT.Square).then_inc(sq_ready, 1)
            act.wait_ge(ada_row, CHUNKS)
            for s in range(2):
                act.activation(act_tmp[0:1, s:s + 1], stage[0:1, 1, 0:1], ACT.Copy).then_inc(acc_free[s], 1)

            def root(n):
                act.wait_ge(var_eps, n + 1)
                act.activation(rstd[:], rstd[:], ACT.Sqrt).then_inc(std_ready, 1)

            def affine(n):
                with act.Fori(0, KT // 2) as t:
                    for s in range(2):
                        if n == 0:
                            act.wait_ge(x_normed, 2 * t + (s + 1))
                            act.wait_ge(h_ready, 2 * t + (s + 1))
                        else:
                            act.wait_ge(xn_ready, 2 * t + (s + 1))
                        for c, r in ((0, slice(0, NP)), (1, slice(NP, R))):
                            src = at(x, 2 * t + s)[:, r] if n == 0 else stage[:, s, r]
                            ins = act.activation(stage[:, s, r], src, ACT.Identity,
                                                 scale=aff[:, c, bass.ds(2 * t + s, 1)],
                                                 bias=mod[:, c, bass.ds(2 * t + (3 * KT * n + s), 1)])
                        ins.then_inc(hf_ready, 1)

            root(0)
            affine(0)
            act.wait_ge(mm_done, G_KPE + 1)
            act.activation(rows(kpe[:]), acc[G_KPE % 2], ACT.Copy).then_inc(acc_free[G_KPE % 2], 1)

            def load_ada(t, s, a):
                act.wait_ge(adr_used, 2 * t + (a + 1))
                act.dma_start(w_adr[:, a % 2], tile_of(wd2, s, t + (a // 2 + 1))).then_inc(adr_in[a % 2], 16)

            def store_loop(g0, first, end, func, out2, base, ada=None):
                with act.Fori(first, end) as t:
                    for s in range(2):
                        if ada is not None:
                            load_ada(t, s, ada + s)
                        slot = (g0 + s) % 2
                        act.wait_ge(mm_done, 2 * t + (g0 + s + 1))
                        act.activation(rows(stage[:, s]), acc[slot], func).then_inc(acc_free[slot], 1)
                        act.wait_ge(acc_free[slot], t + turn_of(g0 + s + 2))
                        act.dma_start(tile_of(out2, s, t), stage[:, s]).then_inc(stored[s], 16)
                    for s in range(2):
                        act.wait_ge(stored[s], 16 * t + (base + 16))

            store_loop(G_Z, 0, ZT // 2, ACT.Copy, z2, 0, ADA_P0)
            store_loop(G_GATE, 0, GT // 2 - 1, ACT.Silu, g2, 16 * ZT // 2, ADA_P0 + ZT)
            store_loop(G_GATE, GT // 2 - 1, GT // 2, ACT.Silu, g2, 16 * ZT // 2)

            act.wait_ge(lam_sum, 1)
            act.activation(lam_w[:, 2:4], lam_w[:, 0:2], ACT.Exp).then_inc(lam_exp, 1)

            act.wait_ge(mq_in, 64)
            act.activation(lat_sq[:, 0], cq[:], ACT.Square).then_inc(mq_sq, 1)
            act.activation(lat_sq[:, 1], ckT[:], ACT.Square).then_inc(mq_sq, 1)
            for a in range(2):
                act.wait_ge(mq_var, a + 1)
                act.activation(qn[:, a], qn[:, a], ACT.Sqrt).then_inc(mq_std, 1)
            act.wait_ge(mq_norm, 2)
            act.dma_start(ckv_out.rearrange("t p r -> p t r"), ckT[:]).then_inc(latent_out, 16)
            act.wait_ge(kp_done, 1)
            act.dma_start(kpe_out, kpe[0:DQK, :]).then_inc(latent_out, 16)
            for j in range(QT + 1):
                nk = P if j < QT else NS
                act.wait_ge(mq_tr, j + 1)
                act.activation(ckR[0:nk, j, :], PS[0:nk, 4 + j % 2, :], ACT.Copy).then_inc(mq_ev, 1)

            with act.Fori(0, HEADS // 2) as t:
                act.wait_ge(ml_item, 6 * t + 2)
                act.activation(rows(qn[:, 1]), PS[:, 2:4, 0:HALF], ACT.Copy).then_inc(ml_ev_a, 1)
                act.wait_ge(ml_item, 6 * t + 4)
                act.activation(kn[:], PS[:, 0:2, :], ACT.Copy).then_inc(ml_ev_a, 1)
                act.wait_ge(ml_item, 6 * t + 5)
                act.activation(vb[:].rearrange("p (a j) e -> p a (j e)", a=2), PS[:, 2:4, :], ACT.Copy).then_inc(ml_ev_a, 1)
                for u in range(8):
                    n = P * (u % QT + 1)
                    if u >= 3:
                        act.wait_ge(ml_tr, 8 * t + u - 2)
                    act.wait_ge(ml_max, 8 * t + u + 1)
                    act.activation(px[:, u % 3, 0:n], PS[:, u % 4, 0:n], ACT.Exp, bias=st[:, 1, u:u + 1],
                                   scale=MLA_SCALE, accum_out=st[:, 2, u:u + 1]).then_inc(ml_exp, 1)

            for g in range(2):
                act.wait_ge(ms_max, g + 1)
                act.activation(rows(pxs[:, g]), PS[:, 2 * g:2 * g + 2, 0:HALF], ACT.Exp, bias=sts[:, g, 1:2],
                               scale=MLA_SCALE, accum_out=sts[:, g, 2:3]).then_inc(ms_exp, 1)
            for g in range(2):
                act.wait_ge(ms_pv, g + 1)
                act.activation(ols[:, :, 4 * g:4 * g + 4, :].rearrange("p c h r -> p c (h r)"),
                               PS[:, g, :].rearrange("p (c n) -> p c n", c=LT), ACT.Copy).then_inc(ms_olev, 1)

            with act.Fori(0, HEADS // 2) as t:
                for s in range(2):
                    act.wait_ge(df_vt, 2 * t + s + 1)
                    act.activation(vr[:, s, 0:QT, :].rearrange("p j e -> p (j e)"), PS[:, 6, :], ACT.Copy)
                    act.activation(vr[0:NS, s, QT, :], PS[0:NS, 7, 0:P], ACT.Copy).then_inc(df_vrev, 1)
                for u in range(8):
                    n, slot = P * (u % QT + 1), u % 3
                    if u >= 3:
                        act.wait_ge(df_tr, 8 * t + u - 2)
                    act.wait_ge(df_max, 8 * t + u + 1)
                    for e in range(2):
                        ins = act.activation(pxd[:, slot, e, 0:n], PS[:, 2 * (u % 2) + e, 0:n], ACT.Exp,
                                             bias=std[:, u, 2 + e:3 + e], scale=DIFF_SCALE,
                                             accum_out=std[:, u, 4 + e:5 + e])
                    ins.then_inc(df_exp, 1)
                    if u == 6:
                        act.wait_ge(df_pv, 2 * t + 1)
                        act.activation(at(od, 2 * t)[:, 0:NP], PS[:, 6, :], ACT.Copy).then_inc(df_od, 1)
                act.wait_ge(dfs_max, t + 1)
                act.activation(rows(pxds[:]), PS[:, 0:2, 0:HALF], ACT.Exp, bias=std[:, 8, 1:2],
                               scale=DIFF_SCALE, accum_out=std[:, 8, 2:3]).then_inc(dfs_exp, 1)
                act.wait_ge(df_pv, 2 * t + 2)
                act.activation(at(od, 2 * t + 1)[:, 0:NP], PS[:, 7, :], ACT.Copy).then_inc(df_od, 1)
                act.wait_ge(dfs_pv, t + 1)
                act.activation(od[:, bass.ds(2 * t, 2), NP:R], PS[:, 2:4, 0:NS], ACT.Copy).then_inc(df_od, 1)
            act.wait_ge(df_od, 3 * (HEADS // 2) + 1)
            for h in range(HEADS):
                if h >= 2:
                    act.wait_ge(df_ssq, h - 1)
                act.activation(sqd[:, h % 2], od[:, h], ACT.Square).then_inc(df_sq, 1)
            act.wait_ge(df_var, 1)
            act.activation(rs8[:], rs8[:], ACT.Sqrt).then_inc(df_std, 1)

            act.wait_ge(condb_in, 32)
            act.activation(cond_b[:], cond_b[:], ACT.Silu).then_inc(condb_ready, 1)

            def gated(t, g0, n, gate_tile, ada=None):
                for s in range(2):
                    if ada is not None:
                        load_ada(t, s, ada + s)
                    slot = (g0 + s) % 2
                    act.wait_ge(mm_done, 2 * t + (g0 + s + 1))
                    act.wait_ge(sq_added, 2 * t + (KT * n + s - 1))
                    for bank, cols, r, c in parts(R):
                        ins = act.activation(stage[:, s, r], PS[:, 2 * slot + bank, cols], ACT.Identity,
                                             scale=mod[:, c, bass.ds(2 * t + (gate_tile + s), 1)])
                    ins.then_inc(acc_free[slot], 1)
                    act.wait_ge(x_new, 2 * t + (KT * (n - 1) + s + 1))
                    square(2 * t + s, stage[:, s])

            with act.Fori(0, KT // 2 - 1) as t:
                gated(t, G_OUT, 1, 2 * KT, ADA_P0 + ADA_P1)
            with act.Fori(KT // 2 - 1, KT // 2) as t:
                gated(t, G_OUT, 1, 2 * KT)
            root(1)
            affine(1)

            act.wait_ge(pad_zero, 1)
            with act.Fori(0, KT) as t:
                us, gs = G_PIN % 2, (G_PIN + 1) % 2
                act.activation(u_ext[:, PAD + NP:2 * PAD + NP], at(pool_pre, t), ACT.Copy)
                act.wait_ge(mm_done, 2 * t + (G_PIN + 1))
                for bank, cols, r, c in parts(R):
                    off = PAD + r.start + PAD * c
                    ins = act.activation(u_ext[:, off:off + r.stop - r.start], PS[:, 2 * us + bank, cols], ACT.Copy)
                ins.then_inc(acc_free[us], 1)
                act.wait_ge(d_ready, t + 1)
                act.dma_start(d_scr[bass.ds(t, 1)].rearrange("t p r -> p (t r)"), d_st[:]).then_inc(d_stored, 16)
                act.wait_ge(mm_done, 2 * t + (G_PIN + 2))
                act.activation(rows(stage[:, 1]), acc[gs], ACT.Silu).then_inc(acc_free[gs], 1)
                act.wait_ge(acc_free[gs], t + turn_of(G_PIN + 3))
                act.dma_start(pg_scr[bass.ds(t, 1)].rearrange("t p r -> p (t r)"), stage[:, 1]).then_inc(pg_stored, 16)
                act.wait_ge(pg_stored, 16 * t + 16)
            act.dma_start(pool_out, pool_last[:]).then_inc(out_done, 16)

            with act.Fori(0, KT // 2) as t:
                gated(t, G_POUT, 2, 5 * KT)
            root(2)

        @block.vector
        def _(dve):
            dve.memset(ssq[:], 0.0).then_inc(split_ready, 1)
            dve.wait_ge(split_ready, 1)

            def row_scale(n):
                dve.wait_ge(var_ready, n + 1)
                sums = PS[:, 6:8, 0:HALF] if n else PS[:, 2:4, 0:HALF]
                dve.tensor_scalar(rows(rstd[:]), sums, 1.0 / D, EPS, ALU.mult, ALU.add).then_inc(var_eps, 1)
                if n < 2:
                    dve.memset(ssq[:], 0.0).then_inc(ssq_zero, 1)
                    dve.wait_ge(ssq_zero, n + 1)
                dve.wait_ge(std_ready, n + 1)
                vchain(dve, dve.reciprocal(rstd[:], rstd[:]))

            def add_bias(a, b):
                for c in range(2):
                    ins = dve.tensor_tensor(mod[:, c, a:b], mod[:, c, a:b], bada_t[:, a:b], ALU.add)
                vchain(dve, ins)

            def fold_scale(n):
                a = (3 * n + 1) * KT
                for c in range(2):
                    ins = dve.scalar_tensor_tensor(out=aff[:, c, :], in0=mod[:, c, a:a + KT], scalar=1.0,
                                                   in1=gnorm_t[:, n, :], op0=ALU.add, op1=ALU.mult)
                vchain(dve, ins)

            def split(g, t2=0, t=0):
                slot = g % 2
                dve.wait_ge(raw_in[slot], 16 * t + 16 * (g // 2 + 1))
                dve.wait_ge(mm_done, t2 + (g - 1))
                vchain(dve, dve.tensor_copy(w_hi[:, slot], w_raw[:, slot]))
                dve.tensor_tensor(w_lo[:, slot], w_raw[:, slot], w_hi[:, slot].bitcast(F32),
                                  ALU.subtract).then_inc(split_ready, 1)

            def make_h(n):
                with dve.Fori(0, KT // 2) as t:
                    dv.loop(t, 2)
                    for s in range(2):
                        if n:
                            dve.tensor_tensor(stage[:, s], at(x, 2 * t + s), rstd[:], ALU.mult).then_inc(xn_ready, 1)
                    for s in range(2):
                        dve.wait_ge(hf_ready, 2 * t + (KT * n + s + 1))
                        vchain(dve, dve.tensor_copy(at(h_hi, 2 * t + s), stage[:, s]))
                        dve.tensor_tensor(at(h_lo, 2 * t + s), stage[:, s], at(h_hi, 2 * t + s).bitcast(F32),
                                          ALU.subtract).then_inc(h_ready, 1)
                    dve.wait_ge(h_ready, 2 * t + (KT * n + 4))
                dv.end(KT // 2)

            def ada_tile(a, t2, t):
                slot = a % 2
                dve.wait_ge(adr_in[slot], 16 * t + 16 * (a // 2 + 1))
                for c in range(2):
                    ins = dve.tensor_tensor_reduce(ada_junk, w_adr[:, slot], cond_b[:, c, :], 1.0, 0.0, ALU.mult, ALU.add,
                                                   ada_acc[:, c:c + 1])
                    if c == 0:
                        vchain(dve, ins)
                ins.then_inc(adr_used, 1)
                dve.wait_ge(adr_used, t2 + a + 1)
                vchain(dve, dve.tensor_copy(mod[:, :, bass.ds(t2 + (ADA_PE + a), 1)].rearrange("p c k -> p (c k)"),
                                            ada_acc[:]))

            dve.wait_ge(condb_ready, 1)
            with dve.Fori(0, ADA_P0 // 2) as t:
                dv.loop(t, 4)
                for s in range(2):
                    ada_tile(s, 2 * t, t)
            dv.end(ADA_P0 // 2)
            row_scale(0)
            for k in range(KT):
                dve.tensor_tensor(x[:, k], x[:, k], rstd[:], ALU.mult).then_inc(x_normed, 1)
            dve.wait_ge(consts_in, CONSTS)
            add_bias(ADA_PE, ADA_PE + ADA_P0)
            split(G_KPE)
            dve.wait_ge(ada_turned, CHUNKS)
            turned = PS[:, 1, 0:2 * ADA_PE].rearrange("p (t c) -> p c t", c=2)
            for c in range(2):
                ins = dve.tensor_tensor(mod[:, c, 0:ADA_PE], turned[:, c, :], bada_t[:, 0:ADA_PE], ALU.add)
            vchain(dve, ins)
            fold_scale(0)
            dve.wait_ge(sq_added, KT)
            for s in range(2):
                dve.memset(ada_acc[:, s:s + 1], 0.0).then_inc(h_ready, 1)
            make_h(0)
            with dve.Fori(0, ZT // 2) as t:
                dv.loop(t, 6)
                for s in range(2):
                    split(G_Z + s, 2 * t, t)
                    ada_tile(ADA_P0 + s, 2 * t, t)
            dv.end(ZT // 2)
            with dve.Fori(0, GT // 2) as t:
                dv.loop(t, 6)
                for s in range(2):
                    split(G_GATE + s, 2 * t, t)
                    ada_tile(ADA_P0 + ZT + s, 2 * t, t)
            dv.end(GT // 2)
            add_bias(ADA_PE + ADA_P0, ADA_PE + ADA_P0 + ADA_P1)

            dve.tensor_copy(maskq_t[:], maskq_f[:]).then_inc(masks_ready, 1)
            dve.tensor_copy(maskk_t[:], maskk_f[:]).then_inc(masks_ready, 1)
            for i in range(2):
                ins = dve.tensor_tensor_reduce(lam_in[:, 2 * i, :], lam_in[:, 2 * i, :], lam_in[:, 2 * i + 1, :], 1.0, 0.0,
                                               ALU.mult, ALU.add, lam_w[:, i:i + 1])
            ins.then_inc(lam_sum, 1)
            dve.wait_ge(lam_exp, 1)
            vchain(dve, dve.tensor_tensor(lam_w[:, 4:5], lam_w[:, 3:4], lam_w[:, 2:3], ALU.subtract))
            vchain(dve, dve.tensor_scalar(neg_lam, lam_w[:, 4:5], -LAM_INIT, None, ALU.add))
            vchain(dve, dve.scalar_tensor_tensor(out=coef, in0=lamsel_t[:, 1:2], scalar=neg_lam, in1=lamsel_t[:, 0:1],
                                                 op0=ALU.mult, op1=ALU.add))
            vchain(dve, dve.tensor_scalar(gsub_v, gsub_v, 1.0 - LAM_INIT, None, ALU.mult))

            dve.wait_ge(mm_done, G_OUT)
            for s in range(2):
                dve.wait_ge(acc_free[s], turn_of(G_OUT + (G_OUT + s) % 2))
            dve.wait_ge(stored[0], 16 * (ZT + GT) // 2)
            dve.wait_ge(stored[1], 16 * (ZT + GT) // 2)
            dve.memset(lam_in[:, 0, 0:1], 0.0).then_inc(qps_free, 1)
            for a in range(2):
                dve.wait_ge(mq_sum, a + 1)
                dve.tensor_scalar(rows(qn[:, a]), PS[:, 2 * a:2 * a + 2, 0:HALF], 1.0 / LORA, EPS, ALU.mult,
                                  ALU.add).then_inc(mq_var, 1)
            dve.wait_ge(kp_swap, 1)
            dve.tensor_tensor(rows(qpr[:]), PS[:, 6:8, 0:HALF], rows(sin_t[:]), ALU.mult)
            vchain(dve, dve.tensor_tensor(kpe[:], kpe[:], cos_t[:], ALU.mult))
            dve.tensor_tensor(kpe[:], kpe[:], qpr[:], ALU.add).then_inc(kp_done, 1)
            for a, (lat, g_v) in enumerate(((cq, gqa_v), (ckT, gkva_v))):
                dve.wait_ge(mq_std, a + 1)
                vchain(dve, dve.reciprocal(qn[:, a], qn[:, a]))
                for c in range(LT):
                    ins = dve.scalar_tensor_tensor(out=lat[:, c, :], in0=lat[:, c, :], scalar=g_v[:, c:c + 1],
                                                   in1=qn[:, a], op0=ALU.mult, op1=ALU.mult)
                ins.then_inc(mq_norm, 1)

            def halves_of_h(src, hi, lo, done):
                vchain(dve, dve.tensor_copy(hi, src))
                dve.tensor_tensor(lo, src, hi.bitcast(F32), ALU.subtract).then_inc(done, 1)

            dve.wait_ge(qps_zero, 1)
            dve.memset(lam_in[:, 0, 0:1], 0.0).then_inc(ml_fin, 1)
            with dve.Fori(0, HEADS // 2) as t:
                dv.loop(t, 1 + 8 * 2 + 2 * 2)
                dve.wait_ge(ml_item, 6 * t + 1)
                dve.tensor_copy(rows(qn[:, 0]), PS[:, 0:2, 0:HALF]).then_inc(ml_ev_d, 1)
                dve.wait_ge(ml_item, 6 * t + 3)
                dve.tensor_copy(rows(qpr[:]), PS[:, 4:6, 0:HALF]).then_inc(ml_ev_d, 1)
                dve.wait_ge(ml_ev_d, 3 * t + 2)
                dve.tensor_tensor(qpe[:], qpr[:], cos_t[:], ALU.mult)
                dve.wait_ge(ml_swap, t + 1)
                vchain(dve, dve.tensor_tensor(rows(qsin[:]), PS[:, 6:8, 0:HALF], rows(sin_t[:]), ALU.mult))
                dve.tensor_tensor(qpe[:], qpe[:], qsin[:], ALU.add).then_inc(ml_qpe, 1)
                dve.wait_ge(ml_item, 6 * t + 6)
                dve.tensor_copy(qls[:, :, bass.ds(2 * t, 2), :].rearrange("p c h r -> p h c r"),
                                PS[:, 4, 0:2 * LT * NS].rearrange("p (h c r) -> p h c r", h=2, c=LT)).then_inc(ml_ev_d, 1)
                dve.wait_ge(ml_qpe, t + 1)
                for s in range(2):
                    e = slice(DQK * s, DQK * s + DQK)
                    dve.tensor_copy(qps[e, bass.ds(2 * t + s, 1), :].rearrange("p h r -> p (h r)"), qpe[e, NP:R])

                def maxima(u):
                    n = P * (u % QT + 1)
                    dve.wait_ge(ml_score, 8 * t + u + 1)
                    vchain(dve, dve.tensor_reduce(st[:, 0, u:u + 1], PS[:, u % 4, 0:n], AX.X, ALU.max))
                    dve.tensor_scalar(st[:, 1, u:u + 1], st[:, 0, u:u + 1], -MLA_SCALE, None, ALU.mult).then_inc(ml_max, 1)

                def normalise(u):
                    n = P * (u % QT + 1)
                    dve.wait_ge(ml_exp, 8 * t + u + 1)
                    vchain(dve, dve.reciprocal(st[:, 3, u:u + 1], st[:, 2, u:u + 1]))
                    dve.tensor_scalar(px[:, u % 3, 0:n], px[:, u % 3, 0:n], st[:, 3, u:u + 1], None,
                                      ALU.mult).then_inc(ml_norm, 1)

                def turned_out(u):
                    i = u % QT
                    dve.wait_ge(ml_tr, 8 * t + u + 1)
                    dve.tensor_copy(pt[:, u // QT, 0:i + 1, P * i:P * i + P],
                                    PS[:, 4 + u % 2, 0:P * (i + 1)].rearrange("p (j q) -> p j q", q=P)).then_inc(ml_ptev, 1)

                def finish(s):
                    dve.wait_ge(ml_pv, 2 * t + s + 1)
                    dve.wait_ge(ml_v_in, 32 * t + 32)
                    if s:
                        dve.wait_ge(ml_fin, 2 * t + 2)
                    vchain(dve, dve.tensor_tensor(fo[:], PS[:, 6 + s, :], sg[:, s, 0:NP], ALU.mult))
                    hi, lo = (at(h, 2 * t + (HEADS + s))[:, 0:NP] for h in (h_hi, h_lo))
                    halves_of_h(fo[:], hi, lo, ml_fin)

                for u in range(10):
                    if u < 8:
                        maxima(u)
                    if 1 <= u < 9:
                        normalise(u - 1)
                    if u >= 2:
                        turned_out(u - 2)
                    if u == 6:
                        finish(0)
                finish(1)
                dve.wait_ge(ml_fin, 2 * t + 3)
            dv.end(HEADS // 2)

            for g in range(2):
                dve.wait_ge(ms_score, g + 1)
                vchain(dve, dve.tensor_reduce(sts[:, g, 0:1], PS[:, 2 * g:2 * g + 2, 0:HALF], AX.XY, ALU.max))
                dve.tensor_scalar(sts[:, g, 1:2], sts[:, g, 0:1], -MLA_SCALE, None, ALU.mult).then_inc(ms_max, 1)
            for g in range(2):
                dve.wait_ge(ms_exp, g + 1)
                vchain(dve, dve.reciprocal(sts[:, g, 3:4], sts[:, g, 2:3]))
                dve.tensor_scalar(pxs[:, g], pxs[:, g], sts[:, g, 3:4], None, ALU.mult).then_inc(ms_norm, 1)
            for g in range(2):
                dve.wait_ge(ms_tr, g + 1)
                dve.tensor_copy(pts[:, g, 0:KTS - 1, :].rearrange("p j q -> p (j q)"), PS[:, 4 + g, :])
                dve.tensor_copy(pts[0:NS, g, KTS - 1, :], PS[0:NS, 6 + g, 0:P]).then_inc(ms_ptev, 1)
            dve.wait_ge(ms_ob, 1)
            vchain(dve, dve.tensor_tensor(ofs[:], PS[:, 2, 0:HEADS * NS].rearrange("p (h r) -> p h r", r=NS), sgs[:], ALU.mult))
            halves_of_h(ofs[:], h_hi[:, HEADS:2 * HEADS, NP:R], h_lo[:, HEADS:2 * HEADS, NP:R], ms_fin)

            dve.memset(lam_in[:, 0, 0:1], 0.0).then_inc(df_od, 1)
            with dve.Fori(0, HEADS // 2) as t:
                dv.loop(t, 8 * 5 + 4)

                def maxima(u):
                    n, b = P * (u % QT + 1), 2 * (u % 2)
                    dve.wait_ge(df_score, 8 * t + u + 1)
                    vchain(dve, dve.tensor_reduce(std[:, u, 0:2], PS[:, b:b + 2, 0:n], AX.X, ALU.max))
                    dve.tensor_scalar(std[:, u, 2:4], std[:, u, 0:2], -DIFF_SCALE, None, ALU.mult).then_inc(df_max, 1)

                def combine(u):
                    n, slot = P * (u % QT + 1), u % 3
                    dve.wait_ge(df_exp, 8 * t + u + 1)
                    vchain(dve, dve.reciprocal(std[:, u, 6:8], std[:, u, 4:6]))
                    vchain(dve, dve.tensor_scalar(std[:, u, 0:1], std[:, u, 7:8], neg_lam, None, ALU.mult))
                    vchain(dve, dve.tensor_scalar(pxd[:, slot, 1, 0:n], pxd[:, slot, 1, 0:n], std[:, u, 0:1], None, ALU.mult))
                    vchain(dve, dve.scalar_tensor_tensor(out=pxd[:, slot, 0, 0:n], in0=pxd[:, slot, 0, 0:n],
                                                         scalar=std[:, u, 6:7], in1=pxd[:, slot, 1, 0:n],
                                                         op0=ALU.mult, op1=ALU.add))
                    dve.memset(lam_in[:, 0, 0:1], 0.0).then_inc(df_norm, 1)

                def turned_out(u):
                    s, i = u // QT, u % QT
                    dve.wait_ge(df_tr, 8 * t + u + 1)
                    dve.tensor_copy(ptd[:, s, 0:i + 1, P * i:P * i + P],
                                    PS[:, 4 + u % 2, 0:P * (i + 1)].rearrange("p (j q) -> p j q", q=P)).then_inc(df_ptev, 1)

                for u in range(10):
                    if u < 8:
                        maxima(u)
                    if u == 8:
                        dve.wait_ge(dfs_score, t + 1)
                        vchain(dve, dve.tensor_reduce(std[:, 8, 0:1], PS[:, 0:2, 0:HALF], AX.XY, ALU.max))
                        dve.tensor_scalar(std[:, 8, 1:2], std[:, 8, 0:1], -DIFF_SCALE, None, ALU.mult).then_inc(dfs_max, 1)
                    if 1 <= u < 9:
                        combine(u - 1)
                    if u >= 2:
                        turned_out(u - 2)
                dve.wait_ge(dfs_exp, t + 1)
                vchain(dve, dve.reciprocal(std[:, 8, 3:4], std[:, 8, 2:3]))
                vchain(dve, dve.tensor_scalar(std[:, 8, 4:5], std[:, 8, 3:4], coef, None, ALU.mult))
                vchain(dve, dve.tensor_scalar(pxds[:], pxds[:], std[:, 8, 4:5], None, ALU.mult))
                dve.memset(lam_in[:, 0, 0:1], 0.0).then_inc(dfs_norm, 1)
                dve.wait_ge(dfs_tr, t + 1)
                most = PS[:, 4, :].rearrange("p (j s e r) -> p j s e r", j=KTS - 1, s=2, e=2)
                rest = PS[0:NS, 5, 0:P].rearrange("p (s e r) -> p s e r", s=2, e=2)
                dve.tensor_copy(ptd1[:, 0:KTS - 1], most[:, :, :, 1, :])
                dve.tensor_copy(ptd1[0:NS, KTS - 1], rest[:, :, 1, :]).then_inc(df_tmp, 1)
                dve.wait_ge(df_tmp, t + 1)
                dve.tensor_tensor(ptds[:, 0:KTS - 1], most[:, :, :, 0, :], ptd1[:, 0:KTS - 1], ALU.add)
                dve.tensor_tensor(ptds[0:NS, KTS - 1], rest[:, :, 0, :], ptd1[0:NS, KTS - 1], ALU.add).then_inc(dfs_ptev, 1)
                dve.wait_ge(dfs_ptev, t + 1)
            dv.end(HEADS // 2)

            dve.wait_ge(dfs_pv, HEADS // 2)
            split(G_OUT)
            dve.wait_ge(df_ssq, HEADS)
            dve.tensor_scalar(rows(rs8[:]), PS[0:HEADS, 4:6, 0:HALF], 1.0 / P, SUB_EPS, ALU.mult, ALU.add).then_inc(df_var, 1)
            dve.wait_ge(df_std, 1)
            dve.reciprocal(rs8[:], rs8[:]).then_inc(df_rs, 1)
            dve.wait_ge(df_g_in, 32)
            for h in range(HEADS):
                b = 4 + 2 * (h % 2)
                dve.wait_ge(df_wide, h + 1)
                vchain(dve, dve.scalar_tensor_tensor(out=rows(od[:, h]), in0=PS[:, b:b + 2, 0:HALF], scalar=gsub_v,
                                                     in1=rows(od[:, h]), op0=ALU.mult, op1=ALU.mult))
                vchain(dve, dve.tensor_tensor(od[:, h], od[:, h], sgd[:, h], ALU.mult))
                halves_of_h(od[:, h], h_hi[:, h], h_lo[:, h], df_fin)

            def update(g, t2, t, n, k, slot):
                dve.wait_ge(acc_free[g % 2], t + turn_of(g + 2))
                dve.tensor_tensor(at(x, t2 + k), at(x, t2 + k), stage[:, slot], ALU.add).then_inc(x_new, 1)

            dve.wait_ge(x_in, 32)
            dve.wait_ge(condb_ready, 2)
            with dve.Fori(0, KT // 2) as t:
                dv.loop(t, 6)
                for s in range(2):
                    split(G_OUT + s + 1, 2 * t, t)
                    ada_tile(ADA_P0 + ADA_P1 + s, 2 * t, t)
                    update(G_OUT + s, 2 * t, t, 1, s, s)
            dv.end(KT // 2)
            add_bias(ADA_PE + ADA_P0 + ADA_P1, ADA_T)
            dve.memset(lam_in[:, 0, 0:1], 0.0).then_inc(pad_free, 1)
            fold_scale(1)
            row_scale(1)
            make_h(1)

            us = G_PIN % 2
            first, samp = slice(PAD, PAD + NP), slice(2 * PAD + NP, 2 * PAD + R)
            for grp, w in enumerate(WIN):
                with dve.Fori(4 * grp, 4 * grp + 4) as t:
                    t0 = t - 4 * grp
                    dv.loop(t0, 2 + grp + 1 + 1 + 1)
                    dve_t2 = 2 * t
                    split(G_PIN + 1, dve_t2, t)
                    dve.wait_ge(acc_free[us], t + turn_of(G_PIN + 2))
                    width = 2 * PAD + R
                    src = u_ext
                    for step, dst in zip(range(grp + 1), (w2, w4, w2, w4)):
                        lag = 1 << step
                        lo = 2 * lag - 1
                        vchain(dve, dve.tensor_tensor(dst[:, lo:width], src[:, lo:width], src[:, lo - lag:width - lag], ALU.add))
                        src = dst
                    dve.scalar_tensor_tensor(out=d_st[:, NP:R], in0=src[:, samp], scalar=1.0 / w, in1=u_ext[:, samp],
                                             op0=ALU.mult, op1=ALU.subtract)
                    dve.tensor_tensor(fix[:], src[:, PAD:PAD + 16], rcount_t[:, grp, :], ALU.mult)
                    vchain(dve, dve.scalar_tensor_tensor(out=d_st[:, 0:NP], in0=src[:, first], scalar=1.0 / w,
                                                         in1=u_ext[:, first], op0=ALU.mult, op1=ALU.subtract))
                    dve.tensor_tensor(d_st[:, 0:16], fix[:], u_ext[:, PAD:PAD + 16], ALU.subtract)
                    last = pool_last[:, bass.ds(t, 1), :, :].rearrange("p t a k -> p (t a) k")
                    dve.tensor_copy(last[:, 0, :], u_ext[:, NP:PAD + NP])
                    vchain(dve, dve.tensor_copy(last[:, 1, :], u_ext[:, PAD + R:2 * PAD + R]))
                    dve.memset(lam_in[:, 0, 0:1], 0.0).then_inc(d_ready, 1)
                    split(G_PIN + 2, dve_t2, t)
                    dve.wait_ge(d_stored, 16 * t + 16)
                dv.end(4)

            for g in range(4):
                dve.wait_ge(grp_in[0], 16 * g + 16)
                if g:
                    dve.wait_ge(grp_mm, 4 * g)
                vchain(dve, dve.tensor_copy(d_hi[:], d_raw[:]))
                dve.tensor_tensor(d_lo[:], d_raw[:], d_hi[:].bitcast(F32), ALU.subtract).then_inc(d_split, 1)
                split(G_GRP + g + 1)
                dve.wait_ge(grp_in[1], 16 * g + 16)
                for n in range(4):
                    q = 4 * g + n
                    dve.wait_ge(grp_mm, q + 1)
                    dve.scalar_tensor_tensor(out=rows(stage[:, n % 2]), in0=acc[n % 2], scalar=scale_v[:, q:q + 1],
                                             in1=rows(pg[:, n]), op0=ALU.mult, op1=ALU.mult).then_inc(grp_y, 1)
                    dve.wait_ge(grp_y, q + 1)
                    halves_of_h(stage[:, n % 2], h_hi[:, q], h_lo[:, q], y_ready)
                dve.memset(lam_in[:, 0, 0:1], 0.0).then_inc(acc_free[(G_GRP + g) % 2], 1)

            with dve.Fori(0, KT // 2 - 1) as t:
                dv.loop(t, 2)
                for s in range(2):
                    split(G_POUT + s + 1, 2 * t, t)
                    update(G_POUT + s, 2 * t, t, 2, s, s)
            dv.end(KT // 2 - 1)
            split(G_END - 1)
            for k in range(KT - 2, KT):
                update(G_POUT + k, 0, 0, 2, k, k % 2)
            row_scale(2)
            for k in range(KT):
                dve.scalar_tensor_tensor(out=x[:, k], in0=x[:, k], scalar=gfin_v[:, k:k + 1], in1=rstd[:],
                                         op0=ALU.mult, op1=ALU.mult).then_inc(y_fin, 1)


def tables():
    half = DQK // 2
    inv = (np.float32(10000.0) ** (-np.arange(half, dtype=np.float32) / np.float32(half))).astype(np.float32)
    pos = np.concatenate([np.arange(NP), PAST + np.arange(NS)]).astype(np.float32)
    ang = (pos[None, :] * inv[:, None]).astype(np.float32)
    cos, sin = np.tile(np.cos(ang), (4, 1)), np.tile(np.sin(ang), (4, 1))
    swap = np.zeros((P, P), np.float32)
    for m in range(P):
        if m % DQK < half:
            swap[m + half, m] = -1.0
        else:
            swap[m - half, m] = 1.0
    maskq = np.zeros((1, P), np.float32)
    maskq[0, :DQK] = 1.0
    maskk = np.full((1, DQK), MASKED, np.float32)
    rcount = np.zeros((P, 4, 16), np.float32)
    for g, w in enumerate(WIN):
        rcount[:, g, :] = np.float32(1.0) / np.minimum(np.arange(16) + 1, w).astype(np.float32)
    lamsel = np.zeros((P, 2), np.float32)
    for r in range(P):
        lamsel[r, (r // NS) % 2] = 1.0
    return {"cosT": cos.astype(np.float32), "sinT": sin.astype(np.float32), "swap": swap, "ident": np.eye(P, dtype=np.float32),
            "maskq": maskq, "maskk": maskk, "rcount": rcount, "lamsel": lamsel,
            "selc": np.ascontiguousarray(np.broadcast_to(np.eye(HEADS, dtype=np.float32), (P, HEADS, HEADS))),
            "selr": np.ascontiguousarray(np.repeat(np.eye(HEADS, dtype=np.float32)[:, :, None], P, axis=2))}


def lay_out(i):
    def tiles(w):
        k, n = w.shape
        return np.ascontiguousarray(w.reshape(k // P, P, n // P, P).transpose(2, 1, 0, 3)).reshape(n // P, P, k)

    def vec(v):
        return np.ascontiguousarray(v.reshape(-1, P).T)

    def featT(a):
        return np.ascontiguousarray(a.T.reshape(-1, P, a.shape[0]).transpose(1, 0, 2))

    f = {k: np.asarray(v) for k, v in i.items()}
    w_in = f["w_in_att"][0]
    c0 = 3 * HEADS * P
    q_w, k_w, v_w = w_in[:, 0:1024], w_in[:, 1024:2048], w_in[:, 2048:c0]
    cq_w, ckv_w, kpe_w = w_in[:, c0:c0 + LORA], w_in[:, c0 + LORA:c0 + 2 * LORA], w_in[:, c0 + 2 * LORA:c0 + 2 * LORA + DQK]
    gate_w = w_in[:, c0 + 2 * LORA + DQK:]
    ada = np.concatenate([f["w_ada"][0], f["w_ada"][1]], axis=1)
    pin = f["w_in_pool"][0].reshape(D, 2, KT, P).transpose(0, 2, 1, 3).reshape(D, 4096)
    c = np.concatenate([f["c_prompt"], f["c_sample"]], axis=0)
    heads_first = lambda w: np.ascontiguousarray(w.reshape(LT, P, HEADS, P).transpose(2, 1, 0, 3)).reshape(HEADS, P, LORA)
    out = {
        "xT": featT(np.concatenate([f["x_prompt"][0], f["x_sample"][0]], axis=0)),
        "cT": np.ascontiguousarray(c.T.reshape(KT, P, 2).transpose(1, 0, 2)),
        "cB": c.reshape(1, 2 * D),
        "w_ada_pe": np.ascontiguousarray(ada[:, :ADA_PE * P].reshape(4, 4, P, CHUNKS, 512).transpose(3, 0, 2, 1, 4))
                    .reshape(ADA_PE, P, D),
        "w_ada_dve": np.ascontiguousarray(ada[:, ADA_PE * P:].T).reshape(ADA_T - ADA_PE, P, D),
        "bada": vec(f["b_ada"].reshape(-1)),
        "gnorm": np.ascontiguousarray(f["g_norm"].reshape(2, KT, P).transpose(2, 0, 1)),
        "w_kpe": tiles(np.concatenate([kpe_w, kpe_w], axis=1))[0],
        "w_z": tiles(np.concatenate([cq_w, ckv_w, q_w, k_w, v_w], axis=1)),
        "w_gate": tiles(gate_w), "w_out": tiles(f["w_out_att"][0]), "w_pin": tiles(pin),
        "w_grp": np.ascontiguousarray(f["w_grp_pool"][0].reshape(4, 4, P, LORA).transpose(0, 2, 1, 3)).reshape(4, P, D),
        "w_pout": tiles(f["w_out_pool"][0]),
        "lamv": np.concatenate([f[k][0] for k in ("lam_q1", "lam_k1", "lam_q2", "lam_k2")]).reshape(1, 4 * DQK),
        "gsub": vec(f["g_subln"][0]), "gqa": vec(f["g_qa"][0]), "gkva": vec(f["g_kva"][0]),
        "w_uq": heads_first(f["w_uq"][0]),
        "w_uqr": np.ascontiguousarray(f["w_uqr"][0].reshape(LT, P, 4, P).transpose(2, 1, 0, 3)).reshape(4, P, LORA),
        "w_ukT": np.ascontiguousarray(f["w_uk"][0].transpose(1, 2, 0)),
        "w_uv": heads_first(f["w_uv"][0]), "w_uk": heads_first(f["w_uk"][0]),
        "w_uv2": np.ascontiguousarray(f["w_uv"][0].reshape(LT, P, 4, 2 * P).transpose(2, 1, 0, 3)).reshape(4, P, 2 * LORA),
        "scale_pool": vec(f["scale_pool"][0]), "gfin": vec(f["g_final"]),
        "kc": np.ascontiguousarray(f["cache_diff_k"][0, 0].transpose(1, 2, 0)),
        "vc": f["cache_diff_v"][0, 0].reshape(PAST, HEADS * P),
        "ckvT": np.ascontiguousarray(f["cache_mla_ckv"][0, 0].T), "ckv": f["cache_mla_ckv"][0, 0],
        "kpeT": np.ascontiguousarray(f["cache_mla_kpe"][0, 0].T),
        "poolT": featT(f["state_pool"][0, 0]),
    }
    out.update(tables())
    return out


_ARGS = ("xT cT cB w_ada_pe w_ada_dve bada gnorm w_kpe w_z w_gate w_out w_pin w_grp w_pout lamv gsub gqa gkva w_uq w_uqr "
         "w_ukT w_uv w_uk w_uv2 scale_pool gfin kc vc ckvT ckv kpeT poolT cosT sinT swap ident maskq maskk rcount lamsel selc selr").split()
_OUTS = (("y", (KT, P, R)), ("z", (ZT, P, R)), ("ckv_new", (LT, P, R)), ("kpe_new", (DQK, R)), ("pool_new", (P, KT, 2, PAD)))


def kernel(**inputs):
    import concourse.bacc as _bacc
    from concourse.bass_utils import run_bass_kernel_spmd as _run

    nc = _bacc.Bacc("TRN2", target_bir_lowering=False, num_devices=1)
    arrays, args = {}, []
    laid = lay_out(inputs)
    for name in _ARGS:
        a = np.ascontiguousarray(laid[name])
        arrays[f"in_{name}"] = a
        args.append(nc.dram_tensor(f"in_{name}", a.shape, mybir.dt.from_np(a.dtype), kind="ExternalInput").ap())
    for name, shape in _OUTS:
        args.append(nc.dram_tensor(f"out_{name}", shape, F32, kind="ExternalOutput").ap())
    program(nc, *args)
    res = _run(nc, [arrays], core_ids=[0]).results[0]
    yT = res["out_y"].reshape(D, R).T
    z = res["out_z"].reshape(ZT * P, R).T
    ck = res["out_ckv_new"].reshape(LORA, R).T
    kp = res["out_kpe_new"].T
    pool = res["out_pool_new"].transpose(2, 3, 1, 0).reshape(2, PAD, D)
    ka, va = z[:, ZK * P:ZV * P], z[:, ZV * P:ZT * P]
    C = np.ascontiguousarray
    group = lambda r0, r1, n: (C(ka[r0:r1]).reshape(1, 1, n, HEADS, P), C(va[r0:r1]).reshape(1, 1, n, HEADS, P),
                               C(ck[r0:r1]).reshape(1, 1, n, LORA), C(kp[r0:r1]).reshape(1, 1, n, DQK))
    return (C(yT[0:NP]).reshape(1, NP, D), C(yT[NP:R]).reshape(1, NS, D),
            *group(0, NP, NP), C(pool[0]).reshape(1, 1, PAD, D),
            *group(NP, R, NS), C(pool[1]).reshape(1, 1, PAD, D))
```

```python
from contextlib import ExitStack
import math

import numpy as np

import concourse.bass as bass
from concourse import mybir

F32 = mybir.dt.float32
F32R = mybir.dt.float32r
ALU = mybir.AluOpType
ACT = mybir.ActivationFunctionType
AX = mybir.AxisListType

P = 128
D = 2048
KT = D // P
NP, NS = 512, 32
R = NP + NS
HALF = R // 2
PAST = 512
HEADS = 8
QT = NP // P
KTS = PAST // P + 1
SKEYS = PAST + NS
LORA = 512
LT = LORA // P
ZT = 32
ZQ, ZK, ZV = 8, 16, 24
GT = 16
ADA_PE = 16
ADA_P0 = 16
ADA_P1 = 48
ADA_T = 96
DQK = 64
LAM_INIT = 0.8 - 0.6 * math.exp(-0.3 * 0)
EPS, SUB_EPS = 1e-6, 1e-5
DIFF_SCALE = DQK ** -0.5
MLA_SCALE = (128 + 64) ** -0.5
MASKED = -float(2 ** 100)
WIN = (2, 4, 8, 16)
PAD = 15
PIN_BYTES = 4 * (3 * (2 * PAD + R) + R + 16)

G_KPE = ADA_PE
G_Z = G_KPE + 1
G_GATE = G_Z + ZT
G_OUT = G_GATE + GT
G_PIN = G_OUT + KT
G_GRP = G_PIN + 2 * KT
G_POUT = G_GRP + 4
G_END = G_POUT + KT
CHUNKS = ADA_PE // 4
LAG = 3
NORM_AT = 8
RING = 6


def turn_of(g):
    return g // 2 - (G_KPE // 2 - 1)


class Tally:

    def __init__(self, sem):
        self.sem, self.base, self.k, self.t, self.per = sem, 0, 0, None, 0

    def loop(self, t, per):
        self.base, self.k, self.t, self.per = self.base + self.k, 0, t, per

    def end(self, count):
        assert self.k == self.per, (self.k, self.per)
        self.base, self.k, self.t, self.per = self.base + self.per * count, 0, None, 0

    def inc(self, ins):
        ins.then_inc(self.sem, 1)
        self.k += 1
        return self.base + self.k + (self.per * self.t if self.t is not None else 0)


def program(nc, xT, cT, cB, w_ada_pe, w_ada_dve, bada, gnorm, w_kpe, w_z, w_gate, w_out, w_pin, w_grp, w_pout,
            lamv, gsub, gqa, gkva, w_uq, w_uqr, w_ukT, w_uv, w_uk, w_uv2, scale_pool, gfin,
            kc, vc, ckvT, ckv, kpeT, poolT, cosT, sinT, swap, ident, rcount, lamsel, selc, selr,
            y_out, z_out, ckv_out, kpe_out, pool_out):
    g_scr = nc.dram_tensor("gate_scratch", (GT, P, R), F32, kind="Internal").ap()
    d_scr = nc.dram_tensor("pool_d_scratch", (KT, P, R), F32, kind="Internal").ap()
    pg_scr = nc.dram_tensor("pool_gate_scratch", (KT, P, R), F32, kind="Internal").ap()

    keep = ExitStack()
    with keep:
        def sb(name, shape, dt=F32, scope=keep):
            return scope.enter_context(nc.sbuf_tensor(name, shape, dt))

        def sem(name):
            return keep.enter_context(nc.semaphore(name))

        h_hi = sb("h_hi", [P, KT, R], F32R)
        h_lo = sb("h_lo", [P, KT, R], F32R)
        w_raw = sb("w_raw", [P, 2, D])
        kpe = sb("kpe", [P, R])
        rstd = sb("rstd", [P, R])
        ssq = sb("ssq", [P, R])
        cos_t = sb("cos_t", [P, R])
        sin_t = sb("sin_t", [P, R])
        swap_t = sb("swap_t", [P, P])
        id_t = sb("id_t", [P, P])
        ones = sb("ones", [P, P])
        maskq_t = sb("maskq_t", [1, P], mybir.dt.bfloat16)
        maskk_t = sb("maskk_t", [1, DQK], mybir.dt.bfloat16)
        sel_col = sb("sel_col", [P, HEADS, HEADS])
        mod = sb("mod", [P, 2, ADA_T])
        bada_t = sb("bada_t", [P, ADA_T])
        gnorm_t = sb("gnorm_t", [P, 2, KT])
        aff = sb("aff", [P, 2, KT])
        cond_t = sb("cond_t", [P, KT, 2])
        vecs = sb("vecs", [P, 3, KT])
        pool_last = sb("pool_last", [P, KT, 2, PAD])
        pool_pre = sb("pool_pre", [P, KT, PAD])
        ada_acc = sb("ada_acc", [P, 2])
        act_tmp = sb("act_tmp", [P, 8])
        rcount_t = sb("rcount_t", [P, 4, 16])
        lam_in = sb("lam_in", [P, 4, DQK])
        lam_w = sb("lam_w", [P, 8])
        lamsel_t = sb("lamsel_t", [P, 2])
        PS = keep.enter_context(nc.psum_tensor("banks", [P, 8, 512], F32))

        scale_v, gfin_v = vecs[:, 0, :], vecs[:, 1, :]
        gsub_v, gqa_v, gkva_v = vecs[:, 2, 0:1], vecs[:, 2, 1:5], vecs[:, 2, 5:9]
        neg_lam, coef = lam_w[:, 6:7], lam_w[:, 7:8]
        rows = lambda ap: ap.rearrange("p (a r) -> p a r", a=2)
        acc = [PS[:, 2 * s:2 * s + 2, 0:HALF] for s in range(2)]
        ada_junk = PS[:, 4:8, :].rearrange("p a b -> p (a b)")

        stream = ExitStack()
        x = sb("x", [P, KT, R], scope=stream)
        p0_stack = ExitStack()
        w_more = sb("w_more", [P, 4, D], scope=p0_stack)
        p0_stack.close()
        w_hi = sb("w_hi", [P, 2, D], F32R, stream)
        w_lo = sb("w_lo", [P, 2, D], F32R, stream)
        stage = sb("stage", [P, 2, R], scope=stream)
        ada_stack = ExitStack()
        w_adr = sb("w_adr", [P, 2, D], scope=ada_stack)
        cond_b = sb("cond_b", [P, 2, D], scope=ada_stack)
        ada_stack.close()
        pin_stack = ExitStack()
        u_ext = sb("u_ext", [P, PAD + NP + PAD + NS], scope=pin_stack)
        w2 = sb("w2", [P, PAD + NP + PAD + NS], scope=pin_stack)
        w4 = sb("w4", [P, PAD + NP + PAD + NS], scope=pin_stack)
        d_st = sb("d_st", [P, R], scope=pin_stack)
        fix = sb("fix", [P, 16], scope=pin_stack)
        pin_stack.close()
        grp_stack = ExitStack()
        d_hi3 = sb("d_hi3", [P, 4, R], F32R, grp_stack)
        sb("rest_of_windows", [P, PIN_BYTES // 4 - 4 * R], scope=grp_stack)
        d_raw = sb("d_raw", [P, 4, R], scope=grp_stack)
        pg = sb("pg", [P, 4, R], scope=grp_stack)
        d_lo3 = sb("d_lo3", [P, 4, R], F32R, grp_stack)
        grp_stack.close()
        stream.close()

        mla = ExitStack()
        ckT = sb("ckT", [P, LT, R], scope=mla)
        kpc = sb("kpc", [P, PAST], scope=mla)
        early = ExitStack()
        lat_sum = sb("lat_sum", [P, 2, R], scope=early)
        lat_sq = sb("lat_sq", [P, R], scope=early)
        early.close()
        ckR = sb("ckR", [P, LORA], scope=mla)
        qls = sb("qls", [P, LT, HEADS, NS], scope=mla)
        qps = sb("qps", [P, HEADS, NS], scope=mla)
        ml_loop = ExitStack()
        cq = sb("cq", [P, LT, R], scope=ml_loop)
        wq = sb("wq", [P, 2, LT, P], scope=ml_loop)
        wk = sb("wk", [P, 2, LT, P], scope=ml_loop)
        wkT = sb("wkT", [P, 2, LORA], scope=ml_loop)
        wr = sb("wr", [P, LT, P], scope=ml_loop)
        wv = sb("wv", [P, LT, 2 * P], scope=ml_loop)
        qn = sb("qn", [P, 2, R], scope=ml_loop)
        qpr = sb("qpr", [P, R], scope=ml_loop)
        qpe = sb("qpe", [P, R], scope=ml_loop)
        qsin = sb("qsin", [P, R], scope=ml_loop)
        kn = sb("kn", [P, 2, NP], scope=ml_loop)
        vb = sb("vb", [P, QT, 2 * P], scope=ml_loop)
        px = sb("px", [P, 3, NP], scope=ml_loop)
        pt = sb("pt", [P, 2, QT, NP], scope=ml_loop)
        fo = sb("fo", [P, NP], scope=ml_loop)
        sg = sb("sg", [P, 2, R], scope=ml_loop)
        st = sb("st", [P, 4, 8], scope=ml_loop)
        lat_r = (qpe, qsin)
        ml_loop.close()
        ml_samp = ExitStack()
        ccT = sb("ccT", [P, LT, PAST], scope=ml_samp)
        ccR = sb("ccR", [P, LT, LORA], scope=ml_samp)
        wva = sb("wva", [P, LT, HEADS * P], scope=ml_samp)
        pxs = sb("pxs", [P, 2, SKEYS], scope=ml_samp)
        pts = sb("pts", [P, 2, KTS, P], scope=ml_samp)
        ols = sb("ols", [P, LT, HEADS, NS], scope=ml_samp)
        sgs = sb("sgs", [P, HEADS, NS], scope=ml_samp)
        ofs = sb("ofs", [P, HEADS, NS], scope=ml_samp)
        sts = sb("sts", [P, 2, 4], scope=ml_samp)
        ml_samp.close()
        mla.close()

        dif = ExitStack()
        od = sb("od", [P, HEADS, R], scope=dif)
        sgd = sb("sgd", [P, HEADS, R], scope=dif)
        qd = sb("qd", [P, 2, R], scope=dif)
        kd = sb("kd", [P, 2, R], scope=dif)
        vd = sb("vd", [P, 2, R], scope=dif)
        kcs = sb("kcs", [P, 2, PAST], scope=dif)
        vcs = sb("vcs", [P, 2, QT, P], scope=dif)
        vr = sb("vr", [P, 2, KTS, P], scope=dif)
        pxd = sb("pxd", [P, 3, 2, NP], scope=dif)
        ptd = sb("ptd", [P, 2, QT, NP], scope=dif)
        pxds = sb("pxds", [P, SKEYS], scope=dif)
        ptds = sb("ptds", [P, KTS, 2, NS], scope=dif)
        ptd1 = sb("ptd1", [P, KTS, 2, NS], scope=dif)
        std = sb("std", [P, 9, 8], scope=dif)
        sqd = sb("sqd", [P, 2, R], scope=dif)
        rs8 = sb("rs8", [HEADS, R], scope=dif)
        sel_row = sb("sel_row", [HEADS, HEADS, P], scope=dif)
        dif.close()

        consts_in = sem("consts_in"); x_in = sem("x_in"); x_rest_in = sem("x_rest_in"); cond_in = sem("cond_in")
        condb_in = sem("condb_in")
        raw_in = [sem(f"raw_in{s}") for s in range(2)]
        ring_in = [sem(f"ring_in{i}") for i in range(RING)]
        adr_in = [sem(f"adr_in{s}") for s in range(2)]
        cond_ready = sem("cond_ready"); mod_ready = sem("mod_ready"); condb_ready = sem("condb_ready")
        adr_used = sem("adr_used")
        split_ready = sem("split_ready")
        mm_done = sem("mm_done")
        acc_free = [sem(f"acc_free{s}") for s in range(2)]
        sq_ready = sem("sq_ready"); sq_added = sem("sq_added"); ssq_zero = sem("ssq_zero"); var_eps = sem("var_eps")
        var_ready = sem("var_ready"); std_ready = sem("std_ready"); rstd_ready = sem("rstd_ready")
        xn_ready = sem("xn_ready"); hf_ready = sem("hf_ready"); h_ready = sem("h_ready")
        dve_step = sem("dve_step"); ada_row = sem("ada_row"); ada_turned = sem("ada_turned")
        x_normed = sem("x_normed"); ones_ready = sem("ones_ready")
        stored = [sem(f"stored{s}") for s in range(2)]
        lam_exp = sem("lam_exp"); lam_sum = sem("lam_sum")
        out_done = sem("out_done")
        dv = Tally(dve_step)
        mq_in = sem("mq_in"); lat_step = sem("lat_step"); mq_sum = sem("mq_sum"); mq_var = sem("mq_var")
        mq_std = sem("mq_std"); mq_norm = sem("mq_norm"); mq_tr = sem("mq_tr"); mq_ev = sem("mq_ev")
        kp_swap = sem("kp_swap"); kp_done = sem("kp_done"); latent_out = sem("latent_out")
        ml_w_in = sem("ml_w_in"); ml_v_in = sem("ml_v_in"); ml_item = sem("ml_item"); ml_ev_d = sem("ml_ev_d")
        ml_ev_a = sem("ml_ev_a")
        ml_swap = sem("ml_swap"); ml_qpe = sem("ml_qpe"); ml_score = sem("ml_score"); ml_max = sem("ml_max")
        ml_exp = sem("ml_exp"); ml_norm = sem("ml_norm"); ml_tr = sem("ml_tr"); ml_ptev = sem("ml_ptev")
        ml_pv = sem("ml_pv"); masks_ready = sem("masks_ready"); ml_fin = sem("ml_fin"); qps_zero = sem("qps_zero")
        ms_in = sem("ms_in"); ms_w_in = sem("ms_w_in"); ms_score = sem("ms_score"); ms_max = sem("ms_max")
        ms_exp = sem("ms_exp")
        ms_norm = sem("ms_norm"); ms_tr = sem("ms_tr"); ms_ptev = sem("ms_ptev"); ms_pv = sem("ms_pv")
        ms_olev = sem("ms_olev"); ms_ob = sem("ms_ob"); ms_fin = sem("ms_fin")
        df_a_in = sem("df_a_in"); df_v_in = sem("df_v_in"); df_g_in = sem("df_g_in"); df_vt = sem("df_vt")
        df_vrev = sem("df_vrev"); df_score = sem("df_score"); df_max = sem("df_max"); df_exp = sem("df_exp")
        df_norm = sem("df_norm"); df_tr = sem("df_tr"); df_ptev = sem("df_ptev"); df_pv = sem("df_pv")
        df_od = sem("df_od"); df_vd_in = sem("df_vd_in"); df_sq = sem("df_sq"); df_ssq = sem("df_ssq"); df_var = sem("df_var")
        df_std = sem("df_std"); df_rs = sem("df_rs"); df_wide = sem("df_wide"); df_tmp = sem("df_tmp")
        df_fin = sem("df_fin"); df_scaled = sem("df_scaled"); df_upper = sem("df_upper")
        dfs_score = sem("dfs_score"); dfs_max = sem("dfs_max"); dfs_exp = sem("dfs_exp")
        dfs_norm = sem("dfs_norm"); dfs_tr = sem("dfs_tr"); dfs_ptev = sem("dfs_ptev"); dfs_pv = sem("dfs_pv")
        x_new = sem("x_new")
        d_ready = sem("d_ready"); d_stored = sem("d_stored")
        pg_stored = sem("pg_stored"); grp_in = sem("grp_in"); pg_in = [sem(f"pg_in{n}") for n in range(4)]
        d_upper = sem("d_upper"); y_upper = sem("y_upper"); grp_mm = sem("grp_mm")
        grp_y = sem("grp_y"); d_split = sem("d_split"); y_ready = sem("y_ready"); y_fin = sem("y_fin")
        pad_zero = sem("pad_zero"); pad_free = sem("pad_free"); qps_free = sem("qps_free")
        y_stored = [sem(f"y_stored{s}") for s in range(2)]

        def vchain(dve, ins):
            dve.wait_ge(dve_step, dv.inc(ins))

        def pairs(ap):
            return ap.rearrange("(t s) p n -> s t p n", s=2)

        def tile_of(pair, s, t):
            return pair[s, bass.ds(t, 1)].rearrange("t p n -> p (t n)")

        def at(ap, k):
            return ap[:, bass.ds(k, 1), :].rearrange("p k r -> p (k r)")

        def unit(u):
            return (0, u) if u < QT else (1, 2 * QT - 1 - u)

        def lower_h0(eng, k):
            eng.wait_ge(hf_ready, k + 1)
            for c, r in GROUP_ROWS:
                ins = eng.scalar_tensor_tensor(out=h_lo[:, k, r], in0=x[:, k, r], scalar=mod[:, c, k:k + 1],
                                               in1=h_hi[:, k, r].bitcast(F32), op0=ALU.add, op1=ALU.subtract)
            ins.then_inc(h_ready, 1)

        GROUP_ROWS = ((0, slice(0, NP)), (1, slice(NP, R)))

        scaled_x = (stage[:, 0], stage[:, 1], w2[:, 0:R], w4[:, 0:R])
        d_halves = [(h_hi[:, 4 * g:4 * g + 4], h_lo[:, 4 * g:4 * g + 4]) for g in range(1, 4)] + [(d_hi3, d_lo3)]
        ring = [w_raw[:, i] if i < 2 else w_more[:, i - 2] for i in range(RING)]

        wz2, wg2, wo2, wp2, wy2 = (pairs(a) for a in (w_z, w_gate, w_out, w_pin, w_pout))
        wd2, z2, g2 = pairs(w_ada_dve), pairs(z_out), pairs(g_scr)
        CONSTS = 16 * 16
        block = keep.enter_context(nc.Block())

        @block.sync
        def _(sp):
            sp.dma_start(cond_t[:], cT).then_inc(cond_in, 16)

            def load_w(src, slot, ready=None):
                if ready is not None:
                    sp.wait_ge(split_ready, ready)
                sp.dma_start(w_raw[:, slot], src).then_inc(raw_in[slot], 16)

            def load_ada(pair_slot, src, used=None):
                if used is not None:
                    sp.wait_ge(adr_used, used)
                sp.dma_start(w_adr[:, pair_slot], src).then_inc(adr_in[pair_slot], 16)

            for g in range(ADA_PE):
                if g >= RING:
                    sp.wait_ge(mm_done, g - RING + 1)
                sp.dma_start(ring[g % RING], w_ada_pe[g]).then_inc(ring_in[g % RING], 16)
                if g == 0:
                    sp.dma_start(cond_b[:], cB.to_broadcast((P, 2 * D)).rearrange("p (a d) -> p a d", a=2)).then_inc(condb_in, 16)
                if g < ADA_P0:
                    load_ada(g % 2, w_ada_dve[g], g - 1 if g >= 2 else None)
                if g == 1:
                    sp.dma_start(x[:], xT).then_inc(x_in, 16)
            sp.wait_ge(mm_done, G_KPE - 1)
            load_w(w_kpe, G_KPE % 2)
            for a in range(ADA_P0, ADA_P0 + 2):
                load_ada(a % 2, w_ada_dve[a], a - 1)
            sp.wait_ge(mm_done, G_KPE)
            with sp.Fori(0, ZT // 2) as t:
                for s in range(2):
                    load_w(tile_of(wz2, s, t), (G_Z + s) % 2, 2 * t + G_Z - G_KPE + s)
            sp.wait_ge(h_ready, KT + 2)
            for s in range(2):
                sp.wait_ge(stored[s], 16 * 2 * LT // 2)
            sp.dma_start(cq[:], z_out[0:LT].rearrange("t p r -> p t r")).then_inc(mq_in, 16)
            sp.dma_start(ckT[:], z_out[LT:2 * LT].rearrange("t p r -> p t r")).then_inc(mq_in, 16)
            for e in range(2):
                sp.dma_start(kpc[64 * e:64 * e + 64, :], kpeT).then_inc(mq_in, 16)
            with sp.Fori(0, GT // 2) as t:
                for s in range(2):
                    load_w(tile_of(wg2, s, t), (G_GATE + s) % 2, 2 * t + G_GATE - G_KPE + s)
            for s in range(2):
                load_w(w_out[s], (G_OUT + s) % 2, G_OUT - G_KPE + s)

            sp.wait_ge(mm_done, G_OUT)
            sp.wait_ge(adr_used, ADA_P0 + ADA_P1)
            for s in range(2):
                sp.wait_ge(stored[s], 16 * (ZT + GT) // 2)

            uq2, uk2, ukT2 = (a.rearrange("(t s) p n -> s t p n", s=2) for a in (w_uq, w_uk, w_ukT))

            def load_mla_w(t):
                for s in range(2):
                    sp.dma_start(wq[:, s].rearrange("p c d -> p (c d)"), tile_of(uq2, s, t)).then_inc(ml_w_in, 16)
                    sp.dma_start(wk[:, s].rearrange("p c d -> p (c d)"), tile_of(uk2, s, t)).then_inc(ml_w_in, 16)
                    sp.dma_start(wkT[:, s], tile_of(ukT2, s, t)).then_inc(ml_w_in, 16)
                sp.dma_start(wr[:].rearrange("p c d -> p (c d)"),
                             w_uqr[bass.ds(t, 1)].rearrange("t p n -> p (t n)")).then_inc(ml_w_in, 16)
                sp.dma_start(wv[:].rearrange("p c d -> p (c d)"),
                             w_uv2[bass.ds(t, 1)].rearrange("t p n -> p (t n)")).then_inc(ml_w_in, 16)

            def load_mla_g(t):
                for s in range(2):
                    sp.dma_start(sg[:, s], tile_of(g2, s, t + HEADS // 2)).then_inc(ml_v_in, 16)

            load_mla_w(0)
            load_mla_g(0)
            with sp.Fori(0, HEADS // 2 - 1) as t:
                sp.wait_ge(ml_item, 6 * t + 6)
                load_mla_w(t + 1)
                sp.wait_ge(ml_fin, 2 * t + 3)
                load_mla_g(t + 1)
            sp.wait_ge(ml_item, 6 * (HEADS // 2))
            sp.dma_start(ccT[:], ckvT.rearrange("(c p) k -> p c k", p=P)).then_inc(ms_in, 16)
            sp.dma_start(ccR[:], ckv.rearrange("(k p) c -> p k c", p=P)).then_inc(ms_in, 16)
            sp.wait_ge(ml_fin, HEADS + 1)
            for h in range(HEADS):
                sp.dma_start(wva[:, :, h * P:(h + 1) * P],
                             w_uv[h].rearrange("p (c v) -> p c v", c=LT)).then_inc(ms_w_in, 16)
            sp.dma_start(sgs[:], g_scr[HEADS:2 * HEADS, :, NP:R].rearrange("h p r -> p h r")).then_inc(ms_w_in, 16)

            sp.wait_ge(ms_fin, 1)
            sp.wait_ge(latent_out, 32)
            kc2 = kc.rearrange("(t s) p k -> s t p k", s=2)
            vc2 = vc.rearrange("(j p) (t s e) -> s t p j e", p=P, s=2, e=P)

            def load_qk(t):
                for s in range(2):
                    sp.dma_start(qd[:, s], tile_of(z2, s, t + ZQ // 2)).then_inc(df_a_in, 16)
                    sp.dma_start(kd[:, s], tile_of(z2, s, t + ZK // 2)).then_inc(df_a_in, 16)
                    sp.dma_start(kcs[:, s], tile_of(kc2, s, t)).then_inc(df_a_in, 16)

            def load_v(t):
                for s in range(2):
                    sp.dma_start(vd[:, s], tile_of(z2, s, t + ZV // 2)).then_inc(df_vd_in, 16)

            def load_vc(t):
                for s in range(2):
                    sp.dma_start(vcs[:, s], vc2[s, bass.ds(t, 1)].rearrange("t p j e -> p (t j) e")).then_inc(df_v_in, 16)

            load_v(0)
            load_qk(0)
            load_vc(0)
            sp.dma_start(sgd[:], g_scr[0:HEADS].rearrange("h p r -> p h r")).then_inc(df_g_in, 16)
            sp.dma_start(sel_row[:], selr).then_inc(df_g_in, 16)
            with sp.Fori(0, HEADS // 2 - 1) as t:
                sp.wait_ge(df_vt, 2 * t + 2)
                load_v(t + 1)
                sp.wait_ge(dfs_score, t + 1)
                load_qk(t + 1)
                sp.wait_ge(dfs_pv, t + 1)
                load_vc(t + 1)

            load_w(w_out[2], G_OUT % 2, G_OUT + 2 - G_KPE)
            sp.wait_ge(df_fin, HEADS)
            sp.dma_start(cond_b[:], cB.to_broadcast((P, 2 * D)).rearrange("p (a d) -> p a d", a=2)).then_inc(condb_in, 16)
            sp.dma_start(x[:, 0:4], xT[:, 0:4]).then_inc(x_in, 16)
            for s in range(2):
                load_ada(s, w_ada_dve[ADA_P0 + ADA_P1 + s])
            load_w(w_out[3], (G_OUT + 1) % 2, G_OUT + 3 - G_KPE)
            sp.dma_start(x[:, 4:KT], xT[:, 4:KT]).then_inc(x_rest_in, 16)
            with sp.Fori(0, KT // 2 - 2) as t:
                for s in range(2):
                    load_w(tile_of(wo2, s, t + 2), (G_OUT + s) % 2, 2 * t + 4 + G_OUT - G_KPE + s)
            with sp.Fori(0, KT) as t:
                for s in range(2):
                    load_w(tile_of(wp2, s, t), (G_PIN + s) % 2, 2 * t + G_PIN - G_KPE + s)
            for g in range(2):
                load_w(w_grp[g], (G_GRP + g) % 2, G_GRP - G_KPE + g)
            for g in range(4):
                sp.wait_ge(d_stored, 16 * (4 * g + 4))
                if g:
                    sp.wait_ge(d_split, 4 * g)
                sp.dma_start(d_raw[:], d_scr[4 * g:4 * g + 4].rearrange("t p r -> p t r")).then_inc(grp_in, 16)
                load_w(w_grp[g + 2] if g < 2 else w_pout[g - 2], (G_GRP + g) % 2, G_GRP + 2 - G_KPE + g)
                sp.wait_ge(pg_stored, 16 * (4 * g + 4))
                for n in range(4):
                    if g:
                        sp.wait_ge(grp_y, 4 * (g - 1) + n + 1)
                    sp.dma_start(pg[:, n], pg_scr[4 * g + n]).then_inc(pg_in[n], 16)
            with sp.Fori(1, KT // 2) as t:
                for s in range(2):
                    load_w(tile_of(wy2, s, t), (G_POUT + s) % 2, 2 * t + G_POUT - G_KPE + s)
            for k in range(KT):
                sp.wait_ge(y_fin, k + 1)
                sp.dma_start(y_out[k], x[:, k]).then_inc(y_stored[k % 2], 16)
            sp.wait_ge(out_done, 16)
            for s in range(2):
                sp.wait_ge(y_stored[s], 16 * KT // 2)

        @block.gpsimd
        def _(pool):
            pool.memset(ones[:], 1.0).then_inc(ones_ready, 1)
            for dst, src in ((cos_t, cosT), (sin_t, sinT), (swap_t, swap), (id_t, ident), (sel_col, selc),
                             (bada_t, bada), (gnorm_t, gnorm), (rcount_t, rcount), (lamsel_t, lamsel), (pool_pre, poolT)):
                pool.dma_start(dst[:], src).then_inc(consts_in, 16)
            for dst, src in ((scale_v, scale_pool), (gfin_v, gfin), (gsub_v, gsub), (gqa_v, gqa), (gkva_v, gkva)):
                pool.dma_start(dst, src).then_inc(consts_in, 16)
            pool.dma_start(lam_in[:], lamv.to_broadcast((P, 4 * DQK)).rearrange("p (a d) -> p a d", a=4)).then_inc(consts_in, 16)

            pool.wait_ge(split_ready, 1)
            for k in range(KT):
                pool.wait_ge(sq_ready, k + 1)
                pool.tensor_tensor(ssq[:], ssq[:], (stage[:, 0], rstd[:])[k % 2], ALU.add).then_inc(sq_added, 1)
                pool.wait_ge(sq_added, k + 1)
            pool.wait_ge(rstd_ready, 1)
            for k in range(KT):
                pool.tensor_tensor(x[:, k], x[:, k], rstd[:], ALU.mult).then_inc(x_normed, 1)

            pool.wait_ge(mq_in, 64)
            for a, lat in enumerate((cq, ckT)):
                for c in range(LT):
                    dst = lat_sum[:, a] if c == 0 else lat_sq[:]
                    pool.tensor_tensor(dst, lat[:, c], lat[:, c], ALU.mult).then_inc(lat_step, 1)
                    pool.wait_ge(lat_step, a * (2 * LT - 1) + max(2 * c, 1))
                    if c:
                        pool.tensor_tensor(lat_sum[:, a], lat_sum[:, a], lat_sq[:], ALU.add).then_inc(lat_step, 1)
                        pool.wait_ge(lat_step, a * (2 * LT - 1) + 2 * c + 1)
            pool.wait_ge(qps_free, 1)
            pool.memset(qps[:], 0.0).then_inc(qps_zero, 1)

            def add_squares(n):
                pool.wait_ge(ssq_zero, n)
                with pool.Fori(0, KT // 2) as t:
                    for s in range(2):
                        pool.wait_ge(sq_ready, 2 * t + (KT * n + s + 1))
                        pool.tensor_tensor(ssq[:], ssq[:], stage[:, s], ALU.add).then_inc(sq_added, 1)
                        pool.wait_ge(sq_added, 2 * t + (KT * n + s + 1))

            add_squares(1)
            pool.wait_ge(pad_free, 1)
            pool.memset(u_ext[:, 0:PAD], 0.0).then_inc(pad_zero, 1)
            add_squares(2)

        @block.tensor
        def _(pe):
            def small(out, lhsT, rhs, start, stop):
                return pe.matmul(out, lhsT, rhs, start=start, stop=stop)

            def row_sums(n):
                if n == 0:
                    pe.wait_ge(ones_ready, 1)
                pe.wait_ge(sq_added, KT * (n + 1))
                for a in range(2):
                    m = small(PS[:, (6 if n else 2) + a, 0:HALF], ones[:], ssq[:, a * HALF:(a + 1) * HALF], True, True)
                m.then_inc(var_ready, 1)

            pe.wait_ge(cond_ready, 1)

            def ada_turn(c):
                if c == 0:
                    pe.wait_ge(consts_in, CONSTS)
                pe.wait_ge(ada_row, c + 1)
                if c:
                    pe.wait_ge(mod_ready, c)
                for q in range(4):
                    f = 2 * (4 * c + q)
                    m = pe.transpose(PS[:, 1, f:f + 2], stage[0:2, 1, q * P:(q + 1) * P], id_t[0:2, 0:2])
                m.then_inc(ada_turned, 1)

            for g in range(ADA_PE):
                c = g // 4
                pe.wait_ge(ring_in[g % RING], 16 * (g // RING + 1))
                if g % 4 == 0 and c:
                    pe.wait_ge(ada_row, c)
                for k in range(4):
                    m = small(PS[0:2, 0, :], cond_t[:, 4 * (g % 4) + k, :], ring[g % RING][:, k * 512:(k + 1) * 512],
                              g % 4 == 0 and k == 0, g % 4 == 3 and k == 3)
                m.then_inc(mm_done, 1)
                if g % 4 == 1 and c:
                    ada_turn(c - 1)
                if g == ADA_PE - 7:
                    row_sums(0)

            def tile_products(slot, k, first, last):
                ks = slice(k * P, (k + 1) * P)
                for i, (w, h) in enumerate(((w_hi, h_hi), (w_hi, h_lo), (w_lo, h_hi))):
                    for a in range(2):
                        m = small(PS[:, 2 * slot + a, 0:HALF], w[:, slot, ks], h[:, k, a * HALF:(a + 1) * HALF],
                                  first and i == 0, last and i == 2)
                return m

            def big_tile(slot, h_wait=None):
                for k in range(KT):
                    if h_wait is not None:
                        pe.wait_ge(h_ready, h_wait + k + 3)
                    m = tile_products(slot, k, k == 0, k == KT - 1)
                m.then_inc(mm_done, 1)

            def big_wait(g, twice_t=0, t=0):
                pe.wait_ge(split_ready, twice_t + (g - G_KPE + 2))
                pe.wait_ge(acc_free[g % 2], t + turn_of(g))

            def big_loop(g0, first, end):
                with pe.Fori(first, end) as t:
                    for s in range(2):
                        big_wait(g0 + s, 2 * t, t)
                        big_tile((g0 + s) % 2)

            ada_turn(CHUNKS - 1)
            big_wait(G_KPE)
            big_tile(G_KPE % 2, 0)
            big_loop(G_Z, 0, ZT // 2)
            big_loop(G_GATE, 0, GT // 2)

            for s in range(2):
                pe.wait_ge(acc_free[s], turn_of(G_OUT + (G_OUT + s) % 2))
            pe.wait_ge(lat_step, 2 * (2 * LT - 1))
            pe.wait_ge(adr_used, ADA_P0 + ADA_P1)
            for a in range(2):
                for hf in range(2):
                    m = small(PS[:, 2 * a + hf, 0:HALF], ones[:], lat_sum[:, a, hf * HALF:(hf + 1) * HALF], True, True)
                m.then_inc(mq_sum, 1)
            for a in range(2):
                m = small(PS[:, 6 + a, 0:HALF], swap_t[:], kpe[:, a * HALF:(a + 1) * HALF], True, True)
            m.then_inc(kp_swap, 1)
            pe.wait_ge(mq_var, 2)
            pe.wait_ge(mq_norm, 1)
            pe.wait_ge(kp_done, 1)

            pe.wait_ge(masks_ready, 1)
            with pe.Fori(0, HEADS // 2) as t:
                halves = [slice(0, HALF), slice(HALF, R)]
                pe.wait_ge(ml_w_in, 128 * t + 128)
                for k in range(3):
                    for hf in range(2):
                        for c in range(LT):
                            w = wq[:, k, c, :] if k < 2 else wr[:, c, :]
                            m = small(PS[:, 2 * k + hf, 0:HALF], w, cq[:, c, halves[hf]], c == 0, c == LT - 1)
                    m.then_inc(ml_item, 1)
                pe.wait_ge(mq_norm, 2)
                pe.wait_ge(ml_ev_d, 3 * t + 1)
                for s in range(2):
                    for c in range(LT):
                        m = small(PS[:, s, :], wk[:, s, c, :], ckT[:, c, 0:NP], c == 0, c == LT - 1)
                m.then_inc(ml_item, 1)
                pe.wait_ge(ml_ev_d, 3 * t + 2)
                pe.wait_ge(ml_fin, 2 * t + 1)
                for hf in range(2):
                    m = small(PS[:, 6 + hf, 0:HALF], swap_t[:], qpr[:, halves[hf]], True, True)
                m.then_inc(ml_swap, 1)
                pe.wait_ge(ml_ev_a, 3 * t + 1)
                for j in range(QT):
                    for c in range(LT):
                        m = small(PS[:, 2 + j // 2, 2 * P * (j % 2):2 * P * (j % 2) + 2 * P], ckT[:, c, j * P:(j + 1) * P],
                                  wv[:, c, :], c == 0, c == LT - 1)
                m.then_inc(ml_item, 1)
                for s in range(2):
                    for c in range(LT):
                        f = NS * (LT * s + c)
                        m = small(PS[:, 4, f:f + NS], wkT[:, s, c * P:(c + 1) * P], qn[:, s, NP:R], True, True)
                m.then_inc(ml_item, 1)

                def scores(u):
                    s, i = unit(u)
                    n, b = P * (i + 1), u % 4
                    if u >= 4:
                        pe.wait_ge(ml_exp, 8 * t + u - 3)
                    qs, e = slice(P * i, P * i + P), slice(DQK * s, DQK * s + DQK)
                    small(PS[:, b, 0:n], qn[:, s, qs], kn[:, s, 0:n], True, False)
                    small(PS[:, b, n - DQK:n], maskq_t[:], maskk_t[:], False, False)
                    small(PS[:, b, 0:n], qpe[e, qs], kpe[e, 0:n], False, True).then_inc(ml_score, 1)

                def turn(u):
                    i = unit(u)[1]
                    pe.wait_ge(ml_norm, 8 * t + u + 1)
                    if u >= 2:
                        pe.wait_ge(ml_ptev, 8 * t + u - 1)
                    for j in range(i + 1):
                        m = pe.transpose(PS[:, 4 + u % 2, j * P:(j + 1) * P], px[:, u % 3, j * P:(j + 1) * P], id_t[:])
                    m.then_inc(ml_tr, 1)

                def values(s):
                    pe.wait_ge(ml_ptev, 8 * t + 4 * s + 4)
                    for j in range(QT):
                        m = small(PS[:, 6 + s, P * j:NP], vb[:, j, s * P:(s + 1) * P], pt[:, s, j, P * j:NP],
                                  j == 0, j == QT - 1)
                    m.then_inc(ml_pv, 1)

                pe.wait_ge(ml_ev_a, 3 * t + 3)
                pe.wait_ge(ml_ev_d, 3 * t + 3)
                pe.wait_ge(ml_qpe, t + 1)
                for u in range(8 + LAG):
                    if u < 8:
                        scores(u)
                    if u >= LAG:
                        turn(u - LAG)
                    if u == QT + LAG:
                        values(0)
                values(1)

            pe.wait_ge(ml_fin, HEADS + 1)
            for c in range(LT):
                m = pe.transpose(PS[0:NS, 4, c * P:(c + 1) * P], ckT[:, c, NP:R], id_t[:])
            m.then_inc(mq_tr, 1)
            pe.wait_ge(ms_in, 32)
            SPLIT = HALF
            for g in range(2):
                heads = slice(4 * g, 4 * g + 4)
                old, new = slice(0, PAST - SPLIT), slice(PAST - SPLIT, SPLIT)
                for bank, cols, keys_c, keys_p in (
                        (2 * g, slice(0, SPLIT), lambda c: ccT[:, c, 0:SPLIT], kpc[:, 0:SPLIT]),
                        (2 * g + 1, old, lambda c: ccT[:, c, SPLIT:PAST], kpc[:, SPLIT:PAST]),
                        (2 * g + 1, new, lambda c: ckT[:, c, NP:R], kpe[:, NP:R])):
                    for c in range(LT):
                        small(PS[:, bank, cols], qls[:, c, heads, :].rearrange("p h r -> p (h r)"), keys_c(c), c == 0, False)
                    m = small(PS[:, bank, cols], qps[:, heads, :].rearrange("p h r -> p (h r)"), keys_p, False, True)
                m.then_inc(ms_score, 1)
            for g in range(2):
                pe.wait_ge(ms_norm, g + 1)
                pe.wait_ge(mq_ev, 1)
                for j in range(KTS):
                    nk = P if j < KTS - 1 else NS
                    dst = PS[0:nk, 4 + g, j * P:(j + 1) * P] if j < KTS - 1 else PS[0:nk, 6 + g, 0:P]
                    m = pe.transpose(dst, pxs[:, g, j * P:j * P + nk], id_t[:])
                m.then_inc(ms_tr, 1)
            for g in range(2):
                pe.wait_ge(ms_ptev, g + 1)
                for c in range(LT):
                    cs = slice(c * P, (c + 1) * P)
                    for j in range(KTS):
                        last = j == KTS - 1
                        m = small(PS[:, g, cs], ckR[0:NS, cs] if last else ccR[:, j, cs],
                                  pts[0:NS, g, j, :] if last else pts[:, g, j, :], j == 0, last)
                m.then_inc(ms_pv, 1)
            pe.wait_ge(ms_olev, 2)
            pe.wait_ge(ms_w_in, 16 * (HEADS + 1))
            for h in range(HEADS):
                for c in range(LT):
                    m = small(PS[:, 2, NS * h:NS * h + NS], wva[:, c, h * P:(h + 1) * P], ols[:, c, h, :], c == 0, c == LT - 1)
            m.then_inc(ms_ob, 1)
            pe.wait_ge(ms_fin, 1)

            with pe.Fori(0, HEADS // 2) as t:
                pe.wait_ge(df_vd_in, 32 * t + 32)
                pe.wait_ge(df_od, 3 * t + 1)
                for s in range(2):
                    if s:
                        pe.wait_ge(df_vrev, 2 * t + 1)
                    for j in range(KTS):
                        nk = P if j < KTS - 1 else NS
                        dst = PS[0:nk, 6, j * P:(j + 1) * P] if j < KTS - 1 else PS[0:nk, 7, 0:P]
                        m = pe.transpose(dst, vd[:, s, j * P:j * P + nk], id_t[:])
                    m.then_inc(df_vt, 1)
                pe.wait_ge(df_a_in, 96 * t + 96)

                def scores(u):
                    s, i = unit(u)
                    n = P * (i + 1)
                    if u >= 2:
                        pe.wait_ge(df_exp, 8 * t + u - 1)
                    for e in range(2):
                        b, es = 2 * (u % 2) + e, slice(DQK * e, DQK * e + DQK)
                        small(PS[:, b, 0:n], qd[es, s, P * i:P * i + P], kd[es, s, 0:n], True, False)
                        m = small(PS[:, b, n - DQK:n], maskq_t[:], maskk_t[:], False, True)
                    m.then_inc(df_score, 1)

                def turn(u):
                    i = unit(u)[1]
                    pe.wait_ge(df_norm, 8 * t + u + 1)
                    if u >= 2:
                        pe.wait_ge(df_ptev, 8 * t + u - 1)
                    for j in range(i + 1):
                        m = pe.transpose(PS[:, 4 + u % 2, j * P:(j + 1) * P], pxd[:, u % 3, 0, j * P:(j + 1) * P], id_t[:])
                    m.then_inc(df_tr, 1)

                def values(s):
                    if s == 0:
                        pe.wait_ge(df_vrev, 2 * t + 2)
                    pe.wait_ge(df_ptev, 8 * t + 4 * s + 4)
                    for j in range(QT):
                        m = small(PS[:, 6 + s, P * j:NP], vr[:, s, j, :], ptd[:, s, j, P * j:NP], j == 0, j == QT - 1)
                    m.then_inc(df_pv, 1)

                def sample_scores():
                    for s in range(2):
                        for e in range(2):
                            r, es = 32 * (2 * s + e), slice(DQK * e, DQK * e + DQK)
                            q = qd[es, s, NP:R]
                            small(PS[r:r + 32, 0, 0:HALF], q, kcs[es, s, 0:HALF], True, True)
                            small(PS[r:r + 32, 1, 0:PAST - HALF], q, kcs[es, s, HALF:PAST], True, True)
                            m = small(PS[r:r + 32, 1, PAST - HALF:HALF], q, kd[es, s, NP:R], True, True)
                    m.then_inc(dfs_score, 1)

                for u in range(8 + LAG):
                    if u < 8:
                        scores(u)
                    if u == 8:
                        pe.wait_ge(df_exp, 8 * t + 7)
                    if u >= LAG:
                        turn(u - LAG)
                    if u == 8:
                        sample_scores()
                    if u == QT + LAG:
                        values(0)
                values(1)
                pe.wait_ge(dfs_norm, t + 1)
                pe.wait_ge(df_ptev, 8 * t + 8)
                for j in range(KTS):
                    nk = P if j < KTS - 1 else NS
                    dst = PS[0:nk, 4, j * P:(j + 1) * P] if j < KTS - 1 else PS[0:nk, 5, 0:P]
                    m = pe.transpose(dst, pxds[:, j * P:j * P + nk], id_t[:])
                m.then_inc(dfs_tr, 1)
                pe.wait_ge(dfs_ptev, t + 1)
                pe.wait_ge(df_exp, 8 * t + 8)
                pe.wait_ge(df_v_in, 32 * t + 32)
                for s in range(2):
                    for j in range(KTS):
                        last = j == KTS - 1
                        m = small(PS[:, 2 + s, 0:NS], vr[0:NS, s, QT, :] if last else vcs[:, s, j, :],
                                  ptds[0:NS, j, s, :] if last else ptds[:, j, s, :], j == 0, last)
                m.then_inc(dfs_pv, 1)

            pe.wait_ge(df_od, 3 * (HEADS // 2) + 1)
            for h in range(HEADS):
                pe.wait_ge(df_sq, h + 1)
                for a in range(2):
                    m = small(PS[0:HEADS, 4 + a, 0:HALF], sel_col[:, h, :], sqd[:, h % 2, a * HALF:(a + 1) * HALF],
                              h == 0, h == HEADS - 1)
                m.then_inc(df_ssq, 1)
            big_wait(G_OUT)
            for k in range(HEADS, 2 * HEADS):
                tile_products(G_OUT % 2, k, k == HEADS, False)
            pe.wait_ge(df_rs, 1)
            pe.wait_ge(df_g_in, 32)
            for h in range(HEADS):
                b = 4 + 2 * (h % 2)
                if h >= 2:
                    pe.wait_ge(df_scaled, h - 1)
                for a in range(2):
                    m = small(PS[:, b + a, 0:HALF], sel_row[:, h, :], rs8[:, a * HALF:(a + 1) * HALF], True, True)
                m.then_inc(df_wide, 1)

            for k in range(HEADS):
                pe.wait_ge(df_fin, k + 1)
                m = tile_products(G_OUT % 2, k, False, k == HEADS - 1)
            m.then_inc(mm_done, 1)
            big_wait(G_OUT + 1)
            big_tile((G_OUT + 1) % 2)
            big_loop(G_OUT, 1, KT // 2)
            row_sums(1)
            for s in range(2):
                big_wait(G_PIN + s)
                big_tile((G_PIN + s) % 2, KT)
            big_loop(G_PIN, 1, KT)
            for g in range(4):
                slot = (G_GRP + g) % 2
                pe.wait_ge(split_ready, G_GRP + g - G_KPE + 2)
                d_hi, d_lo = d_halves[g]
                for n in range(4):
                    if g == 0 and n < 2:
                        pe.wait_ge(acc_free[n], turn_of(G_GRP + (G_GRP + n) % 2))
                    elif g:
                        pe.wait_ge(grp_y, 4 * (g - 1) + n + 1)
                    for k in range(4):
                        if n == 0:
                            pe.wait_ge(d_split, 4 * g + k + 1)
                        ks = slice(k * LORA + n * P, k * LORA + (n + 1) * P)
                        for i, (w, d) in enumerate(((w_hi, d_hi), (w_hi, d_lo), (w_lo, d_hi))):
                            for a in range(2):
                                m = small(PS[:, 2 * n + a, 0:HALF], w[:, slot, ks], d[:, k, a * HALF:(a + 1) * HALF],
                                          k == 0 and i == 0, k == 3 and i == 2)
                    m.then_inc(grp_mm, 1)
                pe.wait_ge(grp_mm, 4 * g + 4)
                pe.nop().then_inc(mm_done, 1)
            pe.wait_ge(grp_y, KT - 2)
            big_wait(G_POUT)
            for k in range(KT):
                pe.wait_ge(y_ready, k + 1)
                m = tile_products(G_POUT % 2, k, k == 0, k == KT - 1)
            m.then_inc(mm_done, 1)
            big_wait(G_POUT + 1)
            big_tile((G_POUT + 1) % 2)
            big_loop(G_POUT, 1, KT // 2)
            row_sums(2)

        def parts(ap_rows):
            return ((0, slice(0, HALF), slice(0, HALF), 0), (1, slice(0, NP - HALF), slice(HALF, NP), 0),
                    (1, slice(NP - HALF, HALF), slice(NP, R), 1))

        @block.scalar
        def _(act):
            act.wait_ge(cond_in, 16)
            act.activation(cond_t[:], cond_t[:], ACT.Silu).then_inc(cond_ready, 1)
            act.wait_ge(condb_in, 16)
            act.activation(cond_b[:], cond_b[:], ACT.Silu).then_inc(condb_ready, 1)

            def square(k, dst):
                act.activation(dst, at(x, k), ACT.Square).then_inc(sq_ready, 1)

            def root(n):
                act.activation(act_tmp[0:1, n + 2:n + 3], ones[0:1, 0:1], ACT.Sqrt)
                act.wait_ge(var_eps, n + 1)
                act.activation(rstd[:], rstd[:], ACT.Sqrt).then_inc(std_ready, 1)

            def affine0(q):
                act.wait_ge(mod_ready, q + 1)
                for k in range(4 * q, 4 * q + 4):
                    act.wait_ge(x_normed, k + 1)
                    for c, r in GROUP_ROWS:
                        ins = act.activation(x[:, k, r], x[:, k, r], ACT.Identity, scale=aff[:, c, k:k + 1])
                    ins.then_inc(xn_ready, 1)
                for k in range(4 * q, 4 * q + 4):
                    act.wait_ge(xn_ready, k + 1)
                    for c, r in GROUP_ROWS:
                        ins = act.activation(h_hi[:, k, r], x[:, k, r], ACT.Identity, bias=mod[:, c, k:k + 1])
                    ins.then_inc(hf_ready, 1)

            def affine1():
                with act.Fori(0, KT // 4) as t:
                    for s in range(4):
                        act.wait_ge(xn_ready, 4 * t + (KT + s + 1))
                        for c, r in GROUP_ROWS:
                            ins = act.activation(at(h_hi, 4 * t + s)[:, r], scaled_x[s][:, r], ACT.Identity,
                                                 bias=mod[:, c, bass.ds(4 * t + (3 * KT + s), 1)])
                        ins.then_inc(hf_ready, 1)

            act.wait_ge(ones_ready, 1)

            for c in range(CHUNKS):
                if c == CHUNKS - 1:
                    affine0(2)
                act.wait_ge(mm_done, 4 * c + 4)
                if c:
                    act.wait_ge(ada_turned, c)
                act.activation(stage[0:2, 1, 0:512], PS[0:2, 0, :], ACT.Copy).then_inc(ada_row, 1)
                for k in range(KT) if c == 0 else ():
                    if k == 0:
                        act.wait_ge(x_in, 16)
                    if k >= 2:
                        act.wait_ge(sq_added, k - 1)
                    act.activation((stage[:, 0], rstd[:])[k % 2], x[:, k], ACT.Square).then_inc(sq_ready, 1)
                if c == 1:
                    root(0)
                if c == 2:
                    affine0(0)
                    affine0(1)
            act.wait_ge(ada_row, CHUNKS)
            for s in range(2):
                act.activation(act_tmp[0:1, s:s + 1], stage[0:1, 1, 0:1], ACT.Copy).then_inc(acc_free[s], 1)

            affine0(CHUNKS - 1)
            act.wait_ge(lam_sum, 1)
            act.activation(lam_w[:, 2:4], lam_w[:, 0:2], ACT.Exp).then_inc(lam_exp, 1)
            act.wait_ge(mm_done, G_KPE + 1)
            act.activation(rows(kpe[:]), acc[G_KPE % 2], ACT.Copy).then_inc(acc_free[G_KPE % 2], 1)

            def load_ada(t, s, a):
                act.wait_ge(adr_used, 2 * t + (a + 1))
                act.dma_start(w_adr[:, a % 2], tile_of(wd2, s, t + (a // 2 + 1))).then_inc(adr_in[a % 2], 16)

            def store_loop(g0, first, end, func, out2, base, ada=None):
                with act.Fori(first, end) as t:
                    for s in range(2):
                        if ada is not None:
                            load_ada(t, s, ada + s)
                        slot = (g0 + s) % 2
                        act.wait_ge(mm_done, 2 * t + (g0 + s + 1))
                        act.activation(rows(stage[:, s]), acc[slot], func).then_inc(acc_free[slot], 1)
                        act.wait_ge(acc_free[slot], t + turn_of(g0 + s + 2))
                        act.dma_start(tile_of(out2, s, t), stage[:, s]).then_inc(stored[s], 16)
                    for s in range(2):
                        act.wait_ge(stored[s], 16 * t + (base + 16))

            store_loop(G_Z, 0, ZT // 2, ACT.Copy, z2, 0, ADA_P0)
            store_loop(G_GATE, 0, GT // 2 - 1, ACT.Silu, g2, 16 * ZT // 2, ADA_P0 + ZT)
            store_loop(G_GATE, GT // 2 - 1, GT // 2, ACT.Silu, g2, 16 * ZT // 2)

            act.wait_ge(mq_in, 64)
            for a in range(2):
                act.wait_ge(mq_var, a + 1)
                act.activation(lat_r[a][:], lat_r[a][:], ACT.Sqrt).then_inc(mq_std, 1)
            act.wait_ge(mq_norm, 2)
            act.dma_start(ckv_out.rearrange("t p r -> p t r"), ckT[:]).then_inc(latent_out, 16)
            act.wait_ge(kp_done, 1)
            act.dma_start(kpe_out, kpe[0:DQK, :]).then_inc(latent_out, 16)
            with act.Fori(0, HEADS // 2) as t:
                act.wait_ge(ml_item, 6 * t + 2)
                act.activation(rows(qn[:, 1]), PS[:, 2:4, 0:HALF], ACT.Copy).then_inc(ml_ev_a, 1)
                act.wait_ge(ml_item, 6 * t + 4)
                act.activation(kn[:], PS[:, 0:2, :], ACT.Copy).then_inc(ml_ev_a, 1)
                act.wait_ge(ml_item, 6 * t + 5)
                act.activation(vb[:].rearrange("p (a j) e -> p a (j e)", a=2), PS[:, 2:4, :], ACT.Copy).then_inc(ml_ev_a, 1)
                for u in range(8):
                    n = P * (unit(u)[1] + 1)
                    if u >= 3:
                        act.wait_ge(ml_tr, 8 * t + u - 2)
                    act.wait_ge(ml_max, 8 * t + u + 1)
                    act.activation(px[:, u % 3, 0:n], PS[:, u % 4, 0:n], ACT.Exp, bias=st[:, 1, u:u + 1],
                                   scale=MLA_SCALE, accum_out=st[:, 2, u:u + 1]).then_inc(ml_exp, 1)

            act.wait_ge(mq_tr, 1)
            act.activation(ckR[0:NS, :], PS[0:NS, 4, :], ACT.Copy).then_inc(mq_ev, 1)
            for g in range(2):
                act.wait_ge(ms_max, g + 1)
                act.activation(rows(pxs[:, g]), PS[:, 2 * g:2 * g + 2, 0:HALF], ACT.Exp, bias=sts[:, g, 1:2],
                               scale=MLA_SCALE, accum_out=sts[:, g, 2:3]).then_inc(ms_exp, 1)
            for g in range(2):
                act.wait_ge(ms_pv, g + 1)
                act.activation(ols[:, :, 4 * g:4 * g + 4, :].rearrange("p c h r -> p c (h r)"),
                               PS[:, g, :].rearrange("p (c n) -> p c n", c=LT), ACT.Copy).then_inc(ms_olev, 1)

            with act.Fori(0, HEADS // 2) as t:
                for s in range(2):
                    act.wait_ge(df_vt, 2 * t + s + 1)
                    act.activation(vr[:, s, 0:QT, :].rearrange("p j e -> p (j e)"), PS[:, 6, :], ACT.Copy)
                    act.activation(vr[0:NS, s, QT, :], PS[0:NS, 7, 0:P], ACT.Copy).then_inc(df_vrev, 1)
                for u in range(8):
                    n, slot = P * (unit(u)[1] + 1), u % 3
                    if u >= 3:
                        act.wait_ge(df_tr, 8 * t + u - 2)
                    act.wait_ge(df_max, 8 * t + u + 1)
                    for e in range(2):
                        ins = act.activation(pxd[:, slot, e, 0:n], PS[:, 2 * (u % 2) + e, 0:n], ACT.Exp,
                                             bias=std[:, u, 2 + e:3 + e], scale=DIFF_SCALE,
                                             accum_out=std[:, u, 4 + e:5 + e])
                    ins.then_inc(df_exp, 1)
                act.wait_ge(dfs_max, t + 1)
                act.activation(rows(pxds[:]), PS[:, 0:2, 0:HALF], ACT.Exp, bias=std[:, 8, 1:2],
                               scale=DIFF_SCALE, accum_out=std[:, 8, 2:3]).then_inc(dfs_exp, 1)
                act.wait_ge(df_pv, 2 * t + 1)
                act.activation(at(od, 2 * t)[:, 0:NP], PS[:, 6, :], ACT.Copy).then_inc(df_od, 1)
                act.wait_ge(df_pv, 2 * t + 2)
                act.activation(at(od, 2 * t + 1)[:, 0:NP], PS[:, 7, :], ACT.Copy).then_inc(df_od, 1)
                act.wait_ge(dfs_pv, t + 1)
                act.activation(od[:, bass.ds(2 * t, 2), NP:R], PS[:, 2:4, 0:NS], ACT.Copy).then_inc(df_od, 1)
            act.wait_ge(df_od, 3 * (HEADS // 2) + 1)
            for h in range(HEADS):
                if h >= 2:
                    act.wait_ge(df_ssq, h - 1)
                act.activation(sqd[:, h % 2], od[:, h], ACT.Square).then_inc(df_sq, 1)
            act.wait_ge(df_var, 1)
            act.activation(rs8[:], rs8[:], ACT.Sqrt).then_inc(df_std, 1)
            for h in range(HEADS):
                act.wait_ge(df_scaled, h + 1)
                act.activation(h_hi[:, h], od[:, h], ACT.Copy).then_inc(df_upper, 1)

            act.wait_ge(condb_in, 32)
            act.activation(cond_b[:], cond_b[:], ACT.Silu).then_inc(condb_ready, 1)

            def gated(t, g0, n, gate_tile, ada=None):
                for s in range(2):
                    if ada is not None:
                        load_ada(t, s, ada + s)
                    slot = (g0 + s) % 2
                    act.wait_ge(mm_done, 2 * t + (g0 + s + 1))
                    act.wait_ge(sq_added, 2 * t + (KT * n + s - 1))
                    for bank, cols, r, c in parts(R):
                        ins = act.activation(stage[:, s, r], PS[:, 2 * slot + bank, cols], ACT.Identity,
                                             scale=mod[:, c, bass.ds(2 * t + (gate_tile + s), 1)])
                    ins.then_inc(acc_free[slot], 1)
                    act.wait_ge(x_new, 2 * t + (KT * (n - 1) + s + 1))
                    square(2 * t + s, stage[:, s])

            with act.Fori(0, KT // 2 - 1) as t:
                gated(t, G_OUT, 1, 2 * KT, ADA_P0 + ADA_P1)
            with act.Fori(KT // 2 - 1, KT // 2) as t:
                gated(t, G_OUT, 1, 2 * KT)
            root(1)
            affine1()

            act.wait_ge(pad_zero, 1)
            def u_and_gate(t, last):
                us, gs = G_PIN % 2, (G_PIN + 1) % 2
                act.activation(u_ext[:, PAD + NP:2 * PAD + NP], at(pool_pre, t), ACT.Copy)
                act.wait_ge(mm_done, 2 * t + (G_PIN + 1))
                for bank, cols, r, c in parts(R):
                    off = PAD + r.start + PAD * c
                    ins = act.activation(u_ext[:, off:off + r.stop - r.start], PS[:, 2 * us + bank, cols], ACT.Copy)
                ins.then_inc(acc_free[us], 1)
                act.wait_ge(d_ready, t + 1)
                act.dma_start(d_scr[bass.ds(t, 1)].rearrange("t p r -> p (t r)"), d_st[:]).then_inc(d_stored, 16)
                act.wait_ge(mm_done, 2 * t + (G_PIN + 2))
                act.activation(rows(stage[:, 1]), acc[gs], ACT.Silu).then_inc(acc_free[gs], 1)
                act.wait_ge(acc_free[gs], t + turn_of(G_PIN + 3))
                act.dma_start(pg_scr[bass.ds(t, 1)].rearrange("t p r -> p (t r)"), stage[:, 1]).then_inc(pg_stored, 16)
                if not last:
                    act.wait_ge(pg_stored, 16 * t + 16)

            with act.Fori(0, KT - 1) as t:
                u_and_gate(t, False)
            with act.Fori(KT - 1, KT) as t:
                u_and_gate(t, True)

            act.wait_ge(mm_done, G_GRP)

            def upper_d(g):
                act.wait_ge(grp_in, 16 * g + 16)
                for k in range(4):
                    act.activation(d_halves[g][0][:, k], d_raw[:, k], ACT.Copy).then_inc(d_upper, 1)

            upper_d(0)
            act.dma_start(pool_out, pool_last[:]).then_inc(out_done, 16)
            for q in range(KT):
                act.wait_ge(grp_y, q + 1)
                act.activation(h_hi[:, q], stage[:, q % 2], ACT.Copy).then_inc(y_upper, 1)
                if q % 4 == 0 and q < KT - 4:
                    upper_d(q // 4 + 1)

            with act.Fori(0, KT // 2) as t:
                gated(t, G_POUT, 2, 5 * KT)
            root(2)

        @block.vector
        def _(dve):
            dve.memset(ssq[:], 0.0).then_inc(split_ready, 1)
            dve.wait_ge(split_ready, 1)

            def row_scale(n):
                dve.wait_ge(var_ready, n + 1)
                sums = PS[:, 6:8, 0:HALF] if n else PS[:, 2:4, 0:HALF]
                dve.tensor_scalar(rows(rstd[:]), sums, 1.0 / D, EPS, ALU.mult, ALU.add).then_inc(var_eps, 1)
                if n < 2:
                    dve.memset(ssq[:], 0.0).then_inc(ssq_zero, 1)
                    dve.wait_ge(ssq_zero, n + 1)
                dve.wait_ge(std_ready, n + 1)
                vchain(dve, dve.reciprocal(rstd[:], rstd[:]))

            def add_bias(a, b):
                for c in range(2):
                    ins = dve.tensor_tensor(mod[:, c, a:b], mod[:, c, a:b], bada_t[:, a:b], ALU.add)
                vchain(dve, ins)

            def fold_scale(n, k0=0, k1=KT):
                a = (3 * n + 1) * KT
                for c in range(2):
                    ins = dve.scalar_tensor_tensor(out=aff[:, c, k0:k1], in0=mod[:, c, a + k0:a + k1], scalar=1.0,
                                                   in1=gnorm_t[:, n, k0:k1], op0=ALU.add, op1=ALU.mult)
                vchain(dve, ins)

            def split(g, t2=0, t=0):
                slot = g % 2
                dve.wait_ge(raw_in[slot], 16 * t + 16 * (g // 2 + 1 - ADA_PE // 2))
                dve.wait_ge(mm_done, t2 + (g - 1))
                vchain(dve, dve.tensor_copy(w_hi[:, slot], w_raw[:, slot]))
                dve.tensor_tensor(w_lo[:, slot], w_raw[:, slot], w_hi[:, slot].bitcast(F32),
                                  ALU.subtract).then_inc(split_ready, 1)

            def make_h1():
                with dve.Fori(0, KT // 4) as t:
                    dve.wait_ge(h_ready, 4 * t + (KT + 2))

                    def scaled(s):
                        for c, r in GROUP_ROWS:
                            ins = dve.scalar_tensor_tensor(out=scaled_x[s][:, r], in0=at(x, 4 * t + s)[:, r],
                                                           scalar=aff[:, c, bass.ds(4 * t + s, 1)], in1=rstd[:, r],
                                                           op0=ALU.mult, op1=ALU.mult)
                        ins.then_inc(xn_ready, 1)

                    def lower(s):
                        dve.wait_ge(hf_ready, 4 * t + (KT + s + 1))
                        for c, r in GROUP_ROWS:
                            ins = dve.scalar_tensor_tensor(out=at(h_lo, 4 * t + s)[:, r], in0=scaled_x[s][:, r],
                                                           scalar=mod[:, c, bass.ds(4 * t + (3 * KT + s), 1)],
                                                           in1=at(h_hi, 4 * t + s)[:, r].bitcast(F32),
                                                           op0=ALU.add, op1=ALU.subtract)
                        ins.then_inc(h_ready, 1)

                    for s in range(3):
                        scaled(s)
                    lower(0)
                    scaled(3)
                    for s in range(1, 4):
                        lower(s)
                dve.wait_ge(h_ready, 2 * KT + 2)

            def ada_tile(a, t2, t):
                slot = a % 2
                dve.wait_ge(adr_in[slot], 16 * t + 16 * (a // 2 + 1))
                for c in range(2):
                    ins = dve.tensor_tensor_reduce(ada_junk, w_adr[:, slot], cond_b[:, c, :], 1.0, 0.0, ALU.mult, ALU.add,
                                                   ada_acc[:, c:c + 1])
                    if c == 0:
                        vchain(dve, ins)
                ins.then_inc(adr_used, 1)
                dve.wait_ge(adr_used, t2 + a + 1)
                vchain(dve, dve.tensor_copy(mod[:, :, bass.ds(t2 + (ADA_PE + a), 1)].rearrange("p c k -> p (c k)"),
                                            ada_acc[:]))

            dve.memset(maskq_t[:, 0:DQK], 1.0)
            dve.memset(maskq_t[:, DQK:P], 0.0)
            dve.memset(maskk_t[:], MASKED).then_inc(masks_ready, 1)
            dve.wait_ge(condb_ready, 1)
            for i in range(2):
                dve.memset(ada_acc[:, i:i + 1], 0.0).then_inc(h_ready, 1)
            dve.wait_ge(h_ready, 2)

            def shifts(q):
                dve.wait_ge(ada_turned, q + 1)
                ks = slice(4 * q, 4 * q + 4)
                turned = PS[:, 1, 8 * q:8 * q + 8].rearrange("p (t c) -> p c t", c=2)
                for c in range(2):
                    ins = dve.tensor_tensor(mod[:, c, ks], turned[:, c, :], bada_t[:, ks], ALU.add)
                vchain(dve, ins)
                dve.memset(ada_acc[:, 0:1], 0.0).then_inc(mod_ready, 1)
                dve.wait_ge(mod_ready, q + 1)

            for a in range(ADA_P0):
                ada_tile(a, 0, 0)
                if a == NORM_AT:
                    row_scale(0)
                    dve.memset(ada_acc[:, 0:1], 0.0).then_inc(rstd_ready, 1)
                    dve.wait_ge(rstd_ready, 1)
                if a == 3:
                    dve.wait_ge(consts_in, CONSTS)
                if a % 4 == 3:
                    add_bias(ADA_PE + a - 3, ADA_PE + a + 1)
                    fold_scale(0, a - 3, a + 1)
                if a % 4 == 1 and a > 4:
                    shifts(a // 4 - 1)
                if a == ADA_P0 - 2:
                    for k in range(3):
                        lower_h0(dve, k)
            shifts(CHUNKS - 1)
            dve.wait_ge(mm_done, ADA_PE)
            split(G_KPE)
            for k in range(3, KT):
                lower_h0(dve, k)
            for i in range(2):
                ins = dve.tensor_tensor_reduce(lam_in[:, 2 * i, :], lam_in[:, 2 * i, :], lam_in[:, 2 * i + 1, :], 1.0, 0.0,
                                               ALU.mult, ALU.add, lam_w[:, i:i + 1])
            ins.then_inc(lam_sum, 1)
            dve.wait_ge(lam_exp, 1)
            vchain(dve, dve.tensor_tensor(lam_w[:, 4:5], lam_w[:, 3:4], lam_w[:, 2:3], ALU.subtract))
            vchain(dve, dve.tensor_scalar(neg_lam, lam_w[:, 4:5], -LAM_INIT, None, ALU.add))
            vchain(dve, dve.scalar_tensor_tensor(out=coef, in0=lamsel_t[:, 1:2], scalar=neg_lam, in1=lamsel_t[:, 0:1],
                                                 op0=ALU.mult, op1=ALU.add))
            vchain(dve, dve.tensor_scalar(gsub_v, gsub_v, 1.0 - LAM_INIT, None, ALU.mult))

            with dve.Fori(0, ZT // 2) as t:
                dv.loop(t, 6)
                for s in range(2):
                    split(G_Z + s, 2 * t, t)
                    ada_tile(ADA_P0 + s, 2 * t, t)
            dv.end(ZT // 2)
            with dve.Fori(0, GT // 2) as t:
                dv.loop(t, 6)
                for s in range(2):
                    split(G_GATE + s, 2 * t, t)
                    ada_tile(ADA_P0 + ZT + s, 2 * t, t)
            dv.end(GT // 2)
            add_bias(ADA_PE + ADA_P0, ADA_PE + ADA_P0 + ADA_P1)

            dve.wait_ge(mm_done, G_OUT)
            for s in range(2):
                dve.wait_ge(acc_free[s], turn_of(G_OUT + (G_OUT + s) % 2))
            dve.wait_ge(stored[0], 16 * (ZT + GT) // 2)
            dve.wait_ge(stored[1], 16 * (ZT + GT) // 2)
            dve.memset(lam_in[:, 0, 0:1], 0.0).then_inc(qps_free, 1)
            for a in range(2):
                dve.wait_ge(mq_sum, a + 1)
                dve.tensor_scalar(rows(lat_r[a][:]), PS[:, 2 * a:2 * a + 2, 0:HALF], 1.0 / LORA, EPS, ALU.mult,
                                  ALU.add).then_inc(mq_var, 1)
            dve.wait_ge(kp_swap, 1)
            dve.tensor_tensor(rows(qpr[:]), PS[:, 6:8, 0:HALF], rows(sin_t[:]), ALU.mult)
            vchain(dve, dve.tensor_tensor(kpe[:], kpe[:], cos_t[:], ALU.mult))
            dve.tensor_tensor(kpe[:], kpe[:], qpr[:], ALU.add).then_inc(kp_done, 1)
            for a, (lat, g_v) in enumerate(((cq, gqa_v), (ckT, gkva_v))):
                dve.wait_ge(mq_std, a + 1)
                vchain(dve, dve.reciprocal(lat_r[a][:], lat_r[a][:]))
                for c in range(LT):
                    ins = dve.scalar_tensor_tensor(out=lat[:, c, :], in0=lat[:, c, :], scalar=g_v[:, c:c + 1],
                                                   in1=lat_r[a][:], op0=ALU.mult, op1=ALU.mult)
                ins.then_inc(mq_norm, 1)

            def halves_of_h(src, hi, lo, done):
                vchain(dve, dve.tensor_copy(hi, src))
                dve.tensor_tensor(lo, src, hi.bitcast(F32), ALU.subtract).then_inc(done, 1)

            dve.wait_ge(qps_zero, 1)
            dve.wait_ge(mq_norm, 2)
            dve.memset(lam_in[:, 0, 0:1], 0.0).then_inc(ml_fin, 1)
            with dve.Fori(0, HEADS // 2) as t:
                dv.loop(t, 1 + 8 * 2 + 2 * 2)
                dve.wait_ge(ml_item, 6 * t + 1)
                dve.tensor_copy(rows(qn[:, 0]), PS[:, 0:2, 0:HALF]).then_inc(ml_ev_d, 1)
                dve.wait_ge(ml_item, 6 * t + 3)
                dve.tensor_copy(rows(qpr[:]), PS[:, 4:6, 0:HALF]).then_inc(ml_ev_d, 1)
                dve.wait_ge(ml_ev_d, 3 * t + 2)
                dve.tensor_tensor(qpe[:], qpr[:], cos_t[:], ALU.mult)
                dve.wait_ge(ml_swap, t + 1)
                vchain(dve, dve.tensor_tensor(rows(qsin[:]), PS[:, 6:8, 0:HALF], rows(sin_t[:]), ALU.mult))
                dve.tensor_tensor(qpe[:], qpe[:], qsin[:], ALU.add).then_inc(ml_qpe, 1)
                dve.wait_ge(ml_item, 6 * t + 6)
                dve.tensor_copy(qls[:, :, bass.ds(2 * t, 2), :].rearrange("p c h r -> p h c r"),
                                PS[:, 4, 0:2 * LT * NS].rearrange("p (h c r) -> p h c r", h=2, c=LT)).then_inc(ml_ev_d, 1)
                dve.wait_ge(ml_qpe, t + 1)
                for s in range(2):
                    e = slice(DQK * s, DQK * s + DQK)
                    dve.tensor_copy(qps[e, bass.ds(2 * t + s, 1), :].rearrange("p h r -> p (h r)"), qpe[e, NP:R])

                def maxima(u):
                    n = P * (unit(u)[1] + 1)
                    dve.wait_ge(ml_score, 8 * t + u + 1)
                    vchain(dve, dve.tensor_reduce(st[:, 0, u:u + 1], PS[:, u % 4, 0:n], AX.X, ALU.max))
                    dve.tensor_scalar(st[:, 1, u:u + 1], st[:, 0, u:u + 1], -MLA_SCALE, None, ALU.mult).then_inc(ml_max, 1)

                def normalise(u):
                    n = P * (unit(u)[1] + 1)
                    dve.wait_ge(ml_exp, 8 * t + u + 1)
                    vchain(dve, dve.reciprocal(st[:, 3, u:u + 1], st[:, 2, u:u + 1]))
                    dve.tensor_scalar(px[:, u % 3, 0:n], px[:, u % 3, 0:n], st[:, 3, u:u + 1], None,
                                      ALU.mult).then_inc(ml_norm, 1)

                def turned_out(u):
                    i = unit(u)[1]
                    dve.wait_ge(ml_tr, 8 * t + u + 1)
                    dve.tensor_copy(pt[:, unit(u)[0], 0:i + 1, P * i:P * i + P],
                                    PS[:, 4 + u % 2, 0:P * (i + 1)].rearrange("p (j q) -> p j q", q=P)).then_inc(ml_ptev, 1)

                def finish(s):
                    dve.wait_ge(ml_pv, 2 * t + s + 1)
                    dve.wait_ge(ml_v_in, 32 * t + 32)
                    if s:
                        dve.wait_ge(ml_fin, 2 * t + 2)
                    vchain(dve, dve.tensor_tensor(fo[:], PS[:, 6 + s, :], sg[:, s, 0:NP], ALU.mult))
                    hi, lo = (at(h, 2 * t + (HEADS + s))[:, 0:NP] for h in (h_hi, h_lo))
                    halves_of_h(fo[:], hi, lo, ml_fin)

                for u in range(8 + LAG):
                    if u < 8:
                        maxima(u)
                    if 1 <= u < 9:
                        normalise(u - 1)
                    if u >= LAG:
                        turned_out(u - LAG)
                    if u == QT + LAG + 1:
                        finish(0)
                finish(1)
                dve.wait_ge(ml_fin, 2 * t + 3)
            dv.end(HEADS // 2)

            for g in range(2):
                dve.wait_ge(ms_score, g + 1)
                vchain(dve, dve.tensor_reduce(sts[:, g, 0:1], PS[:, 2 * g:2 * g + 2, 0:HALF], AX.XY, ALU.max))
                dve.tensor_scalar(sts[:, g, 1:2], sts[:, g, 0:1], -MLA_SCALE, None, ALU.mult).then_inc(ms_max, 1)
            for g in range(2):
                dve.wait_ge(ms_exp, g + 1)
                vchain(dve, dve.reciprocal(sts[:, g, 3:4], sts[:, g, 2:3]))
                dve.tensor_scalar(pxs[:, g], pxs[:, g], sts[:, g, 3:4], None, ALU.mult).then_inc(ms_norm, 1)
            for g in range(2):
                dve.wait_ge(ms_tr, g + 1)
                dve.tensor_copy(pts[:, g, 0:KTS - 1, :].rearrange("p j q -> p (j q)"), PS[:, 4 + g, :])
                dve.tensor_copy(pts[0:NS, g, KTS - 1, :], PS[0:NS, 6 + g, 0:P]).then_inc(ms_ptev, 1)
            dve.wait_ge(ms_ob, 1)
            vchain(dve, dve.tensor_tensor(ofs[:], PS[:, 2, 0:HEADS * NS].rearrange("p (h r) -> p h r", r=NS), sgs[:], ALU.mult))
            halves_of_h(ofs[:], h_hi[:, HEADS:2 * HEADS, NP:R], h_lo[:, HEADS:2 * HEADS, NP:R], ms_fin)

            dve.memset(lam_in[:, 0, 0:1], 0.0).then_inc(df_od, 1)
            with dve.Fori(0, HEADS // 2) as t:
                dv.loop(t, 8 * 5 + 4)

                def maxima(u):
                    n, b = P * (unit(u)[1] + 1), 2 * (u % 2)
                    dve.wait_ge(df_score, 8 * t + u + 1)
                    vchain(dve, dve.tensor_reduce(std[:, u, 0:2], PS[:, b:b + 2, 0:n], AX.X, ALU.max))
                    dve.tensor_scalar(std[:, u, 2:4], std[:, u, 0:2], -DIFF_SCALE, None, ALU.mult).then_inc(df_max, 1)

                def combine(u):
                    n, slot = P * (unit(u)[1] + 1), u % 3
                    dve.wait_ge(df_exp, 8 * t + u + 1)
                    vchain(dve, dve.reciprocal(std[:, u, 6:8], std[:, u, 4:6]))
                    vchain(dve, dve.tensor_scalar(std[:, u, 0:1], std[:, u, 7:8], neg_lam, None, ALU.mult))
                    vchain(dve, dve.tensor_scalar(pxd[:, slot, 1, 0:n], pxd[:, slot, 1, 0:n], std[:, u, 0:1], None, ALU.mult))
                    vchain(dve, dve.scalar_tensor_tensor(out=pxd[:, slot, 0, 0:n], in0=pxd[:, slot, 0, 0:n],
                                                         scalar=std[:, u, 6:7], in1=pxd[:, slot, 1, 0:n],
                                                         op0=ALU.mult, op1=ALU.add))
                    dve.memset(lam_in[:, 0, 0:1], 0.0).then_inc(df_norm, 1)

                def turned_out(u):
                    s, i = unit(u)
                    dve.wait_ge(df_tr, 8 * t + u + 1)
                    dve.tensor_copy(ptd[:, s, 0:i + 1, P * i:P * i + P],
                                    PS[:, 4 + u % 2, 0:P * (i + 1)].rearrange("p (j q) -> p j q", q=P)).then_inc(df_ptev, 1)

                for u in range(8 + LAG):
                    if u < 8:
                        maxima(u)
                    if u == 8:
                        dve.wait_ge(dfs_score, t + 1)
                        vchain(dve, dve.tensor_reduce(std[:, 8, 0:1], PS[:, 0:2, 0:HALF], AX.XY, ALU.max))
                        dve.tensor_scalar(std[:, 8, 1:2], std[:, 8, 0:1], -DIFF_SCALE, None, ALU.mult).then_inc(dfs_max, 1)
                    if 1 <= u < 9:
                        combine(u - 1)
                    if u >= LAG:
                        turned_out(u - LAG)
                dve.wait_ge(dfs_exp, t + 1)
                vchain(dve, dve.reciprocal(std[:, 8, 3:4], std[:, 8, 2:3]))
                vchain(dve, dve.tensor_scalar(std[:, 8, 4:5], std[:, 8, 3:4], coef, None, ALU.mult))
                vchain(dve, dve.tensor_scalar(pxds[:], pxds[:], std[:, 8, 4:5], None, ALU.mult))
                dve.memset(lam_in[:, 0, 0:1], 0.0).then_inc(dfs_norm, 1)
                dve.wait_ge(dfs_tr, t + 1)
                most = PS[:, 4, :].rearrange("p (j s e r) -> p j s e r", j=KTS - 1, s=2, e=2)
                rest = PS[0:NS, 5, 0:P].rearrange("p (s e r) -> p s e r", s=2, e=2)
                dve.tensor_copy(ptd1[:, 0:KTS - 1], most[:, :, :, 1, :])
                dve.tensor_copy(ptd1[0:NS, KTS - 1], rest[:, :, 1, :]).then_inc(df_tmp, 1)
                dve.wait_ge(df_tmp, t + 1)
                dve.tensor_tensor(ptds[:, 0:KTS - 1], most[:, :, :, 0, :], ptd1[:, 0:KTS - 1], ALU.add)
                dve.tensor_tensor(ptds[0:NS, KTS - 1], rest[:, :, 0, :], ptd1[0:NS, KTS - 1], ALU.add).then_inc(dfs_ptev, 1)
                dve.wait_ge(dfs_ptev, t + 1)
            dv.end(HEADS // 2)

            dve.wait_ge(dfs_pv, HEADS // 2)
            split(G_OUT)
            dve.wait_ge(df_g_in, 32)
            for h in range(HEADS):
                dve.wait_ge(df_sq, h + 1)
                ins = dve.scalar_tensor_tensor(out=od[:, h], in0=od[:, h], scalar=gsub_v, in1=sgd[:, h],
                                               op0=ALU.mult, op1=ALU.mult)
            vchain(dve, ins)
            dve.wait_ge(df_ssq, HEADS)
            dve.tensor_scalar(rows(rs8[:]), PS[0:HEADS, 4:6, 0:HALF], 1.0 / P, SUB_EPS, ALU.mult, ALU.add).then_inc(df_var, 1)
            dve.wait_ge(df_std, 1)
            dve.reciprocal(rs8[:], rs8[:]).then_inc(df_rs, 1)
            for h in range(HEADS + 1):
                if h < HEADS:
                    b = 4 + 2 * (h % 2)
                    dve.wait_ge(df_wide, h + 1)
                    dve.tensor_tensor(rows(od[:, h]), PS[:, b:b + 2, 0:HALF], rows(od[:, h]), ALU.mult).then_inc(df_scaled, 1)
                if h:
                    dve.wait_ge(df_upper, h)
                    dve.tensor_tensor(h_lo[:, h - 1], od[:, h - 1], h_hi[:, h - 1].bitcast(F32),
                                      ALU.subtract).then_inc(df_fin, 1)

            def update(g, t2, t, n, k, slot):
                dve.wait_ge(acc_free[g % 2], t + turn_of(g + 2))
                dve.tensor_tensor(at(x, t2 + k), at(x, t2 + k), stage[:, slot], ALU.add).then_inc(x_new, 1)

            split(G_OUT + 1)
            split(G_OUT + 2)
            dve.wait_ge(condb_ready, 2)
            dve.wait_ge(x_in, 32)
            for s in range(2):
                if s:
                    split(G_OUT + 3)
                ada_tile(ADA_P0 + ADA_P1 + s, 0, 0)
                update(G_OUT + s, 0, 0, 1, s, s)
            dve.wait_ge(x_rest_in, 16)
            with dve.Fori(1, KT // 2 - 1) as t:
                dv.loop(t - 1, 6)
                for s in range(2):
                    ada_tile(ADA_P0 + ADA_P1 + s, 2 * t, t)
                    update(G_OUT + s, 2 * t, t, 1, s, s)
                    split(G_OUT + s + 2, 2 * t, t)
            dv.end(KT // 2 - 2)
            for k in range(KT - 2, KT):
                ada_tile(ADA_P0 + ADA_P1 + k, 0, 0)
                update(G_OUT + k, 0, 0, 1, k, k % 2)
                if k == KT - 2:
                    split(G_PIN)
            add_bias(ADA_PE + ADA_P0 + ADA_P1, ADA_T)
            dve.memset(lam_in[:, 0, 0:1], 0.0).then_inc(pad_free, 1)
            fold_scale(1)
            row_scale(1)
            make_h1()

            us = G_PIN % 2
            first, samp = slice(PAD, PAD + NP), slice(2 * PAD + NP, 2 * PAD + R)
            for grp, w in enumerate(WIN):
                with dve.Fori(4 * grp, 4 * grp + 4) as t:
                    t0 = t - 4 * grp
                    dv.loop(t0, 2 + grp + 1 + 1 + 1)
                    dve_t2 = 2 * t
                    split(G_PIN + 1, dve_t2, t)
                    dve.wait_ge(acc_free[us], t + turn_of(G_PIN + 2))
                    width = 2 * PAD + R
                    src = u_ext
                    for step, dst in zip(range(grp + 1), (w2, w4, w2, w4)):
                        lag = 1 << step
                        lo = 2 * lag - 1
                        vchain(dve, dve.tensor_tensor(dst[:, lo:width], src[:, lo:width], src[:, lo - lag:width - lag], ALU.add))
                        src = dst
                    dve.scalar_tensor_tensor(out=d_st[:, NP:R], in0=src[:, samp], scalar=1.0 / w, in1=u_ext[:, samp],
                                             op0=ALU.mult, op1=ALU.subtract)
                    dve.tensor_tensor(fix[:], src[:, PAD:PAD + 16], rcount_t[:, grp, :], ALU.mult)
                    vchain(dve, dve.scalar_tensor_tensor(out=d_st[:, 0:NP], in0=src[:, first], scalar=1.0 / w,
                                                         in1=u_ext[:, first], op0=ALU.mult, op1=ALU.subtract))
                    dve.tensor_tensor(d_st[:, 0:16], fix[:], u_ext[:, PAD:PAD + 16], ALU.subtract)
                    last = pool_last[:, bass.ds(t, 1), :, :].rearrange("p t a k -> p (t a) k")
                    dve.tensor_copy(last[:, 0, :], u_ext[:, NP:PAD + NP])
                    vchain(dve, dve.tensor_copy(last[:, 1, :], u_ext[:, PAD + R:2 * PAD + R]))
                    dve.memset(lam_in[:, 0, 0:1], 0.0).then_inc(d_ready, 1)
                    split(G_PIN + 2, dve_t2, t)
                    dve.wait_ge(d_stored, 16 * t + 16)
                dv.end(4)

            def lower_d(g):
                for k in range(4):
                    dve.wait_ge(d_upper, 4 * g + k + 1)
                    dve.tensor_tensor(d_halves[g][1][:, k], d_raw[:, k], d_halves[g][0][:, k].bitcast(F32),
                                      ALU.subtract).then_inc(d_split, 1)

            def group_out(q):
                n = q % 4
                if q < KT:
                    dve.wait_ge(pg_in[n], 16 * (q // 4 + 1))
                    dve.wait_ge(grp_mm, q + 1)
                    if q >= 2:
                        dve.wait_ge(y_ready, q - 1)
                    dve.scalar_tensor_tensor(out=rows(stage[:, q % 2]), in0=PS[:, 2 * n:2 * n + 2, 0:HALF],
                                             scalar=scale_v[:, q:q + 1], in1=rows(pg[:, n]),
                                             op0=ALU.mult, op1=ALU.mult).then_inc(grp_y, 1)
                if q:
                    dve.wait_ge(y_upper, q)
                    dve.tensor_tensor(h_lo[:, q - 1], stage[:, (q - 1) % 2], h_hi[:, q - 1].bitcast(F32),
                                      ALU.subtract).then_inc(y_ready, 1)

            dve.wait_ge(mm_done, G_GRP)
            lower_d(0)
            dve.wait_ge(pg_stored, 16 * KT)
            for g in range(4):
                split(G_GRP + g + 1)
                group_out(4 * g)
                if g < 3:
                    lower_d(g + 1)
                for n in range(1, 4):
                    group_out(4 * g + n)
                dve.memset(lam_in[:, 0, 0:1], 0.0).then_inc(acc_free[(G_GRP + g) % 2], 1)
            group_out(KT)

            with dve.Fori(0, KT // 2 - 1) as t:
                dv.loop(t, 2)
                for s in range(2):
                    split(G_POUT + s + 1, 2 * t, t)
                    update(G_POUT + s, 2 * t, t, 2, s, s)
            dv.end(KT // 2 - 1)
            split(G_END - 1)
            for k in range(KT - 2, KT):
                update(G_POUT + k, 0, 0, 2, k, k % 2)
            row_scale(2)
            for k in range(KT):
                dve.scalar_tensor_tensor(out=x[:, k], in0=x[:, k], scalar=gfin_v[:, k:k + 1], in1=rstd[:],
                                         op0=ALU.mult, op1=ALU.mult).then_inc(y_fin, 1)


def tables():
    half = DQK // 2
    inv = (np.float32(10000.0) ** (-np.arange(half, dtype=np.float32) / np.float32(half))).astype(np.float32)
    pos = np.concatenate([np.arange(NP), PAST + np.arange(NS)]).astype(np.float32)
    ang = (pos[None, :] * inv[:, None]).astype(np.float32)
    cos, sin = np.tile(np.cos(ang), (4, 1)), np.tile(np.sin(ang), (4, 1))
    swap = np.zeros((P, P), np.float32)
    for m in range(P):
        if m % DQK < half:
            swap[m + half, m] = -1.0
        else:
            swap[m - half, m] = 1.0
    rcount = np.zeros((P, 4, 16), np.float32)
    for g, w in enumerate(WIN):
        rcount[:, g, :] = np.float32(1.0) / np.minimum(np.arange(16) + 1, w).astype(np.float32)
    lamsel = np.zeros((P, 2), np.float32)
    for r in range(P):
        lamsel[r, (r // NS) % 2] = 1.0
    return {"cosT": cos.astype(np.float32), "sinT": sin.astype(np.float32), "swap": swap, "ident": np.eye(P, dtype=np.float32),
            "rcount": rcount, "lamsel": lamsel,
            "selc": np.ascontiguousarray(np.broadcast_to(np.eye(HEADS, dtype=np.float32), (P, HEADS, HEADS))),
            "selr": np.ascontiguousarray(np.repeat(np.eye(HEADS, dtype=np.float32)[:, :, None], P, axis=2))}


def lay_out(i):
    def tiles(w):
        k, n = w.shape
        return np.ascontiguousarray(w.reshape(k // P, P, n // P, P).transpose(2, 1, 0, 3)).reshape(n // P, P, k)

    def vec(v):
        return np.ascontiguousarray(v.reshape(-1, P).T)

    def featT(a):
        return np.ascontiguousarray(a.T.reshape(-1, P, a.shape[0]).transpose(1, 0, 2))

    f = {k: np.asarray(v) for k, v in i.items()}
    w_in = f["w_in_att"][0]
    c0 = 3 * HEADS * P
    q_w, k_w, v_w = w_in[:, 0:1024], w_in[:, 1024:2048], w_in[:, 2048:c0]
    cq_w, ckv_w, kpe_w = w_in[:, c0:c0 + LORA], w_in[:, c0 + LORA:c0 + 2 * LORA], w_in[:, c0 + 2 * LORA:c0 + 2 * LORA + DQK]
    gate_w = w_in[:, c0 + 2 * LORA + DQK:]
    ada = np.concatenate([f["w_ada"][0], f["w_ada"][1]], axis=1)
    pin = f["w_in_pool"][0].reshape(D, 2, KT, P).transpose(0, 2, 1, 3).reshape(D, 4096)
    c = np.concatenate([f["c_prompt"], f["c_sample"]], axis=0)
    heads_first = lambda w: np.ascontiguousarray(w.reshape(LT, P, HEADS, P).transpose(2, 1, 0, 3)).reshape(HEADS, P, LORA)
    out = {
        "xT": featT(np.concatenate([f["x_prompt"][0], f["x_sample"][0]], axis=0)),
        "cT": np.ascontiguousarray(c.T.reshape(KT, P, 2).transpose(1, 0, 2)),
        "cB": c.reshape(1, 2 * D),
        "w_ada_pe": np.ascontiguousarray(ada[:, :ADA_PE * P].reshape(4, 4, P, CHUNKS, 512).transpose(3, 0, 2, 1, 4))
                    .reshape(ADA_PE, P, D),
        "w_ada_dve": np.ascontiguousarray(ada[:, ADA_PE * P:].T).reshape(ADA_T - ADA_PE, P, D),
        "bada": vec(f["b_ada"].reshape(-1)),
        "gnorm": np.ascontiguousarray(f["g_norm"].reshape(2, KT, P).transpose(2, 0, 1)),
        "w_kpe": tiles(np.concatenate([kpe_w, kpe_w], axis=1))[0],
        "w_z": tiles(np.concatenate([cq_w, ckv_w, q_w, k_w, v_w], axis=1)),
        "w_gate": tiles(gate_w), "w_out": tiles(f["w_out_att"][0]), "w_pin": tiles(pin),
        "w_grp": np.ascontiguousarray(f["w_grp_pool"][0].reshape(4, 4, P, LORA).transpose(0, 2, 1, 3)).reshape(4, P, D),
        "w_pout": tiles(f["w_out_pool"][0]),
        "lamv": np.concatenate([f[k][0] for k in ("lam_q1", "lam_k1", "lam_q2", "lam_k2")]).reshape(1, 4 * DQK),
        "gsub": vec(f["g_subln"][0]), "gqa": vec(f["g_qa"][0]), "gkva": vec(f["g_kva"][0]),
        "w_uq": heads_first(f["w_uq"][0]),
        "w_uqr": np.ascontiguousarray(f["w_uqr"][0].reshape(LT, P, 4, P).transpose(2, 1, 0, 3)).reshape(4, P, LORA),
        "w_ukT": np.ascontiguousarray(f["w_uk"][0].transpose(1, 2, 0)),
        "w_uv": heads_first(f["w_uv"][0]), "w_uk": heads_first(f["w_uk"][0]),
        "w_uv2": np.ascontiguousarray(f["w_uv"][0].reshape(LT, P, 4, 2 * P).transpose(2, 1, 0, 3)).reshape(4, P, 2 * LORA),
        "scale_pool": vec(f["scale_pool"][0]), "gfin": vec(f["g_final"]),
        "kc": np.ascontiguousarray(f["cache_diff_k"][0, 0].transpose(1, 2, 0)),
        "vc": f["cache_diff_v"][0, 0].reshape(PAST, HEADS * P),
        "ckvT": np.ascontiguousarray(f["cache_mla_ckv"][0, 0].T), "ckv": f["cache_mla_ckv"][0, 0],
        "kpeT": np.ascontiguousarray(f["cache_mla_kpe"][0, 0].T),
        "poolT": featT(f["state_pool"][0, 0]),
    }
    out.update(tables())
    return out


_ARGS = ("xT cT cB w_ada_pe w_ada_dve bada gnorm w_kpe w_z w_gate w_out w_pin w_grp w_pout lamv gsub gqa gkva w_uq w_uqr "
         "w_ukT w_uv w_uk w_uv2 scale_pool gfin kc vc ckvT ckv kpeT poolT cosT sinT swap ident rcount lamsel selc selr").split()
_OUTS = (("y", (KT, P, R)), ("z", (ZT, P, R)), ("ckv_new", (LT, P, R)), ("kpe_new", (DQK, R)), ("pool_new", (P, KT, 2, PAD)))


def kernel(**inputs):
    import concourse.bacc as _bacc
    from concourse.bass_utils import run_bass_kernel_spmd as _run

    nc = _bacc.Bacc("TRN2", target_bir_lowering=False, num_devices=1)
    arrays, args = {}, []
    laid = lay_out(inputs)
    for name in _ARGS:
        a = np.ascontiguousarray(laid[name])
        arrays[f"in_{name}"] = a
        args.append(nc.dram_tensor(f"in_{name}", a.shape, mybir.dt.from_np(a.dtype), kind="ExternalInput").ap())
    for name, shape in _OUTS:
        args.append(nc.dram_tensor(f"out_{name}", shape, F32, kind="ExternalOutput").ap())
    program(nc, *args)
    res = _run(nc, [arrays], core_ids=[0]).results[0]
    yT = res["out_y"].reshape(D, R).T
    z = res["out_z"].reshape(ZT * P, R).T
    ck = res["out_ckv_new"].reshape(LORA, R).T
    kp = res["out_kpe_new"].T
    pool = res["out_pool_new"].transpose(2, 3, 1, 0).reshape(2, PAD, D)
    ka, va = z[:, ZK * P:ZV * P], z[:, ZV * P:ZT * P]
    C = np.ascontiguousarray
    group = lambda r0, r1, n: (C(ka[r0:r1]).reshape(1, 1, n, HEADS, P), C(va[r0:r1]).reshape(1, 1, n, HEADS, P),
                               C(ck[r0:r1]).reshape(1, 1, n, LORA), C(kp[r0:r1]).reshape(1, 1, n, DQK))
    return (C(yT[0:NP]).reshape(1, NP, D), C(yT[NP:R]).reshape(1, NS, D),
            *group(0, NP, NP), C(pool[0]).reshape(1, 1, PAD, D),
            *group(NP, R, NS), C(pool[1]).reshape(1, 1, PAD, D))
```
